# Optimizing a Trainium2 kernel written in Bass

```python
import jax, jax.numpy as jnp
from jax import lax
import numpy as np

D_MODEL = 1024
BATCH = 1
SEQ = 256
DEPTH = 2
DEC_BATCH = 8
DEC_SEQ = 4
PAST_LEN = 1024
PAGE_SIZE = 128

N_EVEN = (DEPTH + 1) // 2
N_ODD = DEPTH // 2
D_FF = 2816
EPS = 1e-6
H_A = 8
DH_A = 64
H_IDX = 16
D_IDX = 64
TOPK_MAX = 256
IDX_Q_BLOCK = 64
H_B = 8
DH_B = 64
R_DECAY = 64
R_AAA = 64
R_GATE = 128
D_B_IN = 3 * H_B * DH_B + R_DECAY + R_AAA + R_GATE
LNX_EPS = 64e-5
H_C = 4
DK_C = 64
DV_C = 128
ROPE_BASE = 10000.0
H_D = 4
DK_D = 64
DV_D = 128
CONV_W = 4
CHUNK = 64
D_AB_IN = 3 * H_A * DH_A + H_IDX * D_IDX + D_IDX + H_IDX + D_B_IN
D_AB_OUT = H_A * DH_A + H_B * DH_B
D_CD_IN = 2 * H_C * DK_C + 2 * H_C * DV_C + 2 * H_D * DK_D + 2 * H_D * DV_D + 2 * H_D
D_CD_OUT = H_C * DV_C + H_D * DV_D

kernel_name = 'hybrid_dsa_rwkv7_retnet_mlstm_step'

F32 = jnp.float32

def rmsnorm(x, g):
    xf = x.astype(F32)
    y = xf * lax.rsqrt(jnp.mean(xf * xf, axis=-1, keepdims=True) + EPS)
    return (y * g.astype(F32)).astype(x.dtype)

def head_norm(x, g, b=None, eps=1e-5):
    xf = x.astype(F32)
    mu = jnp.mean(xf, axis=-1, keepdims=True)
    var = jnp.mean(jnp.square(xf - mu), axis=-1, keepdims=True)
    y = (xf - mu) * lax.rsqrt(var + eps) * g.astype(F32)
    if b is not None:
        y = y + b.astype(F32)
    return y

def swiglu(x, wg, wu, wd):
    return (jax.nn.silu(x @ wg) * (x @ wu)) @ wd

def split_cols(z, sizes):
    return jnp.split(z, [int(c) for c in np.cumsum(sizes)[:-1]], axis=-1)

def rope(x, pos):
    half = x.shape[-1] // 2
    inv = ROPE_BASE ** (-jnp.arange(half, dtype=F32) / half)
    ang = pos.astype(F32)[:, None] * inv[None, :]
    cos = jnp.cos(ang)[None, :, None, :]
    sin = jnp.sin(ang)[None, :, None, :]
    x1, x2 = x[..., :half], x[..., half:]
    return jnp.concatenate([x1 * cos - x2 * sin, x1 * sin + x2 * cos], axis=-1)

def gather_rows(a, idx):
    return jax.vmap(lambda ab, ib: ab[ib])(a, idx)

def indexer_scores(qi, ki, wi):
    s = jnp.einsum('bqhd,bsd->bqhs', qi, ki)
    return jnp.einsum('bqhs,bqh->bqs', jax.nn.relu(s), wi).astype(F32)

def sparse_attend(q, kg, vg, valid):
    logits = jnp.einsum('bqhd,bqkhd->bqhk', q.astype(F32), kg.astype(F32)) * DH_A ** -0.5
    logits = jnp.where(valid[:, :, None, :], logits, -jnp.inf)
    p = jax.nn.softmax(logits, axis=-1)
    return jnp.einsum('bqhk,bqkhd->bqhd', p, vg.astype(F32))

def dsa_prompt(q, k, v, qi, ki, wi):
    B, T = q.shape[:2]
    topk = min(TOPK_MAX, T // 4)
    nb = T // IDX_Q_BLOCK

    def blocks(a):
        return jnp.swapaxes(a.reshape((B, nb, IDX_Q_BLOCK) + a.shape[2:]), 0, 1)

    t_blk = jnp.arange(T).reshape(nb, IDX_Q_BLOCK)
    s_pos = jnp.arange(T)

    def one_block(args):
        qb, qib, wib, tb = args
        isc = indexer_scores(qib, ki, wib)
        isc = jnp.where((s_pos[None, :] <= tb[:, None])[None], isc, -jnp.inf)
        vals, sel = lax.top_k(isc, topk)
        return sparse_attend(qb, gather_rows(k, sel), gather_rows(v, sel), jnp.isfinite(vals))

    out = lax.map(one_block, (blocks(q), blocks(qi), blocks(wi), t_blk))
    return jnp.swapaxes(out, 0, 1).reshape(B, T, H_A, DH_A)

def dsa_sample(q, k, v, qi, ki, wi, ck, cv, cki, page_table):
    DB, S = q.shape[:2]
    past = page_table.shape[1] * PAGE_SIZE
    L = past + S
    topk = min(TOPK_MAX, L // 4)
    ki_past = cki[page_table].reshape(DB, past, D_IDX).astype(ki.dtype)
    ki_all = jnp.concatenate([ki_past, ki], axis=1)
    isc = indexer_scores(qi, ki_all, wi)
    adm = jnp.arange(L)[None, :] <= (past + jnp.arange(S))[:, None]
    isc = jnp.where(adm[None], isc, -jnp.inf)
    vals, sel = lax.top_k(isc, topk)
    is_past = (sel < past)[..., None, None]
    phys = jax.vmap(lambda pt, s: pt[s])(page_table, jnp.minimum(sel, past - 1) // PAGE_SIZE)
    off = sel % PAGE_SIZE
    new_i = jnp.clip(sel - past, 0, S - 1)
    kg = jnp.where(is_past, ck[phys, off].astype(k.dtype), gather_rows(k, new_i))
    vg = jnp.where(is_past, cv[phys, off].astype(v.dtype), gather_rows(v, new_i))
    return sparse_attend(q, kg, vg, jnp.isfinite(vals))

def rwkv_step(S, inp):
    r_t, w_t, k_t, v_t, a_t, b_t = inp
    sa = jnp.einsum('bhij,bhj->bhi', S, a_t)
    S = S * w_t[:, :, None, :] + sa[..., None] * b_t[:, :, None, :] + v_t[..., None] * k_t[:, :, None, :]
    return S, jnp.einsum('bhij,bhj->bhi', S, r_t)

def rwkv7(zb, shift_prev, S0, e, P):
    B, T, _ = zb.shape
    zb = zb.astype(F32)
    prev = jnp.concatenate([shift_prev.astype(F32)[:, None], zb[:, :-1]], axis=1)
    z = zb + (prev - zb) * P['rwkv_mu'][e].astype(F32)
    r, k, v, xw, xa, xg = split_cols(z, [H_B * DH_B] * 3 + [R_DECAY, R_AAA, R_GATE])
    w_log = -jax.nn.softplus(-(P['rwkv_w0'][e] + jnp.tanh(xw) @ P['rwkv_w2'][e])) - 0.5
    decay = jnp.exp(-jnp.exp(w_log))
    a = jax.nn.sigmoid(P['rwkv_a0'][e] + xa @ P['rwkv_a2'][e])
    g = jax.nn.sigmoid(xg) @ P['rwkv_g2'][e]

    def hs(t):
        return t.reshape(B, T, H_B, DH_B)

    r, k, v, decay, a = hs(r), hs(k), hs(v), hs(decay), hs(a)
    kk = k * P['rwkv_kk'][e].reshape(H_B, DH_B)
    kk = kk * lax.rsqrt(jnp.maximum(jnp.sum(kk * kk, axis=-1, keepdims=True), 1e-24))
    k = k * (1.0 + (a - 1.0) * P['rwkv_ka'][e].reshape(H_B, DH_B))

    def tm(t):
        return jnp.swapaxes(t, 0, 1)

    S_fin, y = lax.scan(rwkv_step, S0.astype(F32), (tm(r), tm(decay), tm(k), tm(v), tm(-kk), tm(kk * a)))
    y = tm(y)
    y = head_norm(y, P['rwkv_lnx_g'][e].reshape(H_B, DH_B), P['rwkv_lnx_b'][e].reshape(H_B, DH_B), eps=LNX_EPS)
    y = y + jnp.sum(r * k * P['rwkv_rk'][e], axis=-1, keepdims=True) * v
    y = y.reshape(B, T, H_B * DH_B) * g
    return y, zb[:, -1], S_fin

def chunked_scan(step, state, xs):
    B, T = xs[0].shape[:2]
    lc = CHUNK if T % CHUNK == 0 else T
    n = T // lc
    xs_c = tuple(jnp.swapaxes(a.reshape((B, n, lc) + a.shape[2:]), 0, 1) for a in xs)
    state, ys = lax.scan(step, state, xs_c)
    return state, jnp.swapaxes(ys, 0, 1).reshape((B, T) + ys.shape[3:])

def retention_chunk(S, inp):
    q, k, v = inp
    lc = q.shape[1]
    lg = jnp.log1p(-jnp.exp2(-5.0 - jnp.arange(H_C, dtype=F32)))
    j = jnp.arange(lc, dtype=F32)
    diff = j[:, None] - j[None, :]
    dmask = jnp.where(diff >= 0, jnp.exp(jnp.maximum(diff, 0.0)[None] * lg[:, None, None]), 0.0)
    scores = jnp.einsum('bjhd,bshd->bhjs', q, k) * dmask[None]
    intra = jnp.einsum('bhjs,bshe->bjhe', scores, v)
    inter = jnp.einsum('bjhd,bhde->bjhe', q, S) * jnp.exp((j[:, None] + 1.0) * lg[None, :])[None, :, :, None]
    w_s = jnp.exp((lc - 1.0 - j)[:, None] * lg[None, :])
    S_new = jnp.exp(lc * lg)[None, :, None, None] * S + jnp.einsum('bshd,bshe,sh->bhde', k, v, w_s)
    return S_new, intra + inter

def mlstm_chunk(state, inp):
    C, n, m = state
    q, k, v, logi, logf = inp
    lc = q.shape[1]
    b = jnp.cumsum(logf, axis=1)
    causal = jnp.tril(jnp.ones((lc, lc), dtype=bool))
    D = b[:, :, None, :] - b[:, None, :, :] + logi[:, None, :, :]
    D = jnp.where(causal[None, :, :, None], D, -jnp.inf)
    inter = b + m[:, None, :]
    m_j = jnp.maximum(inter, jnp.max(D, axis=2))
    A = jnp.exp(D - m_j[:, :, None, :]) * jnp.einsum('bjhd,bshd->bjsh', q, k)
    sc = jnp.exp(inter - m_j)
    num = jnp.einsum('bjsh,bshe->bjhe', A, v) + sc[..., None] * jnp.einsum('bjhd,bhed->bjhe', q, C)
    den = jnp.sum(A, axis=2) + sc * jnp.einsum('bjhd,bhd->bjh', q, n)
    h = num / jnp.maximum(jnp.abs(den), jnp.exp(-m_j))[..., None]
    bL = b[:, -1]
    gs = bL[:, None, :] - b + logi
    m_new = jnp.maximum(bL + m, jnp.max(gs, axis=1))
    ws = jnp.exp(gs - m_new[:, None, :])
    carry = jnp.exp(bL + m - m_new)
    C_new = carry[..., None, None] * C + jnp.einsum('bsh,bshe,bshd->bhed', ws, v, k)
    n_new = carry[..., None] * n + jnp.einsum('bsh,bshd->bhd', ws, k)
    return (C_new, n_new, m_new), h

def causal_conv_silu(u, buf, w, b):
    T = u.shape[1]
    full = jnp.concatenate([buf.astype(u.dtype), u], axis=1)
    y = b
    for i in range(CONV_W):
        y = y + full[:, i:i + T] * w[i]
    return jax.nn.silu(y), full[:, T:]

def ab_mixer(h, e, dsa_fn, shift_prev, S0, P):
    B, T, _ = h.shape
    z = h @ P['ab_w_in'][e]
    q, k, v, qi, ki, wi, zb = split_cols(z, [H_A * DH_A] * 3 + [H_IDX * D_IDX, D_IDX, H_IDX, D_B_IN])
    q = q.reshape(B, T, H_A, DH_A)
    k = k.reshape(B, T, H_A, DH_A)
    v = v.reshape(B, T, H_A, DH_A)
    qi = qi.reshape(B, T, H_IDX, D_IDX)
    ki = rmsnorm(ki, P['kidx_g'][e])
    wi = wi * (H_IDX * D_IDX) ** -0.5
    ya = dsa_fn(e, q, k, v, qi, ki, wi).reshape(B, T, H_A * DH_A)
    yb, shift_new, S_new = rwkv7(zb, shift_prev, S0, e, P)
    y = jnp.concatenate([ya, yb], axis=-1).astype(h.dtype) @ P['ab_w_out'][e]
    return y, (k, v, ki, S_new, shift_new)

def cd_mixer(h, pos, o, ret_S, mC, mn, mm, conv_buf, P):
    B, T, _ = h.shape
    z = h @ P['cd_w_in'][o]
    qc, kc, vc, gc, qkd, vd, ig, fg, og = split_cols(
        z, [H_C * DK_C, H_C * DK_C, H_C * DV_C, H_C * DV_C, 2 * H_D * DK_D, H_D * DV_D, H_D, H_D, H_D * DV_D])
    qc = rope(qc.astype(F32).reshape(B, T, H_C, DK_C), pos)
    kc = rope(kc.astype(F32).reshape(B, T, H_C, DK_C), pos) * DK_C ** -0.5
    vc = vc.astype(F32).reshape(B, T, H_C, DV_C)
    ret_S, yc = chunked_scan(retention_chunk, ret_S.astype(F32), (qc, kc, vc))
    yc = head_norm(yc, P['ret_gn'][o]).reshape(B, T, H_C * DV_C) * jax.nn.silu(gc.astype(F32))
    qkd, conv_new = causal_conv_silu(qkd, conv_buf, P['conv_w'][o], P['conv_b'][o])
    qd, kd = split_cols(qkd.astype(F32), [H_D * DK_D, H_D * DK_D])
    qd = qd.reshape(B, T, H_D, DK_D)
    kd = kd.reshape(B, T, H_D, DK_D) * DK_D ** -0.5
    vd = vd.astype(F32).reshape(B, T, H_D, DV_D)
    b_if = P['mlstm_if_b'][o].astype(F32)
    logi = ig.astype(F32) + b_if[0]
    logf = jax.nn.log_sigmoid(fg.astype(F32) + b_if[1])
    (mC, mn, mm), hd = chunked_scan(mlstm_chunk, (mC.astype(F32), mn.astype(F32), mm.astype(F32)),
                                    (qd, kd, vd, logi, logf))
    yd = head_norm(hd, P['mlstm_gn'][o]).reshape(B, T, H_D * DV_D) * jax.nn.sigmoid(og.astype(F32))
    y = jnp.concatenate([yc, yd], axis=-1).astype(h.dtype) @ P['cd_w_out'][o]
    return y, (ret_S, mC, mn, mm, conv_new)

def trunk(x, pos, dsa_fn, ab_init, cd_init, P):
    ab_new, cd_new = [], []
    for l in range(DEPTH):
        g = P['norm_g'][l]
        hf = swiglu(rmsnorm(x, g[0]), P['ffn_wg'][l, 0], P['ffn_wu'][l, 0], P['ffn_wd'][l, 0])
        x = x + 0.5 * rmsnorm(hf, g[1])
        h = rmsnorm(x, g[2])
        if l % 2 == 0:
            y, st = ab_mixer(h, l // 2, dsa_fn, *ab_init(l // 2), P)
            ab_new.append(st)
        else:
            y, st = cd_mixer(h, pos, l // 2, *cd_init(l // 2), P)
            cd_new.append(st)
        x = x + rmsnorm(y, g[3])
        hf = swiglu(rmsnorm(x, g[4]), P['ffn_wg'][l, 1], P['ffn_wu'][l, 1], P['ffn_wd'][l, 1])
        x = x + 0.5 * rmsnorm(hf, g[5])
    ab = tuple(jnp.stack(s) for s in zip(*ab_new))
    cd = tuple(jnp.stack(s) for s in zip(*cd_new))
    return x, ab, cd

def setup_inputs(seed: int = 0) -> dict:
    key = jax.random.key(seed)
    ks = iter(jax.random.split(key, 64))

    def nrm(shape, s=1.0):
        return jax.random.normal(next(ks), shape, F32) * s

    n_pages = PAST_LEN // PAGE_SIZE
    n_pool = (5 * DEC_BATCH * n_pages + 3) // 4
    kv_shape = (N_EVEN, n_pool, PAGE_SIZE, H_A, DH_A)
    d = {}
    d['x_prompt'] = nrm((BATCH, SEQ, D_MODEL))
    d['x_sample'] = nrm((DEC_BATCH, DEC_SEQ, D_MODEL))
    d['cache_k'] = nrm(kv_shape)
    d['cache_v'] = nrm(kv_shape)
    d['cache_kidx'] = nrm((N_EVEN, n_pool, PAGE_SIZE, D_IDX))
    d['state_rwkv'] = nrm((N_EVEN, DEC_BATCH, H_B, DH_B, DH_B), 0.3)
    d['state_shift'] = nrm((N_EVEN, DEC_BATCH, D_B_IN))
    d['state_ret'] = nrm((N_ODD, DEC_BATCH, H_C, DK_C, DV_C), 0.1)
    d['state_mlstm_C'] = nrm((N_ODD, DEC_BATCH, H_D, DV_D, DK_D), 0.1)
    d['state_mlstm_n'] = nrm((N_ODD, DEC_BATCH, H_D, DK_D), 0.1)
    d['state_mlstm_m'] = nrm((N_ODD, DEC_BATCH, H_D))
    d['state_conv'] = nrm((N_ODD, DEC_BATCH, CONV_W - 1, 2 * H_D * DK_D))
    perm = jax.random.permutation(next(ks), n_pool)
    d['page_table'] = perm[:DEC_BATCH * n_pages].reshape(DEC_BATCH, n_pages).astype(jnp.int32)
    d['norm_g'] = 1.0 + nrm((DEPTH, 6, D_MODEL), 0.02)
    d['ffn_wg'] = nrm((DEPTH, 2, D_MODEL, D_FF), D_MODEL ** -0.5)
    d['ffn_wu'] = nrm((DEPTH, 2, D_MODEL, D_FF), D_MODEL ** -0.5)
    d['ffn_wd'] = nrm((DEPTH, 2, D_FF, D_MODEL), D_FF ** -0.5)
    d['ab_w_in'] = nrm((N_EVEN, D_MODEL, D_AB_IN), D_MODEL ** -0.5)
    d['ab_w_out'] = nrm((N_EVEN, D_AB_OUT, D_MODEL), D_AB_OUT ** -0.5)
    d['kidx_g'] = 1.0 + nrm((N_EVEN, D_IDX), 0.02)
    d['rwkv_mu'] = jax.random.uniform(next(ks), (N_EVEN, D_B_IN), F32)
    d['rwkv_w0'] = nrm((N_EVEN, H_B * DH_B), 0.5)
    d['rwkv_w2'] = nrm((N_EVEN, R_DECAY, H_B * DH_B), R_DECAY ** -0.5)
    d['rwkv_a0'] = nrm((N_EVEN, H_B * DH_B), 0.1)
    d['rwkv_a2'] = nrm((N_EVEN, R_AAA, H_B * DH_B), R_AAA ** -0.5)
    d['rwkv_g2'] = nrm((N_EVEN, R_GATE, H_B * DH_B), R_GATE ** -0.5)
    d['rwkv_kk'] = 1.0 + nrm((N_EVEN, H_B * DH_B), 0.1)
    d['rwkv_ka'] = 1.0 + nrm((N_EVEN, H_B * DH_B), 0.1)
    d['rwkv_rk'] = nrm((N_EVEN, H_B, DH_B), 0.1)
    d['rwkv_lnx_g'] = 1.0 + nrm((N_EVEN, H_B * DH_B), 0.02)
    d['rwkv_lnx_b'] = nrm((N_EVEN, H_B * DH_B), 0.02)
    d['cd_w_in'] = nrm((N_ODD, D_MODEL, D_CD_IN), D_MODEL ** -0.5)
    d['cd_w_out'] = nrm((N_ODD, D_CD_OUT, D_MODEL), D_CD_OUT ** -0.5)
    d['ret_gn'] = 1.0 + nrm((N_ODD, H_C, DV_C), 0.02)
    d['conv_w'] = nrm((N_ODD, CONV_W, 2 * H_D * DK_D), CONV_W ** -0.5)
    d['conv_b'] = nrm((N_ODD, 2 * H_D * DK_D), 0.01)
    f_b = jnp.broadcast_to(jnp.linspace(3.0, 6.0, H_D, dtype=F32), (N_ODD, H_D))
    d['mlstm_if_b'] = jnp.stack([nrm((N_ODD, H_D), 0.1), f_b + nrm((N_ODD, H_D), 0.1)], axis=1)
    d['mlstm_gn'] = 1.0 + nrm((N_ODD, H_D, DV_D), 0.02)
    return d

def reference(x_prompt, x_sample, cache_k, cache_v, cache_kidx, state_rwkv, state_shift, state_ret,
              state_mlstm_C, state_mlstm_n, state_mlstm_m, state_conv, page_table, norm_g, ffn_wg, ffn_wu,
              ffn_wd, ab_w_in, ab_w_out, kidx_g, rwkv_mu, rwkv_w0, rwkv_w2, rwkv_a0, rwkv_a2, rwkv_g2, rwkv_kk,
              rwkv_ka, rwkv_rk, rwkv_lnx_g, rwkv_lnx_b, cd_w_in, cd_w_out, ret_gn, conv_w, conv_b, mlstm_if_b,
              mlstm_gn):
    P = dict(norm_g=norm_g, ffn_wg=ffn_wg, ffn_wu=ffn_wu, ffn_wd=ffn_wd, ab_w_in=ab_w_in, ab_w_out=ab_w_out,
             kidx_g=kidx_g, rwkv_mu=rwkv_mu, rwkv_w0=rwkv_w0, rwkv_w2=rwkv_w2, rwkv_a0=rwkv_a0, rwkv_a2=rwkv_a2,
             rwkv_g2=rwkv_g2, rwkv_kk=rwkv_kk, rwkv_ka=rwkv_ka, rwkv_rk=rwkv_rk, rwkv_lnx_g=rwkv_lnx_g,
             rwkv_lnx_b=rwkv_lnx_b, cd_w_in=cd_w_in, cd_w_out=cd_w_out, ret_gn=ret_gn, conv_w=conv_w,
             conv_b=conv_b, mlstm_if_b=mlstm_if_b, mlstm_gn=mlstm_gn)
    B, T, _ = x_prompt.shape
    DB, DS, _ = x_sample.shape
    past = page_table.shape[1] * PAGE_SIZE

    def ab_zero(e):
        return (jnp.zeros((B, D_B_IN), F32), jnp.zeros((B, H_B, DH_B, DH_B), F32))

    def cd_zero(o):
        return (jnp.zeros((B, H_C, DK_C, DV_C), F32), jnp.zeros((B, H_D, DV_D, DK_D), F32),
                jnp.zeros((B, H_D, DK_D), F32), jnp.zeros((B, H_D), F32),
                jnp.zeros((B, CONV_W - 1, 2 * H_D * DK_D), x_prompt.dtype))

    def ab_cached(e):
        return (state_shift[e], state_rwkv[e])

    def cd_cached(o):
        return (state_ret[o], state_mlstm_C[o], state_mlstm_n[o], state_mlstm_m[o], state_conv[o])

    def dsa_p(e, q, k, v, qi, ki, wi):
        return dsa_prompt(q, k, v, qi, ki, wi)

    def dsa_s(e, q, k, v, qi, ki, wi):
        return dsa_sample(q, k, v, qi, ki, wi, cache_k[e], cache_v[e], cache_kidx[e], page_table)

    y_p, (kp, vp, kip, rwp, shp), (rtp, cp, nvp, mp, cvp) = trunk(
        x_prompt, jnp.arange(T), dsa_p, ab_zero, cd_zero, P)
    y_s, (ks_, vs_, kis, rws, shs), (rts, cs, nvs, ms, cvs) = trunk(
        x_sample, past + jnp.arange(DS), dsa_s, ab_cached, cd_cached, P)
    return (y_p, y_s, kp, vp, kip, rwp, shp, rtp, cp, nvp, mp, cvp,
            ks_, vs_, kis, rws, shs, rts, cs, nvs, ms, cvs)


_drawn_inputs = setup_inputs


def setup_inputs(seed=0):
    import zlib

    import numpy as np

    out = dict(_drawn_inputs(seed))
    spreads = {}
    factors = {'ret_gn': 6.98, 'conv_b': 2.903, 'mlstm_gn': 7.992}
    for name, (base, spread) in spreads.items():
        noise = np.random.default_rng([zlib.crc32(name.encode()), seed]).standard_normal(out[name].shape)
        drawn = base * np.exp(spread * noise) if base else spread * noise
        out[name] = __import__('jax').numpy.asarray(drawn.astype(out[name].dtype))
    for name, factor in factors.items():
        out[name] = (out[name] * factor).astype(out[name].dtype)
    return out
```

```python
from contextlib import ExitStack

import numpy as np

import concourse.bass as bass
from concourse import mybir

F32 = mybir.dt.float32
I32 = mybir.dt.int32
ALU = mybir.AluOpType
ACT = mybir.ActivationFunctionType
AX_X = mybir.AxisListType.X

P = 128
D_MODEL, D_FF = 1024, 2816
KT = D_MODEL // P
FT = D_FF // P
TP = 256
NB, TS = 8, 4
NS = NB * TS
NT = TP + NS
EPS = 1e-6
RING = 4
BANK = 512
F32R = mybir.dt.float32r


class Chip:

    def __init__(self, nc, ctx, ins, outs):
        self.nc, self.ctx, self.ins, self.outs = nc, ctx, ins, outs
        self.n_pool = ins["cache_i"].shape[0]
        self.pairs = 0
        self.pairs_sent = 0
        self.downs = 0
        self.downs_sent = 0
        self.stage_sems = []
        self.stores = 0
        sb, sem = self.sb, self.sem
        self.x = sb("x", [P, KT, NT])
        self.xg, self.xlo = self.two_types("xg", [P, KT, NT])
        self.xscratch, self.xhi = self.two_types("xhi", [P, KT, NT])
        self.rstd = sb("rstd", [P, NT])
        self.xsq = sb("xsq", [P, NT])
        self.gains = sb("gains", [P, 12, KT])
        self.ident = sb("ident", [P, P])
        self.ones = sb("ones", [P, P])
        self.half_ones = sb("half_ones", [P, P])
        self.eps = sb("eps", [P, 4])
        self.ring, self.ring_lo = self.two_types("ring", [P, RING, 2, KT, P])
        self.down, self.down_lo = self.two_types("down", [P, 2, FT, P])
        self.ring_landed = [sem(f"ring_landed{i}") for i in range(RING)]
        self.down_landed = [sem(f"down_landed{i}") for i in range(2)]
        self.pair_masked, self.pair_split = sem("pair_masked"), sem("pair_split")
        self.down_masked, self.down_split = sem("down_masked"), sem("down_split")
        self.xg_made, self.xg_masked = sem("xg_made"), sem("xg_masked")
        self.hidden_raw, self.hidden_masked = sem("hidden_raw"), sem("hidden_masked")
        self.pair_done = sem("pair_done")
        self.down_done = sem("down_done")
        self.stored = sem("stored")
        self.tails = 0
        self.post_sum, self.post_sd, self.x_new, self.x_sq, self.pre_sum, self.pre_sd, self.xsq_ready = (
            sem(n) for n in ("post_sum", "post_sd", "x_new", "x_sq", "pre_sum", "pre_sd", "xsq_ready"))
        self.y_done, self.y_squared, self.ysq_added = (sem(n) for n in ("y_done", "y_squared", "ysq_added"))
        self.gate_scaled, self.up_scaled, self.silu_done, self.hidden_done = (
            sem(n) for n in ("gate_scaled", "up_scaled", "silu_done", "hidden_done"))
        self.chain = {e: sem(f"chain_{e}") for e in ("dve", "act", "pool")}
        self.links = {e: 0 for e in ("dve", "act", "pool")}
        psum = ctx.enter_context(nc.psum_tensor("psum", [P, 8, BANK], F32))
        self.banks = [psum[:, i] for i in range(8)]
        self.two_banks = [psum[:, 2 * b:2 * b + 2] for b in range(2)]

    def sb(self, name, shape, dt=F32, ctx=None):
        return (ctx or self.ctx).enter_context(self.nc.sbuf_tensor(name, shape, dt))

    def two_types(self, name, shape, ctx=None):
        wide = self.sb(name, shape, ctx=ctx)
        size = 4 * int(np.prod(shape[1:]))
        return wide, self.nc.alloc_sbuf_tensor_at(name + "_r", shape, F32R, offset=self.nc.sbuf_base - size)

    def stage_sem(self, name):
        self.stage_sems.append(self.nc.alloc_semaphore(name=name))
        return self.stage_sems[-1]

    def end_stage(self):
        self.nc.clear_and_free_semaphores(self.stage_sems)
        self.nc.all_engine_barrier()
        self.stage_sems = []

    def sem(self, name):
        return self.ctx.enter_context(self.nc.semaphore(name))

    def link(self, engine, which, ins):
        self.links[which] += 1
        ins.then_inc(self.chain[which], 1)
        engine.wait_ge(self.chain[which], self.links[which])

    def store(self, eng, out, src):
        self.stores += 1
        eng.dma_start(out, src).then_inc(self.stored, 16)


def send_pairs(c, sp, stream, first, n):
    for j in range(first, first + n):
        s = c.pairs_sent % RING
        if c.pairs_sent >= RING:
            sp.wait_ge(c.pair_done, c.pairs_sent - RING + 1)
        sp.dma_start(c.ring[:, s].rearrange("p a k m -> p (a k m)"), stream[j]).then_inc(c.ring_landed[s], 16)
        c.pairs_sent += 1


def send_pair_loop(c, sp, stream, first, rounds):
    sent0 = c.pairs_sent
    with sp.Fori(0, rounds) as i:
        for u in range(RING):
            s = (sent0 + u) % RING
            sp.wait_ge(c.pair_done, i * RING + (sent0 + u - RING + 1))
            sp.dma_start(c.ring[:, s].rearrange("p a k m -> p (a k m)"),
                         stream[bass.ds(i * RING + (first + u), 1)].rearrange("a p n -> (a p) n")
                         ).then_inc(c.ring_landed[s], 16)
    c.pairs_sent += rounds * RING


def send_downs(c, sp, stream, first, n):
    for j in range(first, first + n):
        s = c.downs_sent % 2
        if c.downs_sent >= 2:
            sp.wait_ge(c.down_done, c.downs_sent - 1)
        sp.dma_start(c.down[:, s].rearrange("p k m -> p (k m)"), stream[j]).then_inc(c.down_landed[s], 16)
        c.downs_sent += 1


def mask(dve, hi, a):
    return dve.tensor_copy(hi, a)


def low_bits(eng, lo, a, hi):
    return eng.tensor_tensor(lo, a, hi.bitcast(F32), ALU.subtract)


def three_products(pe, out, w_hi, w_lo, x_hi, x_lo, start, stop):
    pe.matmul(out, w_hi, x_hi, start=start, stop=False)
    pe.matmul(out, w_hi, x_lo, start=False, stop=False)
    return pe.matmul(out, w_lo, x_hi, start=False, stop=stop)


def split_pair(c, dve, whi, first, u, i=0):
    s, b = (first + u) % RING, (first + u) % 2
    hi = whi[:, b].rearrange("p a k m -> p (a k m)")
    w, lo = (a[:, s].rearrange("p a k m -> p (a k m)") for a in (c.ring, c.ring_lo))
    dve.wait_ge(c.ring_landed[s], 16 * (i + (first + u) // RING + 1))
    mask(dve, hi, w).then_inc(c.pair_masked, 1)
    dve.wait_ge(c.pair_masked, i * RING + (first + u + 1))
    low_bits(dve, lo, w, hi).then_inc(c.pair_split, 1)


def split_x(c, dve, nth):
    for n in range(KT):
        dve.wait_ge(c.xg_made, KT * nth + n + 1)
        mask(dve, c.xhi[:, n], c.xg[:, n]).then_inc(c.xg_masked, 1)
        dve.wait_ge(c.xg_masked, KT * nth + n + 1)
        last = low_bits(dve, c.xlo[:, n], c.xg[:, n], c.xhi[:, n])
    return last


class Tail:

    def __init__(self, c, name, yg, ysq, factor, next_gain, scratch=None):
        self.c, self.yg, self.ysq, self.factor, self.next_gain = c, yg, ysq, factor, next_gain
        ctx = self.scope = ExitStack()
        self.sd = c.sb(f"sd_{name}", [P, NT], ctx=ctx)
        self.rpost = c.sb(f"rpost_{name}", [P, NT], ctx=ctx)
        self.t, self.sq = scratch or [c.sb(f"{n}_{name}", [P, KT, NT], ctx=ctx) for n in ("t", "sq")]
        self.sd2 = c.sb(f"sd2_{name}", [P, NT], ctx=ctx)
        self.done = c.tails
        c.tails += 1

    def pe(self, pe, ysq_ready, count, bank):
        c = self.c
        self.bank = bank
        pe.wait_ge(ysq_ready, count)
        pe.matmul(bank[:, 0:NT], c.ones[:, :], self.ysq, start=True, stop=True).then_inc(c.post_sum, 1)
        if self.next_gain is None:
            return
        pe.wait_ge(c.xsq_ready, self.done + 1)
        pe.matmul(bank[:, 0:NT], c.ones[:, :], c.xsq[:, :], start=True, stop=True).then_inc(c.pre_sum, 1)

    def act(self, act, bank):
        c = self.c
        f2 = 1.0 / (self.factor * self.factor)
        act.wait_ge(c.post_sum, self.done + 1)
        act.activation(self.sd[:, :], bank[:, 0:NT], ACT.Sqrt, scale=f2 / D_MODEL,
                       bias=c.eps[:, 0:1] if f2 == 1 else c.eps[:, 1:2]).then_inc(c.post_sd, 1)
        if self.next_gain is None:
            return
        for n in range(KT):
            act.wait_ge(c.x_new, KT * self.done + n + 1)
            act.activation(self.sq[:, n], c.x[:, n], ACT.Square).then_inc(c.x_sq, 1)
            act.activation(c.xg[:, n], c.x[:, n], ACT.Copy, scale=c.gains[:, self.next_gain, n:n + 1]).then_inc(c.xg_made, 1)
        act.wait_ge(c.pre_sum, self.done + 1)
        act.activation(self.sd2[:, :], bank[:, 0:NT], ACT.Sqrt, scale=1.0 / D_MODEL,
                       bias=c.eps[:, 0:1]).then_inc(c.pre_sd, 1)

    def dve(self, dve):
        c = self.c
        dve.wait_ge(c.post_sd, self.done + 1)
        c.link(dve, "dve", dve.reciprocal(self.rpost[:, :], self.sd[:, :]))
        for n in range(KT):
            c.link(dve, "dve", dve.tensor_tensor(self.t[:, n], self.yg[:, n], self.rpost[:, :], ALU.mult))
            dve.tensor_tensor(c.x[:, n], c.x[:, n], self.t[:, n], ALU.add).then_inc(c.x_new, 1)
        if self.next_gain is None:
            return
        split_x(c, dve, self.done + 1)
        dve.wait_ge(c.pre_sd, self.done + 1)
        dve.reciprocal(c.rstd[:, :], self.sd2[:, :])

    def pool(self, pool):
        c = self.c
        if self.next_gain is None:
            return
        pool.wait_ge(c.x_sq, KT * self.done + 2)
        last = pool.tensor_tensor(c.xsq[:, :], self.sq[:, 0], self.sq[:, 1], ALU.add)
        for n in range(2, KT):
            c.link(pool, "pool", last)
            pool.wait_ge(c.x_sq, KT * self.done + n + 1)
            last = pool.tensor_tensor(c.xsq[:, :], c.xsq[:, :], self.sq[:, n], ALU.add)
        last.then_inc(c.xsq_ready, 1)


def start_stage(c, gain, prefetch):
    nc = c.nc
    loaded, x_loaded, sq_done, summed, sd_done = (c.sem(n) for n in ("const_loaded", "x_loaded", "x0_sq", "x0_sum", "x0_sd"))
    xsq_ready = c.sem("x0_xsq")
    with ExitStack() as ctx, nc.Block() as block:
        sq = c.sb("sq0", [P, KT, NT], ctx=ctx)
        sd = c.sb("sd0", [P, NT], ctx=ctx)

        @block.sync
        def _(sp):
            sp.dma_start(c.x[:, :, :], c.ins["x"]).then_inc(x_loaded, 16)
            for t, n in ((c.gains, "gains"), (c.ident, "ident"), (c.ones, "ones"), (c.half_ones, "half_ones"),
                         (c.eps, "eps")):
                sp.dma_start(t[:], c.ins[n]).then_inc(loaded, 16)
            prefetch(sp)

        @block.scalar
        def _(act):
            act.wait_ge(x_loaded, 16)
            for n in range(KT):
                act.activation(sq[:, n], c.x[:, n], ACT.Square).then_inc(sq_done, 1)
            act.wait_ge(loaded, 80)
            for n in range(KT):
                act.activation(c.xg[:, n], c.x[:, n], ACT.Copy, scale=c.gains[:, gain, n:n + 1]).then_inc(c.xg_made, 1)
            act.wait_ge(summed, 1)
            act.activation(sd[:, :], c.banks[7][:, 0:NT], ACT.Sqrt, scale=1.0 / D_MODEL,
                           bias=c.eps[:, 0:1]).then_inc(sd_done, 1)

        @block.gpsimd
        def _(pool):
            pool.wait_ge(sq_done, 2)
            last = pool.tensor_tensor(c.xsq[:, :], sq[:, 0], sq[:, 1], ALU.add)
            for n in range(2, KT):
                c.link(pool, "pool", last)
                pool.wait_ge(sq_done, n + 1)
                last = pool.tensor_tensor(c.xsq[:, :], c.xsq[:, :], sq[:, n], ALU.add)
            last.then_inc(xsq_ready, 1)

        @block.tensor
        def _(pe):
            pe.wait_ge(loaded, 80)
            pe.wait_ge(xsq_ready, 1)
            pe.matmul(c.banks[7][:, 0:NT], c.ones[:, :], c.xsq[:, :], start=True, stop=True).then_inc(summed, 1)

        @block.vector
        def _(dve):
            split_x(c, dve, 0)
            dve.wait_ge(sd_done, 1)
            dve.reciprocal(c.rstd[:, :], sd[:, :])


def tile(a, n):
    return a[:, n] if isinstance(n, int) else a[:, bass.ds(n, 1)].rearrange("p a t -> p (a t)")


def ffn_stage(c, f, next_gain, prefetch):
    nc = c.nc
    gain = 6 * (f // 2) + (1 if f % 2 == 0 else 5)
    gu, dn = c.ins["w_gu"][f], c.ins["w_down"][f]
    gate_scaled, up_scaled, silu_done, hidden_done = c.gate_scaled, c.up_scaled, c.silu_done, c.hidden_done
    y_done, y_squared, ysq_added = c.y_done, c.y_squared, c.ysq_added
    pairs0, y0 = FT * f, KT * c.tails
    first, first_down = c.pairs, c.downs
    rounds, rest = (FT - RING) // RING, (FT - RING) % RING
    loops = (FT - 2) // RING
    assert (FT - 2) % RING == 0
    with ExitStack() as ctx:
        def sb(n, shape, dt=F32):
            return c.sb(f"{n}{f}", shape, dt, ctx=ctx)
        hfree, hhi = c.two_types(f"hidden_hi{f}", [P, FT, NT], ctx)
        hidden, hlo = c.two_types(f"hidden{f}", [P, FT, NT], ctx)
        whi, dhi = sb("pair_hi", [P, 2, 2, KT, P], F32R), sb("down_hi", [P, 2, FT, P], F32R)
        gate, silu, up = sb("gate", [P, 2, NT]), sb("silu", [P, 2, NT]), sb("up", [P, 2, NT])
        y, y2 = sb("y", [P, 2, NT]), sb("y2", [P, 2, NT])
        yg = sb("yg", [P, KT, NT])
        ysq = sb("ysq", [P, NT])
        tail = Tail(c, f"ffn{f}", yg, ysq[:, :], 0.5, next_gain, (hfree[:, 0:KT], hidden[:, 0:KT]))
        ctx.enter_context(tail.scope)
        block = ctx.enter_context(nc.Block())

        @block.sync
        def _(sp):
            send_pair_loop(c, sp, gu, RING, rounds)
            send_pairs(c, sp, gu, RING + rounds * RING, rest)
            send_downs(c, sp, dn, 2, KT - 2)
            prefetch(sp)

        @block.tensor
        def _(pe):
            def up_pair(u, i=0):
                s, b = (first + u) % RING, (first + u) % 2
                pe.wait_ge(c.pair_split, i * RING + (first + u + 1))
                if u >= 2 or not isinstance(i, int):
                    pe.wait_ge(up_scaled, i * RING + (pairs0 + u - 1))
                for half in range(2):
                    for k in range(KT):
                        mm = three_products(pe, c.banks[2 * (u % 2) + half][:, 0:NT], whi[:, b, half, k], c.ring_lo[:, s, half, k],
                                            c.xhi[:, k], c.xlo[:, k], k == 0, k == KT - 1)
                mm.then_inc(c.pair_done, 1)
            for u in range(RING):
                up_pair(u)
            with pe.Fori(1, FT // RING) as i:
                for u in range(RING):
                    up_pair(u, i)
            for u in range(FT - FT % RING, FT):
                up_pair(u)
            pe.wait_ge(hidden_done, pairs0 + FT - 2)
            for n in range(KT):
                s = (first_down + n) % 2
                pe.wait_ge(c.down_split, first_down + n + 1)
                if n >= 2:
                    pe.wait_ge(y_done, y0 + n - 1)
                for k in range(FT):
                    if n == 0 and k == FT - 2:
                        pe.wait_ge(hidden_done, pairs0 + FT)
                    mm = three_products(pe, c.banks[4 + n % 2][:, 0:NT], dhi[:, s, k], c.down_lo[:, s, k], hhi[:, k], hlo[:, k],
                                        k == 0, k == FT - 1)
                mm.then_inc(c.down_done, 1)
            tail.pe(pe, ysq_added, y0 + KT, c.banks[6])

        @block.scalar
        def _(act):
            with act.Fori(0, FT // 2) as i:
                for b in range(2):
                    act.wait_ge(gate_scaled, i * 2 + (pairs0 + b + 1))
                    act.activation(silu[:, b], gate[:, b], ACT.Silu).then_inc(silu_done, 1)
            for n in range(KT):
                act.wait_ge(c.down_done, first_down + n + 1)
                if n >= 2:
                    act.wait_ge(ysq_added, y0 + n - 1)
                c.link(act, "act", act.activation(y[:, n % 2], c.banks[4 + n % 2][:, 0:NT], ACT.Copy))
                act.activation(y2[:, n % 2], y[:, n % 2], ACT.Square).then_inc(y_squared, 1)
                act.activation(yg[:, n], y[:, n % 2], ACT.Copy, scale=c.gains[:, gain, n:n + 1]).then_inc(y_done, 1)
            tail.act(act, c.banks[6])

        @block.vector
        def _(dve):
            def scale(u, i=0):
                b = u % 2
                dve.wait_ge(c.pair_done, i * RING + (first + u + 1))
                dve.tensor_tensor(gate[:, b], c.banks[2 * b][:, 0:NT], c.rstd[:, :], ALU.mult).then_inc(gate_scaled, 1)
                dve.tensor_tensor(up[:, b], c.banks[2 * b + 1][:, 0:NT], c.rstd[:, :], ALU.mult).then_inc(up_scaled, 1)

            def mask_hidden(u, i=0):
                dve.wait_ge(c.hidden_raw, i * RING + (pairs0 + u + 1))
                mask(dve, tile(hhi, i * RING + u), tile(hidden, i * RING + u)).then_inc(c.hidden_masked, 1)

            def split_down(n):
                s = (first_down + n) % 2
                hi, w, lo = (a[:, s].rearrange("p k m -> p (k m)") for a in (dhi, c.down, c.down_lo))
                dve.wait_ge(c.down_landed[s], 16 * ((first_down + n) // 2 + 1))
                if n >= 2:
                    dve.wait_ge(c.down_done, first_down + n - 1)
                mask(dve, hi, w).then_inc(c.down_masked, 1)
                dve.wait_ge(c.down_masked, first_down + n + 1)
                low_bits(dve, lo, w, hi).then_inc(c.down_split, 1)

            split_pair(c, dve, whi, first, 0)
            split_pair(c, dve, whi, first, 1)
            with dve.Fori(0, loops) as i:
                for u in range(RING):
                    scale(u, i)
                    split_pair(c, dve, whi, first, u + 2, i)
                    mask_hidden(u, i)
            for j in range(2):
                scale(FT - 2 + j)
                mask_hidden(FT - 2 + j)
                split_down(j)
            for n in range(2, KT):
                split_down(n)
            dve.wait_ge(y_done, y0 + KT)
            tail.dve(dve)

        @block.gpsimd
        def _(pool):
            with pool.Fori(0, FT // 2) as i:
                for b in range(2):
                    n = i * 2 + (pairs0 + b + 1)
                    h = tile(hidden, i * 2 + b)
                    pool.wait_ge(up_scaled, n)
                    pool.wait_ge(silu_done, n)
                    pool.tensor_tensor(h, silu[:, b], up[:, b], ALU.mult).then_inc(c.hidden_raw, 1)
                    pool.wait_ge(c.hidden_masked, n)
                    low_bits(pool, tile(hlo, i * 2 + b), h, tile(hhi, i * 2 + b)).then_inc(hidden_done, 1)
            pool.wait_ge(y_squared, y0 + 1)
            pool.tensor_copy(ysq[:, :], y2[:, 0]).then_inc(ysq_added, 1)
            for n in range(1, KT):
                pool.wait_ge(ysq_added, y0 + n)
                pool.wait_ge(y_squared, y0 + n + 1)
                pool.tensor_tensor(ysq[:, :], ysq[:, :], y2[:, n % 2], ALU.add).then_inc(ysq_added, 1)
            tail.pool(pool)

    c.pairs += FT
    c.downs += KT



def project_pe(c, pe, whi, z_done, npairs):
    first = c.pairs

    def one(u, i=0):
        s, b = (first + u) % RING, (first + u) % 2
        pe.wait_ge(c.pair_split, i * RING + (first + u + 1))
        if u >= 2 or not isinstance(i, int):
            pe.wait_ge(z_done, i * RING + (u - 1))
        for half in range(2):
            for k in range(KT):
                mm = three_products(pe, c.banks[2 * (u % 2) + half][:, 0:NT], whi[:, b, half, k], c.ring_lo[:, s, half, k],
                                    c.xhi[:, k], c.xlo[:, k], k == 0, k == KT - 1)
        mm.then_inc(c.pair_done, 1)

    for u in range(RING):
        one(u)
    with pe.Fori(1, npairs // RING) as i:
        for u in range(RING):
            one(u, i)


def project_dve(c, dve, whi, z, z_done, npairs, first):
    split_pair(c, dve, whi, first, 0)
    split_pair(c, dve, whi, first, 1)
    with dve.Fori(0, npairs // RING) as i:
        for u in range(RING):
            dve.wait_ge(c.pair_done, i * RING + (first + u + 1))
            dve.tensor_tensor(z[:, bass.ds(i * (2 * RING) + 2 * u, 2)], c.two_banks[u % 2][:, :, 0:NT],
                              c.rstd[:, :].rearrange("p (a t) -> p a t", a=1).to_broadcast([P, 2, NT]),
                              ALU.mult).then_inc(z_done, 1)
            split_pair(c, dve, whi, first, u + 2, i)


def project_values(c, pe, whi, pair, tile_done):
    s, b = pair % RING, pair % 2
    assert b == 0
    hi, lo = (a.rearrange("p s a k m -> p (s a k m)").rearrange("p (k n) -> p k n", k=KT) for a in (whi[:, 0:2], c.ring_lo[:, s:s + 2]))
    pe.wait_ge(c.pair_split, pair + 2)
    for i, (t0, n) in enumerate(TOK):
        for k in range(KT):
            cols = slice(t0, t0 + n)
            mm = three_products(pe, c.banks[4 + i][0:n, :], c.xhi[:, k, cols], c.xlo[:, k, cols], hi[:, k], lo[:, k], k == 0, k == KT - 1)
        tile_done(i, mm)


TOK = ((0, P), (P, P), (TP, NS))


def token_rstd_pe(c, pe, rt_sum):
    for i, (t0, n) in enumerate(TOK):
        mm = pe.matmul(c.banks[7][0:n, i:i + 1], c.xsq[:, t0:t0 + n], c.ones[:, 0:1], start=True, stop=True)
    mm.then_inc(rt_sum, 1)


def ab_in_stage(c, z, vtok):
    nc, npairs = c.nc, 16
    stream = c.ins["w_ab"]
    z_done, v_sum, rt_sum, rt_sd, rt_ready, v_done = (
        c.sem(n + "_ab") for n in ("z_done", "v_sum", "rt_sum", "rt_sd", "rt_ready", "v_done"))
    first = c.pairs
    with ExitStack() as ctx:
        rt = c.sb("rt_ab", [P, 2, 3], ctx=ctx)
        whi = c.sb("whi_ab", [P, 2, 2, KT, P], F32R, ctx=ctx)
        block = ctx.enter_context(nc.Block())

        @block.sync
        def _(sp):
            send_pair_loop(c, sp, stream, RING, 3)
            send_pairs(c, sp, stream, 16, 2)
            sp.wait_ge(v_done, 3)
            c.store(sp, c.outs["v_p"], vtok[:, 0:2])
            c.store(sp, c.outs["v_s"], vtok[0:NS, 2])
            sp.wait_ge(z_done, npairs)
            c.store(sp, c.outs["k"], z[:, 4:8])

        @block.tensor
        def _(pe):
            project_pe(c, pe, whi, z_done, npairs)
            token_rstd_pe(c, pe, rt_sum)
            project_values(c, pe, whi, first + 16, lambda i, mm: mm.then_inc(*((v_sum, 1) if i < 2 else (c.pair_done, 2))))

        @block.scalar
        def _(act):
            act.wait_ge(rt_sum, 1)
            for i, (t0, n) in enumerate(TOK):
                act.activation(rt[0:n, 0, i:i + 1], c.banks[7][0:n, i:i + 1], ACT.Sqrt, scale=1.0 / D_MODEL,
                               bias=c.eps[0:n, 0:1]).then_inc(rt_sd, 1)
            for i, (t0, n) in enumerate(TOK):
                act.wait_ge(rt_ready, i + 1)
                if i < 2:
                    act.wait_ge(v_sum, i + 1)
                else:
                    act.wait_ge(c.pair_done, first + npairs + 2)
                act.activation(vtok[0:n, i], c.banks[4 + i][0:n, :], ACT.Copy, scale=rt[0:n, 1, i:i + 1]).then_inc(v_done, 1)

        @block.vector
        def _(dve):
            project_dve(c, dve, whi, z, z_done, npairs, first)
            for i, (t0, n) in enumerate(TOK):
                dve.wait_ge(rt_sd, i + 1)
                dve.reciprocal(rt[0:n, 1, i:i + 1], rt[0:n, 0, i:i + 1]).then_inc(rt_ready, 1)

    c.pairs += npairs + 2


CH = 5
L = 64
NP_ = CH * L
HP = 4
Z_R, Z_K, Z_V, Z_WA, Z_G = 16, 20, 24, 28, 29
EXP_HALF = float(np.exp(-0.5))


def rwkv_stage(c, z, vtok, ymix):
    nc = c.nc
    S = {}
    for n in ("par_loaded", "state_loaded", "shift_ready", "mixed", "lora_in", "lora_sum", "lora_out", "ld_done", "cum_done", "w_done",
              "kk_sq", "kk_sum", "kk_max", "kk_sd", "ar_done", "bk_done", "prod_done", "bonus_sum", "sv_done",
              "act_grp", "act_out", "dve_grp", "dve_out", "pw_sum", "pw_out", "pwt_sum", "pwt_out", "x_sum", "x_out",
              "rhs_sum", "rhs_out", "sa_sum", "sa_out", "y_sum", "y_out", "st_sum", "st_out",
              "i0_sum", "i0_out", "ub_done", "ss_sum", "ss_out", "mean_sum", "yc_done", "yc_sq", "var_sum", "var_sd", "yn_done", "zeroed"):
        S[n] = c.stage_sem(n + "_rk")
    with ExitStack() as ctx:
        def sb(n, shape):
            return c.sb(n + "_rk", shape, ctx=ctx)
        par = sb("par", [P, 14 + 8 * HP])
        mu = par[:, 0:14]
        w0, a0, kkw, ka, rk, lng, lnb, omka = (par[:, 14 + 4 * j:18 + 4 * j] for j in range(8))
        wa2, g2 = sb("wa2", [P, 512]), sb("g2", [P, 512])
        shiftT = sb("shiftT", [P, 14, NB])
        zlast = sb("zlast", [P, 14, 1 + NB])
        s0t = sb("s0t", [P, NB, HP, L])
        seg = sb("seg", [P, NT])
        gmask = sb("gmask", [P, 2, P])
        amask = sb("amask", [P, 2, L])
        bmask = sb("bmask", [P, NB])
        id2 = sb("id2", [P, L])
        D = sb("D", [P, 14, NT])
        lw = sb("lw", [P, 2, NT])
        e1, e2, e3 = D[:, 0:4], D[:, 4:8], D[:, 8:12]
        f1, f2, f3 = (sb(n, [P, HP, NT]) for n in ("f1", "f2", "f3"))
        U = sb("U", [P, CH, 2, HP, L])
        spare = c.ring[:, :].rearrange("p s a k m -> p (s a k m)")
        AR = spare[:, 0:2 * HP * NP_].rearrange("p (a h n) -> p a h n", a=2, h=HP)
        BK = spare[:, 2 * HP * NP_:4 * HP * NP_].rearrange("p (h c a l) -> p h c a l", h=HP, c=CH, a=2)
        BKt = spare[:, 4 * HP * NP_:4 * HP * NP_ + CH * HP * P].rearrange("p (c h n) -> p c h n", c=CH, h=HP)
        G = c.down[:, :].rearrange("p s k m -> p (s k m)")[:, 0:CH * 2 * HP * P].rearrange("p (c q h n) -> p c q h n", c=CH, q=2, h=HP)
        av, Gt = c.xg[:, 0:HP], c.xg[:, HP:2 * HP]
        spare = z[:, 0:16].rearrange("p a t -> p (a t)")
        PW = [spare[:, o:o + CH * HP * L].rearrange("p (m l) -> p m l", l=L) for o in (0, CH * HP * L)]
        PWT = [spare[:, 2 * CH * HP * L:3 * CH * HP * L].rearrange("p (m l) -> p m l", l=L),
               vtok[:, :].rearrange("p a n -> p (a n)")[:, 0:CH * HP * L].rearrange("p (m l) -> p m l", l=L)]
        xflat = c.xscratch[:, :].rearrange("p k t -> p (k t)")
        X = xflat[:, 0:CH * HP * L].rearrange("p (n l) -> p n l", l=L)
        AKV = sb("AKV", [P, CH, HP, L])
        RHS, STt = (xflat[:, o:o + HP * L].rearrange("p (h l) -> p h l", h=HP) for o in (CH * HP * L, (CH + 1) * HP * L))
        ST = sb("ST", [P, 2, HP, L])
        I0 = xflat[:, (CH + 2) * HP * L:(CH + 3) * HP * L].rearrange("p (h a n) -> p h a n", h=HP, a=2)
        block = ctx.enter_context(nc.Block())
        B = c.banks
        r, k, v = z[:, Z_R:Z_R + 4], z[:, Z_K:Z_K + 4], z[:, Z_V:Z_V + 4]
        yT = f3
        UB = z[:, 0:4].rearrange("p a t -> p (a t)")[:, 0:2 * NB * L].rearrange("p (u b l) -> p u b l", u=2, b=NB)

        def half(q):
            return slice(q * 64, q * 64 + 64)

        def bc(ap, shape):
            return ap.to_broadcast(shape)

        @block.sync
        def _(sp):
            for dst, src in ((par[:, 0:14 + 7 * HP], "rk_par"), (wa2[:, :], "wa2"), (g2[:, :], "g2"), (shiftT[:, :, :], "shiftT"),
                             (seg[:, :], "seg"), (gmask[:, :, :], "gmask"), (amask[:, :, :], "amask"), (bmask[:, :], "bmask"),
                             (id2[:, :], "id2")):
                sp.dma_start(dst, c.ins[src]).then_inc(S["par_loaded"], 16)
            sp.dma_start(s0t[:, :, :, :], c.ins["s0t"]).then_inc(S["state_loaded"], 16)
            sp.wait_ge(S["shift_ready"], 1)
            c.store(sp, c.outs["shift"], zlast[:, :, :])
            sp.wait_ge(S["st_out"], 4)
            c.store(sp, c.outs["rwkv_p"], ST[:, 1])
            sp.wait_ge(S["ss_out"], HP)
            c.store(sp, c.outs["rwkv_s"], s0t[:, :, :, :])

        @block.gpsimd
        def _(pool):
            pool.memset(AR[:, :, :, NT:NP_], 0.0).then_inc(S["zeroed"], 1)
            pool.memset(BK[:, :, 4, :, NS:L], 0.0).then_inc(S["zeroed"], 1)
            pool.memset(U[:, :, :, :, :], 0.0).then_inc(S["zeroed"], 1)

        @block.vector
        def _(dve):
            def ln(ins):
                c.link(dve, "dve", ins)
            dve.wait_ge(S["par_loaded"], 16 * 9)
            zz = z[:, 16:30]
            dve.tensor_copy(zlast[:, :, 0:1], zz[:, :, TP - 1:TP])
            ln(dve.tensor_copy(zlast[:, :, 1:1 + NB], zz[:, :, TP + TS - 1:NT:TS]))
            dve.tensor_scalar(omka, ka, -1.0, 1.0, ALU.mult, ALU.add)
            dve.tensor_tensor(D[:, :, 1:TP], zz[:, :, 0:TP - 1], zz[:, :, 1:TP], ALU.subtract).then_inc(S["shift_ready"], 1)
            dve.tensor_scalar(D[:, :, 0:1], zz[:, :, 0:1], -1.0, None, ALU.mult)
            Ds = D[:, :, TP:NT].rearrange("p a (b t) -> p a b t", t=TS)
            zs = zz[:, :, TP:NT].rearrange("p a (b t) -> p a b t", t=TS)
            dve.tensor_tensor(Ds[:, :, :, 1:TS], zs[:, :, :, 0:TS - 1], zs[:, :, :, 1:TS], ALU.subtract)
            ln(dve.tensor_tensor(Ds[:, :, :, 0], shiftT[:, :, :], zs[:, :, :, 0], ALU.subtract))
            for j in [12, 13, 4, 5, 6, 7, 0, 1, 2, 3, 8, 9, 10, 11]:
                ins = dve.scalar_tensor_tensor(zz[:, j], D[:, j], mu[:, j:j + 1], zz[:, j], ALU.mult, ALU.add).then_inc(S["mixed"], 1)
            dve.wait_ge(S["mixed"], 14)
            for h in range(HP):
                dve.tensor_scalar(f1[:, h], k[:, h], kkw[:, h:h + 1], None, ALU.mult).then_inc(S["kk_sq"], 1)
            for h in range(HP):
                dve.wait_ge(S["kk_sum"], h + 1)
                dve.tensor_scalar(f2[:, h], B[4 + h][:, 0:NT], 1e-24, None, ALU.max).then_inc(S["kk_max"], 1)
            dve.wait_ge(S["lora_out"], HP)
            ln(dve.tensor_scalar(e1, e1, -EXP_HALF, None, ALU.mult))
            for h in range(HP):
                last = dve.tensor_tensor_scan(e2[:, h], seg[:, :], e1[:, h], 0.0, ALU.mult, ALU.add)
            ln(last)
            dve.wait_ge(c.chain["dve"], c.links["dve"])
            dve.tensor_tensor(e3, e2, e1, ALU.subtract).then_inc(S["cum_done"], 1)
            dve.wait_ge(S["kk_sd"], HP)
            ln(dve.reciprocal(f2[:, :, :], f2[:, :, :]))
            ln(dve.tensor_tensor(f1[:, :, :], f1[:, :, :], f2[:, :, :], ALU.mult))
            dve.wait_ge(S["lora_out"], 2 * HP)
            dve.tensor_tensor(f2[:, :, :], f1[:, :, :], av[:, :, :], ALU.mult)
            for h in range(HP):
                last = dve.tensor_scalar(f3[:, h], av[:, h], ka[:, h:h + 1], omka[:, h:h + 1], ALU.mult, ALU.add)
            ln(last)
            ln(dve.tensor_tensor(k, k, f3[:, :, :], ALU.mult))
            dve.wait_ge(S["w_done"], 3)
            dve.wait_ge(S["zeroed"], 3)
            dve.scalar_tensor_tensor(AR[:, 0, :, 0:NT], f1[:, :, :], -1.0, e3, ALU.mult, ALU.mult)
            dve.tensor_tensor(AR[:, 1, :, 0:NT], r, e1, ALU.mult).then_inc(S["ar_done"], 1)
            for q in range(2):
                for slot, a in ((q, f2), (1 - q, k)):
                    for c0, c1, n in ((0, 4, L), (4, 5, NS)):
                        cols = slice(c0 * L, c0 * L + (c1 - c0) * n)
                        last = dve.tensor_tensor(BK[half(q), :, c0:c1, slot, 0:n],
                                                 a[half(q), :, cols].rearrange("p h (c l) -> p h c l", l=n),
                                                 e2[half(q), :, cols].rearrange("p h (c l) -> p h c l", l=n), ALU.mult)
            last.then_inc(S["bk_done"], 1)
            dve.wait_ge(S["bk_done"], 1)
            for h in range(HP):
                dve.scalar_tensor_tensor(e2[:, h], r[:, h], rk[:, h:h + 1], k[:, h], ALU.mult, ALU.mult).then_inc(S["prod_done"], 1)
            for c_ in range(CH):
                var = 0 if c_ < 4 else 1
                for q in range(2):
                    g = 2 * c_ + q
                    dve.wait_ge(S["dve_grp"], g + 1)
                    last = dve.tensor_tensor(G[:, c_, q], B[4 + g % 2][:, :].rearrange("p (h n) -> p h n", h=HP),
                                             bc(gmask[:, var:var + 1, :], [P, HP, P]), ALU.mult).then_inc(S["dve_out"], 1)
            for c_ in range(CH):
                var = 0 if c_ < 4 else 1
                g = 10 + c_
                dve.wait_ge(S["dve_grp"], g + 1)
                dve.tensor_tensor(PW[0][:, c_ * HP:c_ * HP + HP], B[4 + g % 2][:, 0:256].rearrange("p (h n) -> p h n", h=HP),
                                  bc(amask[:, var:var + 1, :], [P, HP, L]), ALU.mult).then_inc(S["dve_out"], 1)
            dve.wait_ge(S["dve_out"], 15)
            for q in range(2):
                for c_ in range(CH):
                    dve.tensor_copy(PWT[0][half(q), c_ * HP:c_ * HP + HP], G[half(q), c_, q, :, 0:L])
                    last = dve.tensor_tensor(X[half(q), c_ * HP:c_ * HP + HP], G[half(q), c_, q, :, 0:L],
                                             bc(id2[half(q), :].rearrange("p (a n) -> p a n", a=1), [64, HP, L]), ALU.add)
            last.then_inc(S["pwt_out"], 1)
            for c_ in range(CH):
                dve.wait_ge(S["dve_grp"], 16 + c_)
                dve.tensor_copy(AKV[:, c_], B[4 + (15 + c_) % 2][:, 0:256].rearrange("p (h n) -> p h n", h=HP)).then_inc(S["dve_out"], 1)
            dve.wait_ge(S["pwt_out"], 1)
            n = 0
            for it in range(1, 6):
                for g, (m0, m1) in enumerate(GROUPS[it > 1]):
                    n += 1
                    dve.wait_ge(S["x_sum"], n)
                    w = (m1 - m0) * L
                    dve.tensor_tensor(X[:, m0:m1], X[:, m0:m1], B[6 + n % 2][:, 0:w].rearrange("p (m n) -> p m n", n=L), ALU.add).then_inc(S["x_out"], 1)
            dve.wait_ge(S["bonus_sum"], HP)
            for h in range(HP):
                last = dve.tensor_tensor(f1[:, h], B[h][:, 0:NT], v[:, h], ALU.mult)
                last.then_inc(S["sv_done"], 1)
            for c_ in range(4):
                if c_ == 0:
                    dve.wait_ge(S["dve_out"], 20)
                    dve.tensor_copy(RHS[:, :, :], AKV[:, 0]).then_inc(S["rhs_out"], 1)
                else:
                    dve.wait_ge(S["rhs_sum"], c_)
                    dve.tensor_tensor(RHS[:, :, :], AKV[:, c_], B[0][:, 0:256].rearrange("p (h n) -> p h n", h=HP), ALU.add).then_inc(S["rhs_out"], 1)
                wc = bc(e1[:, :, c_ * L + L - 1:c_ * L + L], [P, HP, L])
                dve.wait_ge(S["st_sum"], c_ + 1)
                ps = B[3][:, 0:256].rearrange("p (h n) -> p h n", h=HP)
                if c_ == 0:
                    dve.tensor_tensor(ST[:, 0], ps, wc, ALU.mult).then_inc(S["st_out"], 1)
                else:
                    dve.wait_ge(S["st_out"], c_)
                    ln(dve.tensor_tensor(STt[:, :, :], ps, ST[:, (c_ - 1) % 2], ALU.add))
                    dve.tensor_tensor(ST[:, c_ % 2], STt[:, :, :], wc, ALU.mult).then_inc(S["st_out"], 1)
            dve.wait_ge(S["sa_sum"], 4)
            ln(dve.memset(RHS[:, :, :], 0.0))
            dve.wait_ge(S["rhs_sum"], 4)
            for q in range(2):
                lo = slice(q * 64, q * 64 + NS)
                last = dve.tensor_tensor(RHS[lo], AKV[lo, 4], B[0][lo, 0:256].rearrange("p (h n) -> p h n", h=HP), ALU.add)
            last.then_inc(S["rhs_out"], 1)
            dve.wait_ge(S["sa_out"], 5)
            for h in range(HP):
                if h > 0:
                    dve.wait_ge(S["ss_sum"], h)
                for q in range(2):
                    last = dve.tensor_tensor(UB[:, q], bc(U[:, 4, q, h].rearrange("p (a l) -> p a l", a=1), [P, NB, L]),
                                      bc(bmask[:, :].rearrange("p (b a) -> p b a", a=1), [P, NB, L]), ALU.mult)
                last.then_inc(S["ub_done"], 1)
                dve.wait_ge(S["ss_sum"], h + 1)
                ln(dve.tensor_tensor(s0t[:, :, h], s0t[:, :, h], B[4][:, :].rearrange("p (b l) -> p b l", b=NB), ALU.add))
                dve.tensor_tensor(s0t[:, :, h], s0t[:, :, h],
                                  bc(e1[:, h, TP + TS - 1:NT:TS].rearrange("p (b a) -> p b a", a=1), [P, NB, L]), ALU.mult).then_inc(S["ss_out"], 1)
            dve.wait_ge(S["y_out"], 5)
            dve.wait_ge(S["mean_sum"], HP)
            for h in range(HP):
                dve.scalar_tensor_tensor(e2[:, h], B[h][:, 0:NT], -1.0 / 64, yT[:, h], ALU.mult, ALU.add).then_inc(S["yc_done"], 1)
            dve.wait_ge(S["var_sd"], HP)
            ln(dve.reciprocal(f2[:, :, :], f2[:, :, :]))
            ln(dve.tensor_tensor(e2, e2, f2[:, :, :], ALU.mult))
            for h in range(HP):
                last = dve.tensor_scalar(e3[:, h], e2[:, h], lng[:, h:h + 1], lnb[:, h:h + 1], ALU.mult, ALU.add)
            ln(last)
            ln(dve.tensor_tensor(e3, e3, f1[:, :, :], ALU.add))
            dve.tensor_tensor(ymix[:, 4:8], e3, Gt[:, :, :], ALU.mult).then_inc(S["yn_done"], 1)

        @block.scalar
        def _(act):
            act.wait_ge(S["mixed"], 2)
            act.activation(lw[0:64, 0], z[0:64, Z_WA], ACT.Tanh).then_inc(S["lora_in"], 1)
            act.activation(lw[:, 1], z[:, Z_G], ACT.Sigmoid).then_inc(S["lora_in"], 1)
            act.wait_ge(S["mixed"], 14)
            for h in range(HP):
                act.wait_ge(S["lora_sum"], h + 1)
                act.activation(e1[:, h], B[h][:, 0:NT], ACT.Sigmoid, bias=w0[:, h:h + 1]).then_inc(S["lora_out"], 1)
            for h in range(HP):
                act.wait_ge(S["lora_sum"], HP + h + 1)
                act.activation(av[:, h], B[4 + h][:, 0:NT], ACT.Sigmoid, bias=a0[:, h:h + 1]).then_inc(S["lora_out"], 1)
            for h in range(HP):
                act.wait_ge(S["lora_sum"], 2 * HP + h + 1)
                act.activation(Gt[:, h], B[h][:, 0:NT], ACT.Copy).then_inc(S["lora_out"], 1)
            act.wait_ge(S["kk_sq"], HP)
            act.activation(f2[:, :, :], f1[:, :, :], ACT.Square).then_inc(S["ld_done"], 1)
            for h in range(HP):
                act.wait_ge(S["kk_max"], h + 1)
                act.activation(f2[:, h], f2[:, h], ACT.Sqrt).then_inc(S["kk_sd"], 1)
            act.wait_ge(S["cum_done"], 1)
            act.activation(e3, e3, ACT.Exp).then_inc(S["w_done"], 1)
            act.activation(e1, e2, ACT.Exp).then_inc(S["w_done"], 1)
            act.wait_ge(S["w_done"], 2)
            act.activation(e2, e2, ACT.Exp, scale=-1.0).then_inc(S["w_done"], 1)
            act.wait_ge(S["zeroed"], 3)
            for c_ in range(CH):
                act.wait_ge(S["act_grp"], c_ + 1)
                n = L if c_ < 4 else NS
                for q in range(2):
                    lo = (1 - q) * 64
                    last = act.activation(U[lo:lo + n, c_, q], B[c_ % 3][lo:lo + n, 0:256].rearrange("p (h l) -> p h l", h=HP), ACT.Copy)
                last.then_inc(S["act_out"], 1)
            for c_ in range(CH):
                act.wait_ge(S["act_grp"], CH + c_ + 1)
                act.activation(BKt[:, c_], B[(CH + c_) % 3][:, :].rearrange("p (h l) -> p h l", h=HP), ACT.Copy).then_inc(S["act_out"], 1)
            n = 0
            for it in range(1, 6):
                src, dst = (it - 1) % 2, it % 2
                for g, (m0, m1) in enumerate(GROUPS[it > 1]):
                    n += 1
                    act.wait_ge(S["pw_sum"], n)
                    w = (m1 - m0) * L
                    act.activation(PW[dst][:, m0:m1], B[g][:, 0:w].rearrange("p (m n) -> p m n", n=L), ACT.Copy).then_inc(S["pw_out"], 1)
                    if it < 5:
                        act.wait_ge(S["pwt_sum"], n)
                        act.activation(PWT[dst][:, m0:m1], B[3 + g][:, 0:w].rearrange("p (m n) -> p m n", n=L), ACT.Copy).then_inc(S["pwt_out"], 1)
            act.wait_ge(S["i0_sum"], 1)
            act.activation(I0[:, :, :, :], B[5][:, 0:256].rearrange("p (h a t) -> p h a t", h=HP, a=2), ACT.Copy).then_inc(S["i0_out"], 1)
            for c_ in range(CH):
                act.wait_ge(S["sa_sum"], c_ + 1)
                for q in range(2):
                    last = act.activation(U[half(q), c_, q], B[1][half(q), 0:256].rearrange("p (h l) -> p h l", h=HP), ACT.Copy)
                last.then_inc(S["sa_out"], 1)
                act.wait_ge(S["y_sum"], c_ + 1)
                n = L if c_ < 4 else NS
                act.activation(yT[:, :, c_ * L:c_ * L + n], B[2][:, 0:HP * n].rearrange("p (h t) -> p h t", h=HP), ACT.Copy).then_inc(S["y_out"], 1)
            for h in range(HP):
                act.wait_ge(S["yc_done"], h + 1)
                act.activation(f2[:, h], e2[:, h], ACT.Square).then_inc(S["yc_sq"], 1)
            for h in range(HP):
                act.wait_ge(S["var_sum"], h + 1)
                act.activation(f2[:, h], B[4 + h][:, 0:NT], ACT.Sqrt, scale=1.0 / 64, bias=c.eps[:, 3:4]).then_inc(S["var_sd"], 1)

        @block.tensor
        def _(pe):
            pe.wait_ge(S["lora_in"], 2)
            for h in range(HP):
                pe.matmul(B[h][:, 0:NT], wa2[0:64, h * P:h * P + P], lw[0:64, 0], start=True, stop=True).then_inc(S["lora_sum"], 1)
            for h in range(HP):
                pe.matmul(B[4 + h][:, 0:NT], wa2[64:128, h * P:h * P + P], z[64:128, Z_WA], start=True, stop=True).then_inc(S["lora_sum"], 1)
            for h in range(HP):
                pe.wait_ge(S["lora_out"], h + 1)
                pe.matmul(B[h][:, 0:NT], g2[:, h * P:h * P + P], lw[:, 1], start=True, stop=True).then_inc(S["lora_sum"], 1)
            pe.wait_ge(S["lora_out"], 2 * HP)
            pe.wait_ge(S["ld_done"], 1)
            for h in range(HP):
                pe.matmul(B[4 + h][:, 0:NT], c.half_ones[:, :], f2[:, h], start=True, stop=True).then_inc(S["kk_sum"], 1)
            pe.wait_ge(S["lora_out"], 3 * HP)
            pe.wait_ge(S["mixed"], 14)
            for c_ in range(CH):
                n = L if c_ < 4 else NS
                if c_ >= 3:
                    pe.wait_ge(S["act_out"], c_ - 2)
                for q in range(2):
                    lo = (1 - q) * 64
                    for h in range(HP):
                        mm = pe.matmul(B[c_ % 3][lo:lo + n, h * L:h * L + L], v[:, h, c_ * L:c_ * L + n],
                                       c.ident[:, half(q)], start=True, stop=True)
                mm.then_inc(S["act_grp"], 1)
            pe.wait_ge(S["bk_done"], 1)
            for c_ in range(CH):
                pe.wait_ge(S["act_out"], CH + c_ - 2)
                for h in range(HP):
                    mm = pe.transpose(B[(CH + c_) % 3][:, h * P:h * P + P], BK[:, h, c_].rearrange("p a l -> p (a l)"), c.ident[:, :])
                mm.then_inc(S["act_grp"], 1)
            pe.wait_ge(S["kk_sd"], HP)
            g = 0
            for c_ in range(CH):
                for q in range(2):
                    if g >= 2:
                        pe.wait_ge(S["dve_out"], g - 1)
                    for h in range(HP):
                        mm = pe.matmul(B[4 + g % 2][:, h * P:h * P + P], BK[half(q), h, c_].rearrange("p a l -> p (a l)"),
                                       AR[half(q), :, h, c_ * L:c_ * L + L], start=True, stop=True)
                    mm.then_inc(S["dve_grp"], 1)
                    g += 1
            for c_ in range(CH):
                pe.wait_ge(S["dve_out"], g - 1)
                for h in range(HP):
                    for q in range(2):
                        mm = pe.matmul(B[4 + g % 2][half(q), h * L:h * L + L], AR[half(q), 0, h, c_ * L:c_ * L + L],
                                       BK[half(q), h, c_, q], start=True, stop=True)
                mm.then_inc(S["dve_grp"], 1)
                g += 1
            pe.wait_ge(S["act_out"], CH)
            for c_ in range(CH):
                pe.wait_ge(S["dve_out"], g - 1)
                for h in range(HP):
                    for q in range(2):
                        o = half(1 - q)
                        mm = pe.matmul(B[4 + g % 2][half(q), h * L:h * L + L], G[o, c_, q, h, 0:L], U[o, c_, q, h], start=True, stop=True)
                mm.then_inc(S["dve_grp"], 1)
                g += 1
            pe.wait_ge(S["dve_out"], 20)
            pe.wait_ge(S["act_out"], 2 * CH)
            pe.wait_ge(S["pwt_out"], 1)
            n = 0
            for it in range(1, 6):
                src, dst = (it - 1) % 2, it % 2
                n0 = n
                groups = GROUPS[it > 1]
                if it == 2:
                    pe.wait_ge(S["pw_out"], n)
                    pe.wait_ge(S["pwt_out"], 1 + n)
                for g, (m0, m1) in enumerate(groups):
                    n += 1
                    if it > 2:
                        pe.wait_ge(S["pw_out"], n - len(groups))
                        pe.wait_ge(S["pwt_out"], 1 + n - len(groups))
                    for m in range(m0, m1):
                        for q in range(2):
                            mm = pe.matmul(B[g][half(q), (m - m0) * L:(m - m0) * L + L], PWT[src][half(q), m], PW[src][half(q), m], start=True, stop=True)
                    mm.then_inc(S["pw_sum"], 1)
                    if it < 5:
                        for m in range(m0, m1):
                            for q in range(2):
                                mm = pe.matmul(B[3 + g][half(q), (m - m0) * L:(m - m0) * L + L], PW[src][half(q), m], PWT[src][half(q), m], start=True, stop=True)
                        mm.then_inc(S["pwt_sum"], 1)
                n = n0
                for g, (m0, m1) in enumerate(groups):
                    n += 1
                    pe.wait_ge(S["pw_out"], n)
                    if n > 2:
                        pe.wait_ge(S["x_out"], n - 2)
                    if it > 1:
                        pe.wait_ge(S["x_out"], n - len(groups) if it > 2 else 3)
                    for m in range(m0, m1):
                        for q in range(2):
                            mm = pe.matmul(B[6 + n % 2][half(q), (m - m0) * L:(m - m0) * L + L], PW[dst][half(q), m], X[half(q), m], start=True, stop=True)
                    mm.then_inc(S["x_sum"], 1)
            n_x = n
            pe.wait_ge(S["prod_done"], HP)
            for h in range(HP):
                pe.matmul(B[h][:, 0:NT], c.half_ones[:, :], e2[:, h], start=True, stop=True).then_inc(S["bonus_sum"], 1)
            pe.wait_ge(S["state_loaded"], 16)
            for b in range(NB):
                for h in range(HP):
                    for q in range(2):
                        mm = pe.matmul(B[5][half(q), 0:256].rearrange("p (h a t) -> p h a t", h=HP, a=2)[:, h, :, b * TS:b * TS + TS],
                                       s0t[half(q), b, h], AR[half(q), :, h, TP + b * TS:TP + b * TS + TS], start=True, stop=True)
            mm.then_inc(S["i0_sum"], 1)
            pe.wait_ge(S["x_out"], n_x)
            pe.wait_ge(S["sv_done"], HP)
            for c_ in range(CH):
                if 0 < c_ < 4:
                    pe.wait_ge(S["st_out"], c_)
                    for h in range(HP):
                        for q in range(2):
                            mm = pe.matmul(B[0][half(q), h * L:h * L + L], AR[half(q), 0, h, c_ * L:c_ * L + L], ST[half(q), (c_ - 1) % 2, h], start=True, stop=True)
                    mm.then_inc(S["rhs_sum"], 1)
                if c_ == 4:
                    pe.wait_ge(S["i0_out"], 1)
                    for h in range(HP):
                        for q in range(2):
                            mm = pe.matmul(B[0][q * 64:q * 64 + NS, h * L:h * L + L], I0[half(q), h, 0], c.ident[half(q), half(q)], start=True, stop=True)
                    mm.then_inc(S["rhs_sum"], 1)
                pe.wait_ge(S["rhs_out"], c_ + 1)
                for h in range(HP):
                    for q in range(2):
                        mm = pe.matmul(B[1][half(q), h * L:h * L + L], X[half(q), c_ * HP + h], RHS[half(q), h], start=True, stop=True)
                mm.then_inc(S["sa_sum"], 1)
                pe.wait_ge(S["sa_out"], c_ + 1)
                n = L if c_ < 4 else NS
                if c_ < 4:
                    if c_ > 0:
                        pe.wait_ge(S["st_out"], c_)
                    for h in range(HP):
                        for q in range(2):
                            mm = pe.matmul(B[3][half(q), h * L:h * L + L], BKt[:, c_, h, half(q)], U[:, c_, q, h], start=True, stop=True)
                    mm.then_inc(S["st_sum"], 1)
                if c_ > 0:
                    pe.wait_ge(S["y_out"], c_)
                for h in range(HP):
                    for q in range(2):
                        mm = pe.matmul(B[2][half(q), h * n:h * n + n], U[:, c_, q, h], G[:, c_, q, h, L:L + n], start=True, stop=(c_ == 0))
                        if 0 < c_ < 4:
                            mm = pe.matmul(B[2][half(q), h * n:h * n + n], ST[half(q), (c_ - 1) % 2, h], AR[half(q), 1, h, c_ * L:c_ * L + L], start=False, stop=True)
                        if c_ == 4:
                            mm = pe.matmul(B[2][half(q), h * n:h * n + n], c.ident[half(q), half(q)], I0[half(q), h, 1], start=False, stop=True)
                mm.then_inc(S["y_sum"], 1)
            for h in range(HP):
                pe.wait_ge(S["ub_done"], h + 1)
                if h > 0:
                    pe.wait_ge(S["ss_out"], h)
                for q in range(2):
                    mm = pe.matmul(B[4][half(q), :], BKt[:, 4, h, half(q)], UB[:, q], start=True, stop=True)
                mm.then_inc(S["ss_sum"], 1)
            pe.wait_ge(S["y_out"], 5)
            for h in range(HP):
                pe.matmul(B[h][:, 0:NT], c.half_ones[:, :], yT[:, h], start=True, stop=True).then_inc(S["mean_sum"], 1)
            pe.wait_ge(S["ss_out"], HP)
            for h in range(HP):
                pe.wait_ge(S["yc_sq"], h + 1)
                pe.matmul(B[4 + h][:, 0:NT], c.half_ones[:, :], f2[:, h], start=True, stop=True).then_inc(S["var_sum"], 1)


GROUPS = (((0, 8), (8, 16), (16, 20)), ((0, 8), (8, 16)))



NEG = -1.0e30
TAKEN = -3.0e38
KP = 64
KS = 256
PAST = 1024
NPG = 8
KEYS = PAST + NS
CHUNKS = ((0, 512), (512, 512), (PAST, NS))
SCALE_A = 64 ** -0.5


def dsa_stage(c, z, vtok, ymix):
    nc = c.nc
    S = {n: c.stage_sem(n + "_ds") for n in (
        "par_loaded", "table_loaded", "kix_landed", "ki_sq", "ki_sum", "ki_sd", "ki_done", "wi_sum", "wi_done", "qi_done", "qz_zero", "qz_done",
        "ip_sum", "ip_rel", "ip_acc", "is_sum", "is_rel", "is_used", "is_acc", "is_out",
        "tp_max", "tp_rep", "mp_done", "ts_max", "ts_rep", "ms_done",
        "sp_sum", "sp_masked", "nb_done", "sp_exp", "pn_done", "pt_sum", "pt_out", "op_sum", "op_out",
        "ks_sum", "ks_out", "mb_sum", "mb_done", "ss_nb", "ss_exp", "ss_norm", "st_sum", "st_out", "pv_sum", "kv_used", "ys_done")}
    kv_landed = [c.sem(f"kv_landed{i}") for i in range(2)]
    with ExitStack() as ctx:
        def sb(n, shape, dt=F32):
            return c.sb(n + "_ds", shape, dt, ctx=ctx)
        table = sb("table", [1, NB * NPG], I32)
        kidg = sb("kidg", [P, 1])
        free_slots = sb("free_slots", [1, 1])
        cmask = sb("cmask", [P, 2, TP])
        nmask = sb("nmask", [NS, NS])
        esel = sb("esel", [16, P])
        wmask = sb("wmask", [P, 4, NS])
        bsel = sb("bsel", [NS, 2, P])
        kix = sb("kix", [P, NB, PAST])
        kisq, kisd = sb("kisq", [P, NT]), sb("kisd", [P, NT])
        wip, wsel = sb("wip", [P, 32]), sb("wsel", [P, 4, NS])
        qi = sb("qi", [P, NB, 8, TS])
        qz = sb("qz", [P, NB, HP, NS])
        spare = c.down[:, :].rearrange("p s k m -> p (s k m)")
        rel = spare[:, 0:3 * 512].rearrange("p (u n) -> p u n", u=3)
        sc = spare[:, 3 * 512:3 * 512 + 2 * KEYS].rearrange("p (g n) -> p g n", g=2)
        ip = sb("ip", [P, 2, TP])
        work = sb("work", [P, 2, TP])
        t8 = sb("t8", [P, 2, 8])
        mp = sb("mp", [P, 2, TP])
        iss, wks = sb("iss", [NS, KEYS]), sb("wks", [NS, KEYS])
        t8s = sb("t8s", [NS, 8])
        xflat = c.xscratch[:, :].rearrange("p k t -> p (k t)")
        pa = xflat[:, 0:4 * TP].rearrange("p (a b t) -> p a b t", a=2, b=2)
        pt = xflat[:, 4 * TP:8 * TP].rearrange("p (a b t) -> p a b t", a=2, b=2)
        mx, nb_, rs, ri = (sb(n, [P, 2, 2]) for n in ("mx", "nb", "rs", "ri"))
        mxs, nbs, rss, ris = (sb(n, [P, 2]) for n in ("mxs", "nbs", "rss", "ris"))
        pts = c.xg[:, :].rearrange("p k t -> p (k t)")[:, 0:9 * 2 * P].rearrange("p (g j r) -> p g j r", g=2, j=9)
        kv = c.ring[:, :].rearrange("p (s u) a k m -> p s (u a k m)", s=2)
        block = ctx.enter_context(nc.Block())
        B = c.banks
        q, k, qz_src, ki = z[:, 0:4], z[:, 4:8], z[:, 8:16], z[:, 30]

        def half(u):
            return slice(u * 64, u * 64 + 64)

        @block.sync
        def _(sp):
            sp.dma_start(table[:, :], c.ins["table"]).then_inc(S["table_loaded"], 16)
            for dst, src in ((kidg[:, :], "kidg"), (cmask[:, :, :], "cmask"), (nmask[:, :], "nmask"), (esel[:, :], "esel"),
                             (wmask[:, :, :], "wmask"), (bsel[:, :, :], "bsel")):
                sp.dma_start(dst, c.ins[src]).then_inc(S["par_loaded"], 16)
            sp.wait_ge(S["table_loaded"], 16)
            with sp.Fori(0, NB) as b:
                for j in range(NPG):
                    page = sp.value_load(table[0:1, bass.ds(b * NPG + j, 1)], min_val=0, max_val=c.n_pool - 1)
                    sp.dma_start(kix[:, bass.ds(b, 1), j * P:(j + 1) * P].rearrange("p a n -> p (a n)"),
                                 c.ins["cache_i"][bass.ds(page, 1)].rearrange("a p n -> (a p) n")).then_inc(S["kix_landed"], 16)
            for kind, src in ((0, "cache_k"), (1, "cache_v")):
                with sp.Fori(0, NB // 2) as i:
                    for s in range(2):
                        n = i * 2 + (kind * NB + s)
                        sp.wait_ge(S["kv_used"], n + 1)
                        for j in range(NPG):
                            page = sp.value_load(table[0:1, bass.ds(i * (2 * NPG) + (s * NPG + j), 1)], min_val=0, max_val=c.n_pool - 1)
                            sp.dma_start(kv[:, s, j * 512:(j + 1) * 512],
                                         c.ins[src][bass.ds(page, 1)].rearrange("a p n -> (a p) n")).then_inc(kv_landed[s], 16)
            sp.wait_ge(S["ki_done"], 1)
            c.store(sp, c.outs["kidx"], ki[0:64])

        @block.gpsimd
        def _(pool):
            pool.memset(free_slots[:, :], 2.0).then_inc(S["kv_used"], 2)
            pool.memset(qz[:, :, :, :], 0.0).then_inc(S["qz_zero"], 1)

        @block.tensor
        def _(pe):
            pe.wait_ge(S["ki_sq"], 1)
            pe.matmul(B[0][:, 0:NT], c.half_ones[:, :], kisq[:, :], start=True, stop=True).then_inc(S["ki_sum"], 1)
            pe.wait_ge(S["par_loaded"], 96)
            for t in range(2):
                pe.matmul(B[1][:, t * 16:t * 16 + 16], z[0:16, 31, t * P:t * P + P], c.ident[0:16, 0:16], start=True, stop=True)
            pe.matmul(B[1][:, 32:64], esel[:, :], z[0:16, 31, TP:NT], start=True, stop=True).then_inc(S["wi_sum"], 1)
            pe.wait_ge(S["ki_done"], 1)
            for u in range(16):
                t, j, p_ = u // 8, (u // 2) % 4, u % 2
                if u >= 4:
                    pe.wait_ge(S["ip_rel"], u - 3)
                for e in range(2):
                    mm = pe.matmul(B[2 + u % 4][:, e * TP:(e + 1) * TP], qz_src[half(p_), 2 * j + e, t * P:(t + 1) * P], ki[half(p_), 0:TP],
                                   start=True, stop=True)
                mm.then_inc(S["ip_sum"], 1)
            pe.wait_ge(S["qi_done"], 1)
            pe.wait_ge(S["wi_done"], 1)
            pe.wait_ge(S["ip_rel"], 16)

            def weigh(n):
                g, ch = n // 3, n % 3
                c0, w = CHUNKS[ch]
                pe.wait_ge(S["is_rel"], n + 1)
                pe.matmul(B[5 + ch][0:NS, 0:w], wsel[:, g], rel[:, n % 3, 0:w], start=(g == 0), stop=(g == 3)).then_inc(S["is_used"], 1)

            for n in range(12):
                g, ch = n // 3, n % 3
                c0, w = CHUNKS[ch]
                if ch == 0:
                    pe.wait_ge(S["kix_landed"], 16 * NB * NPG)
                if n >= 3:
                    pe.wait_ge(S["is_rel"], n - 2)
                for e in range(2):
                    for p_ in range(2):
                        b = 2 * g + e
                        o = 64 * e + 32 * p_
                        rhs = kix[half(p_), b, c0:c0 + w] if ch < 2 else ki[half(p_), TP:NT]
                        mm = pe.matmul(B[2 + n % 3][o:o + 32, 0:w], qi[half(p_), b].rearrange("p h t -> p (h t)"), rhs, start=True, stop=True)
                mm.then_inc(S["is_sum"], 1)
                if n >= 1:
                    weigh(n - 1)
            weigh(11)
            pe.wait_ge(S["wi_done"], 1)

            def probs_out(h):
                pe.wait_ge(S["pn_done"], h + 1)
                if h >= 2:
                    pe.wait_ge(S["pt_out"], h - 1)
                for kt in range(2):
                    for t in range(2):
                        mm = pe.transpose(B[2 + h % 2][:, kt * TP + t * P:kt * TP + t * P + P], pa[:, h % 2, t, kt * P:kt * P + P], c.ident[:, :])
                mm.then_inc(S["pt_sum"], 1)

            def values(h):
                hp, p_ = h // 2, h % 2
                pe.wait_ge(S["pt_out"], h + 1)
                if h == 0:
                    pe.wait_ge(S["is_rel"], 12)
                if p_ == 0 and hp >= 1:
                    pe.wait_ge(S["op_out"], hp)
                for kt in range(2):
                    mm = pe.matmul(B[4][half(p_), 0:TP], vtok[:, kt, h * 64:h * 64 + 64], pt[:, h % 2, kt], start=(kt == 0), stop=(kt == 1))
                mm.then_inc(S["op_sum"], 1)

            for h in range(8):
                if h >= 2:
                    pe.wait_ge(S["sp_masked"], h - 1)
                for t in range(2):
                    mm = pe.matmul(B[h % 2][:, t * TP:(t + 1) * TP], q[half(h % 2), h // 2, t * P:(t + 1) * P], k[half(h % 2), h // 2, 0:TP],
                                   start=True, stop=True)
                mm.then_inc(S["sp_sum"], 1)
                if h >= 1:
                    probs_out(h - 1)
                if h >= 2:
                    values(h - 2)
            probs_out(7)
            values(6)
            values(7)
            pe.wait_ge(S["qz_done"], 1)
            pe.wait_ge(S["is_out"], 3)
            pe.wait_ge(S["op_out"], 4)
            pe.wait_ge(S["pt_out"], 8)
            for b in range(NB):
                g, b4 = b // 4, b % 4
                pe.wait_ge(kv_landed[b % 2], 128 * (b // 2 + 1))
                kb = kv[:, b % 2].rearrange("p (j h n) -> p j h n", j=NPG, h=HP)
                for ch, (c0, w) in enumerate(CHUNKS):
                    for h in range(HP):
                        rhs = kb[:, 4 * ch:4 * ch + 4, h] if ch < 2 else k[:, h, TP:NT]
                        mm = pe.matmul(B[3 * g + ch][32 * b4:32 * b4 + 32, 0:w], qz[:, b, h], rhs, start=(h == 0), stop=(h == HP - 1))
                    if ch == 1:
                        mm.then_inc(S["kv_used"], 1)
                mm.then_inc(S["ks_sum"], 1)
            pe.wait_ge(S["ms_done"], 1)
            for n in range(6):
                g, ch = n // 3, n % 3
                c0, w = CHUNKS[ch]
                if n >= 2:
                    pe.wait_ge(S["mb_done"], n - 1)
                pe.matmul(B[6 + n % 2][:, 0:w], bsel[:, g], iss[:, c0:c0 + w], start=True, stop=True).then_inc(S["mb_sum"], 1)
            pe.wait_ge(S["ks_out"], 6)
            for g in range(2):
                pe.wait_ge(S["ss_norm"], g + 1)
                for m in range(3):
                    n = 3 * g + m
                    if n >= 3:
                        pe.wait_ge(S["st_out"], n - 2)
                    for j in range(4 * m, min(4 * m + 4, 9)):
                        w = P if j < 8 else NS
                        mm = pe.transpose(B[m][0:w, (j - 4 * m) * P:(j - 4 * m + 1) * P], sc[:, g, j * P:j * P + w], c.ident[:, :])
                    mm.then_inc(S["st_sum"], 1)
            for b in range(NB):
                g, b4 = b // 4, b % 4
                n = NB + b
                pe.wait_ge(kv_landed[b % 2], 128 * (n // 2 + 1))
                if b4 == 0:
                    pe.wait_ge(S["st_out"], 3 * g + 3)
                vb = kv[:, b % 2].rearrange("p (j n) -> p j n", j=NPG)
                for h in range(HP):
                    cols = slice(32 * b4 + 8 * h, 32 * b4 + 8 * h + 8)
                    o = (b * HP + h) * 8
                    for j in range(NPG):
                        pe.matmul(B[5][:, o:o + 8], vb[:, j, h * P:h * P + P], pts[:, g, j, cols], start=(j == 0), stop=False)
                    mm = pe.matmul(B[5][:, o:o + 8], vtok[0:NS, 2, h * P:h * P + P], pts[0:NS, g, 8, cols], start=False, stop=True)
                mm.then_inc(S["kv_used"] if b < NB - 1 else S["pv_sum"], 1)

        def pt_out(act, h):
            act.wait_ge(S["pt_sum"], h + 1)
            if h >= 2:
                act.wait_ge(S["op_sum"], h - 1)
            act.activation(pt[:, h % 2], B[2 + h % 2][:, :].rearrange("p (k n) -> p k n", k=2), ACT.Copy).then_inc(S["pt_out"], 1)

        @block.scalar
        def _(act):
            act.activation(kisq[:, :], ki, ACT.Square).then_inc(S["ki_sq"], 1)
            act.wait_ge(S["ki_sum"], 1)
            act.activation(kisd[:, :], B[0][:, 0:NT], ACT.Sqrt, scale=1.0 / 64, bias=c.eps[:, 0:1]).then_inc(S["ki_sd"], 1)
            for u in range(16):
                act.wait_ge(S["ip_sum"], u + 1)
                if u >= 3:
                    act.wait_ge(S["ip_acc"], 2 * (u - 2))
                act.activation(rel[:, u % 3], B[2 + u % 4][:, :], ACT.Relu).then_inc(S["ip_rel"], 1)
            act.wait_ge(S["ip_acc"], 32)
            for n in range(12):
                w = CHUNKS[n % 3][1]
                act.wait_ge(S["is_sum"], n + 1)
                if n >= 3:
                    act.wait_ge(S["is_used"], n - 2)
                act.activation(rel[:, n % 3, 0:w], B[2 + n % 3][:, 0:w], ACT.Relu).then_inc(S["is_rel"], 1)
            for h in range(8):
                act.wait_ge(S["nb_done"], h + 1)
                if h >= 2:
                    act.wait_ge(S["pn_done"], h - 1)
                for t in range(2):
                    ins = act.activation(pa[:, h % 2, t], pa[:, h % 2, t], ACT.Exp, scale=SCALE_A, bias=nb_[:, h % 2, t:t + 1],
                                         accum_out=rs[:, h % 2, t:t + 1])
                ins.then_inc(S["sp_exp"], 1)
                if h >= 1:
                    pt_out(act, h - 1)
            pt_out(act, 7)
            for n in range(6):
                g, ch = n // 3, n % 3
                c0, w = CHUNKS[ch]
                act.wait_ge(S["ks_sum"], 4 * g + 4)
                act.activation(sc[:, g, c0:c0 + w], B[3 * g + ch][:, 0:w], ACT.Copy).then_inc(S["ks_out"], 1)
            for g in range(2):
                act.wait_ge(S["ss_nb"], g + 1)
                act.activation(sc[:, g], sc[:, g], ACT.Exp, scale=SCALE_A, bias=nbs[:, g:g + 1], accum_out=rss[:, g:g + 1]).then_inc(S["ss_exp"], 1)
            for n in range(6):
                g, m = n // 3, n % 3
                act.wait_ge(S["st_sum"], n + 1)
                if m < 2:
                    act.activation(pts[:, g, 4 * m:4 * m + 4], B[m][:, :].rearrange("p (j r) -> p j r", j=4), ACT.Copy).then_inc(S["st_out"], 1)
                else:
                    act.activation(pts[0:NS, g, 8], B[m][0:NS, 0:P], ACT.Copy).then_inc(S["st_out"], 1)

        @block.vector
        def _(dve):
            def ln(ins):
                c.link(dve, "dve", ins)
            dve.wait_ge(S["par_loaded"], 96)
            dve.wait_ge(S["ki_sd"], 1)
            ln(dve.reciprocal(kisd[:, :], kisd[:, :]))
            dve.scalar_tensor_tensor(ki, ki, kidg[:, 0:1], kisd[:, :], ALU.mult, ALU.mult).then_inc(S["ki_done"], 1)
            dve.wait_ge(S["wi_sum"], 1)
            dve.tensor_scalar(wip[:, :], B[1][:, 0:32], 1.0 / 32, None, ALU.mult)
            dve.tensor_tensor(wsel[:, :, :], wmask[:, :, :], B[1][:, 32:64].rearrange("p (a n) -> p a n", a=1).to_broadcast([P, 4, NS]),
                              ALU.mult).then_inc(S["wi_done"], 1)
            dve.tensor_copy(qi[:, :, :, :], qz_src[:, :, TP:NT].rearrange("p h (b t) -> p b h t", t=TS)).then_inc(S["qi_done"], 1)
            ln(dve.tensor_copy(ip[:, :, :], cmask[:, :, :]))
            n = 0
            for u in range(16):
                t, j, p_ = u // 8, (u // 2) % 4, u % 2
                dve.wait_ge(S["ip_rel"], u + 1)
                for e in range(2):
                    h = 2 * (2 * j + e) + p_
                    if n and n != 16:
                        dve.wait_ge(S["ip_acc"], n)
                    dve.scalar_tensor_tensor(ip[:, t], rel[:, u % 3, e * TP:(e + 1) * TP], wip[:, t * 16 + h:t * 16 + h + 1], ip[:, t],
                                             ALU.mult, ALU.add).then_inc(S["ip_acc"], 1)
                    n += 1
            dve.wait_ge(S["ip_acc"], 32)
            ln(dve.tensor_copy(work[:, :, :], ip[:, :, :]))
            n = 0
            for i in range(KP // 8):
                for t in range(2):
                    if i:
                        dve.wait_ge(S["tp_rep"], n - 1)
                    dve.max(t8[:, t], work[:, t]).then_inc(S["tp_max"], 1)
                    n += 1
                for t in range(2):
                    dve.wait_ge(S["tp_max"], n - 1 + t)
                    dve.match_replace(out=work[:, t], in_to_replace=t8[:, t], in_values=work[:, t], imm_value=TAKEN).then_inc(S["tp_rep"], 1)
            dve.wait_ge(S["tp_rep"], n)
            ln(dve.tensor_scalar(work[:, :, :], work[:, :, :], -2.0e38, NEG, ALU.is_gt, ALU.mult))
            ln(dve.tensor_tensor(mp[:, :, :], work[:, :, :], cmask[:, :, :], ALU.add))
            dve.wait_ge(S["qz_zero"], 1)
            for h in range(HP):
                for p_ in range(2):
                    last = dve.tensor_copy(qz[half(p_), :, h, (2 * h + p_) * TS:(2 * h + p_) * TS + TS],
                                           q[half(p_), h, TP:NT].rearrange("p (b t) -> p b t", t=TS))
            last.then_inc(S["qz_done"], 1)

            def head(h):
                bf = h % 2
                dve.wait_ge(S["sp_sum"], h + 1)
                if h >= 2:
                    dve.wait_ge(S["pt_sum"], h - 1)
                dve.tensor_tensor(pa[:, bf], B[bf][:, :].rearrange("p (t n) -> p t n", t=2), mp[:, :, :], ALU.add).then_inc(S["sp_masked"], 1)
                dve.wait_ge(S["sp_masked"], h + 1)
                ln(dve.tensor_reduce(mx[:, bf], pa[:, bf], AX_X, ALU.max))
                dve.tensor_scalar(nb_[:, bf], mx[:, bf], -SCALE_A, None, ALU.mult).then_inc(S["nb_done"], 1)

            def norm(h):
                bf = h % 2
                dve.wait_ge(S["sp_exp"], h + 1)
                ln(dve.reciprocal(ri[:, bf], rs[:, bf]))
                for t in range(2):
                    last = dve.tensor_scalar(pa[:, bf, t], pa[:, bf, t], ri[:, bf, t:t + 1], None, ALU.mult)
                last.then_inc(S["pn_done"], 1)

            def out(hp):
                dve.wait_ge(S["op_sum"], 2 * hp + 2)
                dve.tensor_copy(ymix[:, hp, 0:TP], B[4][:, 0:TP]).then_inc(S["op_out"], 1)

            for ch, (c0, w) in enumerate(CHUNKS):
                dve.wait_ge(S["is_used"], 10 + ch)
                if ch < 2:
                    dve.tensor_copy(iss[:, c0:c0 + w], B[5 + ch][0:NS, 0:w]).then_inc(S["is_out"], 1)
                else:
                    dve.tensor_tensor(iss[:, c0:c0 + w], B[5 + ch][0:NS, 0:w], nmask[:, :], ALU.add).then_inc(S["is_out"], 1)
            for h in range(8):
                head(h)
                if h >= 1:
                    norm(h - 1)
                if h >= 4 and h % 2 == 0:
                    out(h // 2 - 2)
            norm(7)
            out(2)
            out(3)
            dve.wait_ge(S["is_out"], 3)
            ln(dve.tensor_copy(wks[:, :], iss[:, :]))
            dve.max(t8s[:, :], wks[:, :]).then_inc(S["ts_max"], 1)
            dve.wait_ge(S["ts_max"], 1)
            dve.match_replace(out=wks[:, :], in_to_replace=t8s[:, :], in_values=wks[:, :], imm_value=TAKEN).then_inc(S["ts_rep"], 1)
            for i in range(1, KS // 8):
                dve.wait_ge(S["ts_rep"], i)
                dve.max(t8s[:, :], wks[:, :]).then_inc(S["ts_max"], 1)
                dve.wait_ge(S["ts_max"], i + 1)
                dve.match_replace(out=wks[:, :], in_to_replace=t8s[:, :], in_values=wks[:, :], imm_value=TAKEN).then_inc(S["ts_rep"], 1)
            dve.wait_ge(S["ts_rep"], KS // 8)
            ln(dve.tensor_scalar(iss[:, :], wks[:, :], -2.0e38, NEG, ALU.is_gt, ALU.mult))
            dve.tensor_tensor(iss[:, PAST:KEYS], iss[:, PAST:KEYS], nmask[:, :], ALU.add).then_inc(S["ms_done"], 1)
            for g in range(2):
                for ch, (c0, w) in enumerate(CHUNKS):
                    n = 3 * g + ch
                    dve.wait_ge(S["ks_out"], n + 1)
                    dve.wait_ge(S["mb_sum"], n + 1)
                    dve.tensor_tensor(sc[:, g, c0:c0 + w], sc[:, g, c0:c0 + w], B[6 + n % 2][:, 0:w], ALU.add).then_inc(S["mb_done"], 1)
                dve.wait_ge(S["mb_done"], 3 * g + 3)
                ln(dve.tensor_reduce(mxs[:, g:g + 1], sc[:, g], AX_X, ALU.max))
                dve.tensor_scalar(nbs[:, g:g + 1], mxs[:, g:g + 1], -SCALE_A, None, ALU.mult).then_inc(S["ss_nb"], 1)
            for g in range(2):
                dve.wait_ge(S["ss_exp"], g + 1)
                ln(dve.reciprocal(ris[:, g:g + 1], rss[:, g:g + 1]))
                dve.tensor_scalar(sc[:, g], sc[:, g], ris[:, g:g + 1], None, ALU.mult).then_inc(S["ss_norm"], 1)
            dve.wait_ge(S["pv_sum"], 1)
            for p_ in range(2):
                src = B[5][half(p_), 0:NB * HP * 8].rearrange("p (b h q t) -> p b h q t", b=NB, h=HP, q=2)
                dve.tensor_copy(ymix[half(p_), 0:HP, TP:NT].rearrange("p h (b t) -> p b h t", t=TS), src[:, :, :, p_])



def cd_in_stage(c, z, vtok):
    nc, npairs = c.nc, 8
    stream = c.ins["w_cd"]
    z_done, v_sum, rt_sum, rt_sd, rt_ready, v_done = (
        c.sem(n + "_cd") for n in ("z_done", "v_sum", "rt_sum", "rt_sd", "rt_ready", "v_done"))
    first = c.pairs
    assert first % RING == 0
    with ExitStack() as ctx:
        rt = c.sb("rt_cd", [P, 2, 3], ctx=ctx)
        whi = c.sb("whi_cd", [P, 2, 2, KT, P], F32R, ctx=ctx)
        block = ctx.enter_context(nc.Block())

        @block.sync
        def _(sp):
            send_pairs(c, sp, stream, RING, 9)

        @block.tensor
        def _(pe):
            project_pe(c, pe, whi, z_done, npairs)
            token_rstd_pe(c, pe, rt_sum)
            for w in range(2):
                if w == 1:
                    pe.wait_ge(v_done, 3)
                project_values(c, pe, whi, first + npairs + 2 * w,
                               lambda i, mm: mm.then_inc(*((v_sum, 1) if i < 2 else (c.pair_done, 2))))
            s, b = (first + 12) % RING, (first + 12) % 2
            pe.wait_ge(c.pair_split, first + 13)
            pe.wait_ge(z_done, npairs)
            for half in range(2):
                for k in range(KT):
                    mm = three_products(pe, c.banks[half][:, 0:NT], whi[:, b, half, k], c.ring_lo[:, s, half, k], c.xhi[:, k], c.xlo[:, k],
                                        k == 0, k == KT - 1)
            mm.then_inc(c.pair_done, 1)

        @block.scalar
        def _(act):
            act.wait_ge(rt_sum, 1)
            for i, (t0, n) in enumerate(TOK):
                act.activation(rt[0:n, 0, i:i + 1], c.banks[7][0:n, i:i + 1], ACT.Sqrt, scale=1.0 / D_MODEL,
                               bias=c.eps[0:n, 0:1]).then_inc(rt_sd, 1)
            for w in range(2):
                for i, (t0, n) in enumerate(TOK):
                    act.wait_ge(rt_ready, i + 1)
                    if i < 2:
                        act.wait_ge(v_sum, 2 * w + i + 1)
                    else:
                        act.wait_ge(c.pair_done, first + npairs + 2 * w + 2)
                    act.activation(vtok[0:n, 3 * w + i], c.banks[4 + i][0:n, :], ACT.Copy, scale=rt[0:n, 1, i:i + 1]).then_inc(v_done, 1)

        @block.vector
        def _(dve):
            project_dve(c, dve, whi, z, z_done, npairs, first)
            for i, (t0, n) in enumerate(TOK):
                dve.wait_ge(rt_sd, i + 1)
                dve.reciprocal(rt[0:n, 1, i:i + 1], rt[0:n, 0, i:i + 1]).then_inc(rt_ready, 1)
            for u in range(10, 13):
                dve.wait_ge(c.pair_done, first + (10 if u < 12 else 12))
                split_pair(c, dve, whi, first, u)
            dve.wait_ge(c.pair_done, first + 13)
            for half in range(2):
                dve.tensor_tensor(z[:, 16 + half], c.banks[half][:, 0:NT], c.rstd[:, :], ALU.mult)

    c.pairs += npairs + 5


SEQ = TP + TS - 1
ST_COLS = 384
EXT = 3 + TP


def cd_mix_stage(c, z, vtok, ymix):
    nc = c.nc
    S = {n: c.sem(n + "_cm") for n in (
        "par_loaded", "rs_loaded", "c_loaded", "rot_sum", "rope_done", "qdec_done", "ext_pad", "ext_done", "conv_out", "conv_done", "silu_done",
        "gate_x", "gate_e", "gate_ln", "gate_arg", "gate_exp", "m_done", "s_sum", "s_out", "kt_sum", "kt_out", "y_sum", "y_out", "rp_sum", "rp_out",
        "vb_done", "rn_sum", "rn_out", "e_sum", "e_min", "e_exp", "qk_sum", "a_done", "emj_sum", "emj_out", "sq_sum", "qsc_done", "car_sum", "car_out",
        "wt_sum", "wt_out", "kd_sum", "kd_out", "num_sum", "h_done", "cp_sum", "cp_out", "kb_done", "cn_sum", "cn_out", "n_sum", "n_out",
        "mean_sum", "yc_done", "yc_sq", "var_sum", "var_sd", "gates_done")}
    with ExitStack() as ctx:
        def sb(n, shape, dt=F32):
            return c.sb(n + "_cm", shape, dt, ctx=ctx)
        par = sb("par", [P, 8 + 4 * 5 + 2])
        gn, tap, g4 = par[:, 0:8], par[:, 8:28].rearrange("p (a i) -> p a i", i=5), par[:, 28:30]
        ifb = sb("ifb", [4, 2])
        cs = sb("cs", [P, 2, NT])
        rot = sb("rot", [P, P])
        dmask, dms = sb("dmask", [P, 4, TP]), sb("dms", [NS, 4, NS])
        gq = sb("gq", [P, 2, NS])
        wS = sb("wS", [P, 3, 4])
        lmask, lms = sb("lmask", [P, TP]), sb("lms", [NS, NS])
        sel = sb("sel", [4, 4, P])
        selq = sb("selq", [4, 2, P])
        rows = sb("rows", [4, 2, NT])
        m0 = sb("m0", [4, 1 + NB])
        bm = sb("bm", [NS, NB])
        convT = sb("convT", [P, 4, NB, 3])
        spare = c.ring[:, :].rearrange("p s a k m -> p (s a k m)")
        rs0 = spare[:, 0:2048].rearrange("p (b h e) -> p b h e", b=NB, h=2)
        c0t = spare[:, 2048:4096].rearrange("p (b h e) -> p b h e", b=NB, h=2)
        c0 = spare[:, 4096:6144].rearrange("p (b h d) -> p b h d", b=NB, h=4)
        ext = spare[:, 6144:6144 + 4 * 315].rearrange("p (a n) -> p a n", a=4)
        spare2 = c.down[:, :].rearrange("p s k m -> p (s k m)")
        scT = spare2[:, 0:8 * ST_COLS].rearrange("p (h n) -> p h n", h=8)
        E = spare2[:, 8 * ST_COLS:12 * ST_COLS].rearrange("p (h n) -> p h n", h=4)
        n0 = sb("n0", [NB, 256])
        n0t = sb("n0t", [P, NB, 2])
        tmp = sb("tmp", [P, 2, NT])
        qdec, qsc, qn = sb("qdec", [P, 2, NS]), sb("qsc", [P, 2, NS]), sb("qn", [P, 2, NS])
        cacc = sb("cacc", [P, 4, NT])
        qk = sb("qk", [P, 4, NT])
        clast = sb("clast", [P, 4, 3 * (1 + NB)])
        g = sb("g", [4, 9, NT])
        gx, gn_, ge, gb, gu, gM, gsc, gem, gws = (g[:, j] for j in range(9))
        negM = sb("negM", [4, NT])
        car, mnew = sb("car", [4, NB]), sb("mnew", [4, 1 + NB])
        scs = sb("scs", [NS, 8, NS])
        Es = sb("Es", [NS, 4, NS])
        kw, kws = sb("kw", [P, 3, 256]), sb("kws", [P, 3, 256])
        wt = sb("wt", [P, 3, 4])
        emj = sb("emj", [P, 4, NT])
        carp = sb("carp", [P, 4, NB])
        carb = sb("carb", [NB, 4])
        VB = sb("VB", [NS, 2, NB, P])
        KB = sb("KB", [NS, 4, NB, 64])
        hN = c.xscratch
        hd, hr = sb("hd", [P, NT]), sb("hr", [P, NT])
        yc, ysq = c.xg, sb("ysq", [P, 8, NT])
        rsp = spare2[:, 4608:4864].rearrange("p (h e) -> p h e", h=2)
        csp = spare2[:, 4864:5120].rearrange("p (h d) -> p h d", h=4)
        nsp = spare2[0:1, 5120:5376]
        block = ctx.enter_context(nc.Block())
        B = c.banks
        vc, vd = vtok[:, 0:3], vtok[:, 3:6]
        Q, K, GC, OG = z[:, 0:2], z[:, 2:4], z[:, 4:8], z[:, 12:16]

        def half(u):
            return slice(u * 64, u * 64 + 64)

        def sel_row(h):
            return sel[:, h, 0:1].to_broadcast([4, TP])

        def seqs_(ap):
            return ap.rearrange("p (b t) -> p b t", t=TS)

        def seqs(ap):
            return ap[..., TP:NT].rearrange("p (b t) -> p b t", t=TS)

        @block.sync
        def _(sp):
            loads = [(par[:, :], "cd_par"), (ifb[:, :], "ifb"), (cs[:, :, :], "cs"), (rot[:, :], "rot"), (dmask[:, :, :], "dmask"),
                     (dms[:, :, :], "dms"), (gq[:, :, :], "gq"), (wS[:, :, :], "wS"), (lmask[:, :], "lmask"), (lms[:, :], "lms"),
                     (sel[:, :, :], "sel"), (selq[:, :, :], "selq"), (rows[:, :, :], "rows"), (m0[:, :], "m0"), (bm[:, :], "bm"),
                     (convT[:, :, :, :], "convT"), (n0[:, :], "n0"), (n0t[:, :, :], "n0t")]
            assert len(loads) == 18
            for dst, src in loads:
                sp.dma_start(dst, c.ins[src]).then_inc(S["par_loaded"], 16)
            sp.dma_start(rs0, c.ins["rs0"]).then_inc(S["rs_loaded"], 16)
            sp.dma_start(c0t, c.ins["c0t"]).then_inc(S["c_loaded"], 16)
            sp.dma_start(c0, c.ins["c0"]).then_inc(S["c_loaded"], 16)
            sp.wait_ge(S["conv_out"], 2)
            c.store(sp, c.outs["conv"], clast[:, :, :])
            sp.wait_ge(S["gate_arg"], 1)
            c.store(sp, c.outs["m"], mnew[:, :])
            sp.wait_ge(S["rp_out"], 1)
            c.store(sp, c.outs["ret_p"], rsp[:, :, :])
            sp.wait_ge(S["rn_out"], 4)
            c.store(sp, c.outs["ret_s"], rs0)
            sp.wait_ge(S["cp_out"], 1)
            c.store(sp, c.outs["C_p"], csp[:, :, :])
            sp.wait_ge(S["cn_out"], 4)
            c.store(sp, c.outs["C_s"], c0)
            sp.wait_ge(S["n_out"], 2)
            c.store(sp, c.outs["n_p"], nsp[:, :])
            c.store(sp, c.outs["n_s"], n0[:, :])

        @block.gpsimd
        def _(pool):
            pool.memset(ext[:, :, 0:3], 0.0).then_inc(S["ext_pad"], 1)

        @block.vector
        def _(dve):
            def ln(ins):
                c.link(dve, "dve", ins)
            dve.wait_ge(S["par_loaded"], 16 * 18)
            ln(dve.tensor_scalar(gx, z[0:4, 17], ifb[:, 1:2], None, ALU.add))
            ln(dve.tensor_scalar(gn_, gx, -1.0, None, ALU.mult))
            dve.tensor_tensor(ge, gx, gn_, ALU.min).then_inc(S["gate_x"], 1)
            dve.tensor_scalar(gx, gx, 0.0, None, ALU.min)
            dve.tensor_scalar(gu, z[0:4, 16], ifb[:, 0:1], None, ALU.add)
            for i in range(4):
                dve.wait_ge(S["rot_sum"], i + 1)
                dve.tensor_tensor(tmp[:, 0], z[:, i], cs[:, 0], ALU.mult)
                ln(dve.tensor_tensor(tmp[:, 1], B[i][:, 0:NT], cs[:, 1], ALU.mult))
                dve.tensor_tensor(z[:, i], tmp[:, 0], tmp[:, 1], ALU.add).then_inc(S["rope_done"], 1)
                dve.wait_ge(S["rope_done"], i + 1)
            dve.tensor_tensor(qdec[:, :, :], Q[:, :, TP:NT], gq[:, :, :], ALU.mult).then_inc(S["qdec_done"], 1)
            dve.wait_ge(S["gate_ln"], 1)
            ln(dve.tensor_tensor(gx, gx, ge, ALU.subtract))
            ln(dve.tensor_tensor_scan(gb, rows[:, 0], gx, 0.0, ALU.mult, ALU.add))
            ln(dve.tensor_tensor(gu, gu, gb, ALU.subtract))
            ln(dve.tensor_copy(gn_, gu))
            dve.tensor_scalar(gn_[:, 0:1], gu[:, 0:1], 0.0, None, ALU.max)
            ln(dve.tensor_tensor(gn_[:, TP:NT:TS], gu[:, TP:NT:TS], m0[:, 1:], ALU.max))
            ln(dve.tensor_tensor_scan(gM, rows[:, 1], gn_, 0.0, ALU.add, ALU.max))
            dve.tensor_scalar(negM[:, :], gM, -1.0, None, ALU.mult)
            dve.tensor_tensor(seqs(gsc), m0[:, 1:].rearrange("p (b a) -> p b a", a=1).to_broadcast([4, NB, TS]), seqs(gM), ALU.subtract)
            ln(dve.tensor_tensor(gem, gb, gM, ALU.add))
            dve.tensor_scalar(gws[:, 0:TP], gu[:, 0:TP], gM[:, TP - 1:TP], None, ALU.subtract)
            dve.tensor_tensor(seqs(gws), seqs(gu), gM[:, SEQ::TS].rearrange("p (b a) -> p b a", a=1).to_broadcast([4, NB, TS]), ALU.subtract)
            dve.tensor_tensor(car[:, :], m0[:, 1:], gM[:, SEQ::TS], ALU.subtract)
            dve.tensor_copy(mnew[:, 0:1], gem[:, TP - 1:TP])
            dve.tensor_copy(mnew[:, 1:], gem[:, SEQ::TS]).then_inc(S["gate_arg"], 1)
            for h in range(4):
                dve.wait_ge(S["s_sum"], h + 1)
                dve.tensor_tensor(scT[:, h, 0:TP], B[h][:, 0:TP], dmask[:, h], ALU.mult)
                dve.tensor_tensor(scT[:, h, TP:ST_COLS], B[h][:, TP:ST_COLS], dmask[:, h, 0:P], ALU.mult)
                dve.tensor_tensor(scs[:, h], B[h][0:NS, ST_COLS:ST_COLS + NS], dms[:, h], ALU.mult).then_inc(S["s_out"], 1)
            dve.wait_ge(S["kt_sum"], 1)
            for i, (t0, n) in enumerate(TOK):
                last = dve.tensor_tensor(kw[0:n, i].rearrange("p (h d) -> p h d", h=4),
                                         B[4 + i // 2][0:n, (i % 2) * 256:(i % 2) * 256 + 256].rearrange("p (h d) -> p h d", h=4),
                                         wS[0:n, i].rearrange("p (h a) -> p h a", a=1).to_broadcast([n, 4, 64]), ALU.mult)
            last.then_inc(S["kt_out"], 1)
            dve.wait_ge(S["ext_pad"], 1)
            es = ext[:, :, EXT:].rearrange("p a (b t) -> p a b t", t=7)
            dve.tensor_copy(ext[:, :, 3:EXT], z[:, 8:12, 0:TP])
            for a in range(4):
                dve.tensor_copy(es[:, a, :, 0:3], convT[:, a])
                last = dve.tensor_copy(es[:, a, :, 3:7], seqs(z[:, 8 + a]))
            ln(last)
            dve.tensor_copy(clast[:, :, 0:3], ext[:, :, TP:EXT]).then_inc(S["conv_out"], 1)
            for a in range(4):
                last = dve.tensor_copy(clast[:, a, 3:].rearrange("p (b t) -> p b t", t=3), es[:, a, :, 4:7])
            last.then_inc(S["conv_out"], 1)
            for i in range(4):
                for a in range(4):
                    for dst, src in ((cacc[:, a, 0:TP], ext[:, a, 3 - i:3 - i + TP]), (seqs(cacc[:, a]), es[:, a, :, 3 - i:7 - i])):
                        if i == 0:
                            last = dve.tensor_scalar(dst, src, tap[:, a, 3:4], tap[:, a, 4:5], ALU.mult, ALU.add)
                        else:
                            last = dve.scalar_tensor_tensor(dst, src, tap[:, a, 3 - i:4 - i], dst, ALU.mult, ALU.add)
                if i < 3:
                    ln(last)
            last.then_inc(S["conv_done"], 1)
            for hp in range(2):
                if hp:
                    dve.wait_ge(S["rn_sum"], 1)
                for p_ in range(2):
                    h = 2 * hp + p_
                    last = dve.tensor_tensor(VB[:, p_], vc[0:NS, 2, h * P:h * P + P].rearrange("p (a e) -> p a e", a=1).to_broadcast([NS, NB, P]),
                                             bm[:, :].rearrange("p (b a) -> p b a", a=1).to_broadcast([NS, NB, P]), ALU.mult)
                last.then_inc(S["vb_done"], 1)
                dve.wait_ge(S["rn_sum"], hp + 1)
                for m in range(2):
                    dve.scalar_tensor_tensor(rs0[:, 4 * m:4 * m + 4, hp], rs0[:, 4 * m:4 * m + 4, hp], g4[:, hp:hp + 1],
                                             B[6 + m][:, :].rearrange("p (b e) -> p b e", b=4), ALU.mult, ALU.add).then_inc(S["rn_out"], 1)
            for h in range(4):
                dve.wait_ge(S["e_exp"], h + 1)
                dve.wait_ge(S["qk_sum"], h + 1)
                bk = B[4 + h % 2]
                dve.scalar_tensor_tensor(scT[:, 4 + h], bk[:, 0:ST_COLS], 0.125, E[:, h], ALU.mult, ALU.mult)
                dve.scalar_tensor_tensor(scs[:, 4 + h], bk[0:NS, ST_COLS:ST_COLS + NS], 0.125, Es[:, h], ALU.mult, ALU.mult).then_inc(S["a_done"], 1)
            dve.wait_ge(S["sq_sum"], 1)
            ln(dve.tensor_tensor(qsc[:, :, :], qk[:, 0:2, TP:NT], B[6][:, 0:2 * NS].rearrange("p (h n) -> p h n", h=2), ALU.mult))
            for hp in range(2):
                last = dve.tensor_tensor(seqs_(qn[:, hp]), seqs_(qsc[:, hp]), n0t[:, :, hp:hp + 1].to_broadcast([P, NB, TS]), ALU.mult)
            last.then_inc(S["qsc_done"], 1)
            dve.wait_ge(S["wt_sum"], 1)
            ln(dve.tensor_scalar(wt[:, 0:2], B[7][:, 0:8].rearrange("p (i h) -> p i h", i=2), 0.125, None, ALU.mult))
            ln(dve.tensor_scalar(wt[0:NS, 2], B[7][0:NS, 8:12], 0.125, None, ALU.mult))
            dve.wait_ge(S["kd_sum"], 1)
            for i, (t0, n) in enumerate(TOK):
                last = dve.tensor_tensor(kws[0:n, i].rearrange("p (h d) -> p h d", h=4),
                                         B[4 + i // 2][0:n, (i % 2) * 256:(i % 2) * 256 + 256].rearrange("p (h d) -> p h d", h=4),
                                         wt[0:n, i].rearrange("p (h a) -> p h a", a=1).to_broadcast([n, 4, 64]), ALU.mult)
            last.then_inc(S["kd_out"], 1)
            for h in range(4):
                dve.wait_ge(S["num_sum"], h + 1)
                dve.wait_ge(S["emj_out"], 4)
                bn = 2 * (h % 2)
                ln(dve.scalar_tensor_tensor(hd[:, :], B[bn + 1][:, 0:NT], -1.0, emj[:, h], ALU.mult, ALU.max))
                ln(dve.tensor_tensor(hd[:, :], B[bn + 1][:, 0:NT], hd[:, :], ALU.max))
                ln(dve.reciprocal(hr[:, :], hd[:, :]))
                dve.tensor_tensor(hN[:, 4 + h], B[bn][:, 0:NT], hr[:, :], ALU.mult).then_inc(S["h_done"], 1)
            dve.wait_ge(S["kd_out"], 1)
            for h in range(4):
                last = dve.tensor_tensor(KB[:, h], kws[0:NS, 2, h * 64:h * 64 + 64].rearrange("p (a d) -> p a d", a=1).to_broadcast([NS, NB, 64]),
                                         bm[:, :].rearrange("p (b a) -> p b a", a=1).to_broadcast([NS, NB, 64]), ALU.mult)
                last.then_inc(S["kb_done"], 1)
            for h in range(4):
                dve.wait_ge(S["car_out"], 1)
                ln(dve.tensor_tensor(c0[:, :, h], c0[:, :, h], carp[:, h].rearrange("p (b a) -> p b a", a=1).to_broadcast([P, NB, 64]), ALU.mult))
                dve.wait_ge(S["cn_sum"], h + 1)
                dve.tensor_tensor(c0[:, :, h], c0[:, :, h], B[4 + h % 2][:, :].rearrange("p (b d) -> p b d", b=NB), ALU.add).then_inc(S["cn_out"], 1)
            ln(dve.tensor_tensor(n0[:, :].rearrange("p (h d) -> p h d", h=4), n0[:, :].rearrange("p (h d) -> p h d", h=4),
                                 carb[:, :].rearrange("p (h a) -> p h a", a=1).to_broadcast([NB, 4, 64]), ALU.mult))
            dve.wait_ge(S["n_sum"], 1)
            dve.tensor_tensor(n0[:, :], n0[:, :], B[7][0:NB, 0:256], ALU.add).then_inc(S["n_out"], 1)
            for h in range(8):
                dve.wait_ge(S["mean_sum"], h + 1)
                dve.scalar_tensor_tensor(yc[:, h], B[h % 4][:, 0:NT], -1.0 / P, hN[:, h], ALU.mult, ALU.add).then_inc(S["yc_done"], 1)
            for h in range(8):
                dve.wait_ge(S["var_sd"], h + 1)
                ln(dve.reciprocal(ysq[:, h], ysq[:, h]))
                ln(dve.scalar_tensor_tensor(yc[:, h], yc[:, h], gn[:, h:h + 1], ysq[:, h], ALU.mult, ALU.mult))
                if h == 0:
                    dve.wait_ge(S["gates_done"], 8)
                last = dve.tensor_tensor(ymix[:, h], yc[:, h], ymix[:, h], ALU.mult)
            ln(last)


        @block.scalar
        def _(act):
            act.wait_ge(S["gate_x"], 1)
            c.link(act, "act", act.activation(ge, ge, ACT.Exp))
            act.activation(ge, ge, ACT.Ln, bias=c.ones[0:4, 0:1]).then_inc(S["gate_ln"], 1)
            act.wait_ge(S["gate_arg"], 1)
            act.activation(gsc[:, TP:NT], gsc[:, TP:NT], ACT.Exp)
            act.activation(gws, gws, ACT.Exp)
            act.activation(car[:, :], car[:, :], ACT.Exp).then_inc(S["gate_exp"], 1)
            for h in range(4):
                act.wait_ge(S["e_sum"], h + 1)
                act.activation(E[:, h], B[6 + h % 2][:, 0:ST_COLS], ACT.Exp)
                act.activation(Es[:, h], B[6 + h % 2][0:NS, ST_COLS:ST_COLS + NS], ACT.Exp).then_inc(S["e_exp"], 1)
            for h in range(4):
                act.wait_ge(S["y_sum"], h + 1)
                act.activation(hN[:, h], B[h][:, 0:NT], ACT.Copy).then_inc(S["y_out"], 1)
            act.wait_ge(S["rp_sum"], 1)
            act.activation(rsp[:, :, :], B[4][:, 0:256].rearrange("p (h e) -> p h e", h=2), ACT.Copy).then_inc(S["rp_out"], 1)
            act.wait_ge(S["conv_done"], 1)
            for a in range(4):
                act.activation(qk[:, a], cacc[:, a], ACT.Silu).then_inc(S["silu_done"], 1)
            for h in range(4):
                act.activation(ymix[:, h], GC[:, h], ACT.Silu).then_inc(S["gates_done"], 1)
            for h in range(4):
                act.activation(ymix[:, 4 + h], OG[:, h], ACT.Sigmoid).then_inc(S["gates_done"], 1)
            for h in range(4):
                act.wait_ge(S["emj_sum"], h + 1)
                act.activation(emj[:, h], B[h][:, 0:NT], ACT.Exp, scale=-1.0).then_inc(S["emj_out"], 1)
            act.wait_ge(S["car_sum"], 1)
            act.activation(carp[:, :, :], B[5][:, 0:4 * NB].rearrange("p (h b) -> p h b", h=4), ACT.Copy)
            act.activation(carb[:, :], B[5][0:NB, 64:68], ACT.Copy).then_inc(S["car_out"], 1)
            act.wait_ge(S["cp_sum"], 1)
            act.activation(csp[:, :, :], B[6][:, 0:256].rearrange("p (h d) -> p h d", h=4), ACT.Copy).then_inc(S["cp_out"], 1)
            act.wait_ge(S["n_sum"], 1)
            act.wait_ge(S["n_out"], 1)
            act.activation(nsp[:, :], B[7][0:1, 256:512], ACT.Copy).then_inc(S["n_out"], 1)
            for h in range(8):
                act.wait_ge(S["yc_done"], h + 1)
                act.activation(ysq[:, h], yc[:, h], ACT.Square).then_inc(S["yc_sq"], 1)
            for h in range(8):
                act.wait_ge(S["var_sum"], h + 1)
                act.activation(ysq[:, h], B[4 + h % 4][:, 0:NT], ACT.Sqrt, scale=1.0 / P, bias=c.eps[:, 2:3]).then_inc(S["var_sd"], 1)

        @block.tensor
        def _(pe):
            sg_ = dict(skip_group_check=True)
            pe.wait_ge(S["par_loaded"], 16 * 18)
            for i in range(4):
                pe.matmul(B[i][:, 0:NT], rot[:, :], z[:, i], start=True, stop=True).then_inc(S["rot_sum"], 1)
            for h in range(4):
                pe.wait_ge(S["rope_done"], 4)
                hf, hp = half(h % 2), h // 2
                pe.matmul(B[h][:, 0:TP], K[hf, hp, 0:P], Q[hf, hp, 0:TP], start=True, stop=True)
                pe.matmul(B[h][:, TP:ST_COLS], K[hf, hp, P:TP], Q[hf, hp, P:TP], start=True, stop=True)
                pe.matmul(B[h][0:NS, ST_COLS:ST_COLS + NS], K[hf, hp, TP:NT], Q[hf, hp, TP:NT], start=True, stop=True).then_inc(S["s_sum"], 1)
            for i, (t0, n) in enumerate(TOK):
                for hp in range(2):
                    o = (i % 2) * 256 + hp * P
                    mm = pe.transpose(B[4 + i // 2][0:n, o:o + P], K[:, hp, t0:t0 + n], c.ident[:, :])
            mm.then_inc(S["kt_sum"], 1)
            pe.wait_ge(S["gate_arg"], 1)
            for h in range(4):
                if h >= 2:
                    pe.wait_ge(S["e_exp"], h - 1)
                bk = B[6 + h % 2]
                for o, w, s0, j0 in ((0, TP, 0, 0), (TP, P, P, P)):
                    pe.matmul(bk[:, o:o + w], gu[:, s0:s0 + P], sel_row(h)[:, 0:w], start=True, stop=False)
                    pe.matmul(bk[:, o:o + w], sel[:, h], negM[:, j0:j0 + w], start=False, stop=False)
                    pe.matmul(bk[:, o:o + w], c.ident[:, :], lmask[:, 0:w], start=False, stop=True)
                o = ST_COLS
                pe.matmul(bk[0:NS, o:o + NS], gu[:, TP:NT], sel_row(h)[:, 0:NS], start=True, stop=False)
                pe.matmul(bk[0:NS, o:o + NS], sel[:, h, 0:NS], negM[:, TP:NT], start=False, stop=False)
                pe.matmul(bk[0:NS, o:o + NS], c.ident[0:NS, 0:NS], lms[:, :], start=False, stop=True).then_inc(S["e_sum"], 1)
            pe.wait_ge(S["qdec_done"], 1)
            pe.wait_ge(S["rs_loaded"], 16)
            for h in range(4):
                hf, hp = half(h % 2), h // 2
                pe.wait_ge(S["s_out"], h + 1)
                v_ = vc[:, :, h * P:h * P + P]
                pe.matmul(B[h][:, 0:TP], v_[:, 0], scT[:, h, 0:TP], start=True, stop=False, **sg_)
                pe.matmul(B[h][:, P:TP], v_[:, 1], scT[:, h, TP:ST_COLS], start=False, stop=True, **sg_)
                pe.matmul(B[h][:, TP:NT], v_[0:NS, 2], scs[:, h], start=False, stop=False, **sg_)
                for b in range(NB):
                    o = TP + b * TS
                    mm = pe.matmul(B[h][:, o:o + TS], rs0[hf, b, hp], qdec[hf, hp, b * TS:b * TS + TS], start=False, stop=True, **sg_)
                mm.then_inc(S["y_sum"], 1)
            pe.wait_ge(S["kt_out"], 1)
            for h in range(4):
                hf, hp = half(h % 2), h // 2
                for i in range(2):
                    mm = pe.matmul(B[4][hf, hp * P:hp * P + P], kw[:, i, h * 64:h * 64 + 64], vc[:, i, h * P:h * P + P], start=(i == 0), stop=(i == 1))
            mm.then_inc(S["rp_sum"], 1)
            pe.wait_ge(S["e_exp"], 4)
            for hp in range(2):
                pe.wait_ge(S["vb_done"], hp + 1)
                if hp:
                    pe.wait_ge(S["rn_out"], 2)
                for m in range(2):
                    for p_ in range(2):
                        h = 2 * hp + p_
                        mm = pe.matmul(B[6 + m][half(p_), :], kw[0:NS, 2, h * 64:h * 64 + 64],
                                       VB[:, p_, 4 * m:4 * m + 4].rearrange("p b e -> p (b e)"), start=True, stop=True)
                mm.then_inc(S["rn_sum"], 1)
            pe.wait_ge(S["silu_done"], 4)
            pe.wait_ge(S["rp_out"], 1)
            for h in range(4):
                hf, hp = half(h % 2), h // 2
                if h >= 2:
                    pe.wait_ge(S["a_done"], h - 1)
                bk = B[4 + h % 2]
                pe.matmul(bk[:, 0:TP], qk[hf, 2 + hp, 0:P], qk[hf, hp, 0:TP], start=True, stop=True)
                pe.matmul(bk[:, TP:ST_COLS], qk[hf, 2 + hp, P:TP], qk[hf, hp, P:TP], start=True, stop=True)
                pe.matmul(bk[0:NS, ST_COLS:ST_COLS + NS], qk[hf, 2 + hp, TP:NT], qk[hf, hp, TP:NT], start=True, stop=True).then_inc(S["qk_sum"], 1)
            pe.wait_ge(S["rn_out"], 4)
            pe.wait_ge(S["gate_exp"], 1)
            for hp in range(2):
                mm = pe.matmul(B[6][:, hp * NS:hp * NS + NS], selq[:, hp], gsc[:, TP:NT], start=True, stop=True)
            mm.then_inc(S["sq_sum"], 1)
            for i, (t0, n) in enumerate(TOK):
                mm = pe.matmul(B[7][0:n, 4 * i:4 * i + 4], gws[:, t0:t0 + n], c.ident[0:4, 0:4], start=True, stop=True)
            mm.then_inc(S["wt_sum"], 1)
            for h in range(4):
                pe.wait_ge(S["y_out"], h + 1)
                pe.matmul(B[h][:, 0:NT], sel[:, h], gem, start=True, stop=True).then_inc(S["emj_sum"], 1)
            pe.wait_ge(S["a_done"], 4)
            for i, (t0, n) in enumerate(TOK):
                for hp in range(2):
                    o = (i % 2) * 256 + hp * P
                    mm = pe.transpose(B[4 + i // 2][0:n, o:o + P], qk[:, 2 + hp, t0:t0 + n], c.ident[:, :])
            mm.then_inc(S["kd_sum"], 1)
            pe.wait_ge(S["qsc_done"], 1)
            pe.wait_ge(S["c_loaded"], 32)
            pe.wait_ge(S["emj_out"], 4)
            for h in range(4):
                hf, hp = half(h % 2), h // 2
                if h >= 2:
                    pe.wait_ge(S["h_done"], h - 1)
                v_ = vd[:, :, h * P:h * P + P]
                for bn, l0, l1, l2 in ((2 * (h % 2), v_[:, 0], v_[:, 1], v_[0:NS, 2]),
                                       (2 * (h % 2) + 1, c.ones[:, :], c.ones[:, :], c.ones[0:NS, :])):
                    pe.matmul(B[bn][:, 0:TP], l0, scT[:, 4 + h, 0:TP], start=True, stop=False, **sg_)
                    pe.matmul(B[bn][:, P:TP], l1, scT[:, 4 + h, TP:ST_COLS], start=False, stop=True, **sg_)
                    pe.matmul(B[bn][:, TP:NT], l2, scs[:, 4 + h], start=False, stop=False, **sg_)
                for b in range(NB):
                    o = TP + b * TS
                    pe.matmul(B[2 * (h % 2)][:, o:o + TS], c0t[hf, b, hp], qsc[hf, hp, b * TS:b * TS + TS], start=False, stop=True, **sg_)
                pe.matmul(B[2 * (h % 2) + 1][:, TP:NT], c.ones[hf, :], qn[hf, hp], start=False, stop=True, **sg_).then_inc(S["num_sum"], 1)
            pe.wait_ge(S["kd_out"], 1)
            for h in range(4):
                for i in range(2):
                    mm = pe.matmul(B[6][:, h * 64:h * 64 + 64], vd[:, i, h * P:h * P + P], kws[:, i, h * 64:h * 64 + 64], start=(i == 0), stop=(i == 1))
            mm.then_inc(S["cp_sum"], 1)
            pe.matmul(B[7][0:NB, 0:256], bm[:, :], kws[0:NS, 2], start=True, stop=True)
            for i in range(2):
                mm = pe.matmul(B[7][0:1, 256:512], c.ones[:, 0:1], kws[:, i], start=(i == 0), stop=(i == 1))
            mm.then_inc(S["n_sum"], 1)
            for h in range(4):
                mm = pe.matmul(B[5][:, h * NB:h * NB + NB], sel[:, h], car[:, :], start=True, stop=True)
            mm = pe.matmul(B[5][0:NB, 64:68], car[:, :], c.ident[0:4, 0:4], start=True, stop=True)
            mm.then_inc(S["car_sum"], 1)
            for h in range(4):
                pe.wait_ge(S["kb_done"], h + 1)
                if h == 0:
                    pe.wait_ge(S["car_out"], 1)
                if h >= 2:
                    pe.wait_ge(S["cn_out"], h - 1)
                pe.matmul(B[4 + h % 2][:, :], vd[0:NS, 2, h * P:h * P + P], KB[:, h].rearrange("p b d -> p (b d)"), start=True, stop=True).then_inc(S["cn_sum"], 1)
            pe.wait_ge(S["h_done"], 4)
            for h in range(8):
                if h >= 4:
                    pe.wait_ge(S["yc_done"], h - 3)
                pe.matmul(B[h % 4][:, 0:NT], c.ones[:, :], hN[:, h], start=True, stop=True).then_inc(S["mean_sum"], 1)
            pe.wait_ge(S["cp_out"], 1)
            pe.wait_ge(S["n_out"], 2)
            pe.wait_ge(S["cn_out"], 4)
            for h in range(8):
                pe.wait_ge(S["yc_sq"], h + 1)
                if h >= 4:
                    pe.wait_ge(S["var_sd"], h - 3)
                pe.matmul(B[4 + h % 4][:, 0:NT], c.ones[:, :], ysq[:, h], start=True, stop=True).then_inc(S["var_sum"], 1)



def out_stage(c, name, ymix, ymix_lo, gain, next_gain, prefetch):
    nc = c.nc
    out_sum, y_done, y_squared, ysq_added = c.sem(f"out_sum_{name}"), c.y_done, c.y_squared, c.ysq_added
    y0 = KT * c.tails
    ymix_split = c.sem(f"ymix_split_{name}")
    first = c.pairs
    with ExitStack() as ctx:
        whi = c.sb(f"whi_{name}", [P, 2, 2, KT, P], F32R, ctx=ctx)
        y = c.sb(f"y_{name}", [P, 2, NT], ctx=ctx)
        y2 = c.sb(f"y2_{name}", [P, 2, NT], ctx=ctx)
        yg = c.sb(f"yg_{name}", [P, KT, NT], ctx=ctx)
        ysq = c.sb(f"ysq_{name}", [P, NT], ctx=ctx)
        tail = Tail(c, name, yg, ysq[:, :], 1.0, next_gain)
        ctx.enter_context(tail.scope)
        block = ctx.enter_context(nc.Block())

        @block.sync
        def _(sp):
            send_pairs(c, sp, c.ins["w_" + name], 0, 4)
            prefetch(sp)

        @block.tensor
        def _(pe):
            for n in range(KT):
                s, b = (first + n // 2) % RING, (first + n // 2) % 2
                if n % 2 == 0:
                    pe.wait_ge(c.pair_split, first + n // 2 + 1)
                if n >= 2:
                    pe.wait_ge(y_done, y0 + n - 1)
                for k in range(KT):
                    if n == 0:
                        pe.wait_ge(ymix_split, k + 1)
                    mm = three_products(pe, c.banks[4 + n % 2][:, 0:NT], whi[:, b, n % 2, k], c.ring_lo[:, s, n % 2, k], c.xhi[:, k], ymix_lo[:, k],
                                        k == 0, k == KT - 1)
                mm.then_inc(*((c.pair_done, 1) if n % 2 else (out_sum, 1)))
            tail.pe(pe, ysq_added, y0 + KT, c.banks[6])

        @block.scalar
        def _(act):
            for n in range(KT):
                if n % 2:
                    act.wait_ge(c.pair_done, first + n // 2 + 1)
                else:
                    act.wait_ge(out_sum, n // 2 + 1)
                if n >= 2:
                    act.wait_ge(ysq_added, y0 + n - 1)
                c.link(act, "act", act.activation(y[:, n % 2], c.banks[4 + n % 2][:, 0:NT], ACT.Copy))
                act.activation(y2[:, n % 2], y[:, n % 2], ACT.Square).then_inc(y_squared, 1)
                act.activation(yg[:, n], y[:, n % 2], ACT.Copy, scale=c.gains[:, gain, n:n + 1]).then_inc(y_done, 1)
            tail.act(act, c.banks[6])

        @block.vector
        def _(dve):
            split_pair(c, dve, whi, first, 0)
            for k in range(KT):
                c.link(dve, "dve", mask(dve, c.xhi[:, k], ymix[:, k]))
                low_bits(dve, ymix_lo[:, k], ymix[:, k], c.xhi[:, k]).then_inc(ymix_split, 1)
            split_pair(c, dve, whi, first, 1)
            for u in range(2, 4):
                dve.wait_ge(c.pair_done, first + u - 1)
                split_pair(c, dve, whi, first, u)
            dve.wait_ge(y_done, y0 + KT)
            tail.dve(dve)

        @block.gpsimd
        def _(pool):
            pool.wait_ge(y_squared, y0 + 1)
            pool.tensor_copy(ysq[:, :], y2[:, 0]).then_inc(ysq_added, 1)
            for n in range(1, KT):
                pool.wait_ge(ysq_added, y0 + n)
                pool.wait_ge(y_squared, y0 + n + 1)
                pool.tensor_tensor(ysq[:, :], ysq[:, :], y2[:, n % 2], ALU.add).then_inc(ysq_added, 1)
            tail.pool(pool)

    c.pairs += 4


def program(nc, ins, outs, stages="all"):
    with ExitStack() as ctx:
        c = Chip(nc, ctx, ins, outs)

        def ffn_prefetch(f):
            def prefetch(sp):
                send_pairs(c, sp, c.ins["w_gu"][f], 0, RING)
                send_downs(c, sp, c.ins["w_down"][f], 0, 2)
            return prefetch

        def pair_prefetch(name):
            return lambda sp: send_pairs(c, sp, c.ins[name], 0, RING)

        def dump(**t):
            with nc.Block() as block:
                @block.sync
                def _(sp):
                    for n, a in t.items():
                        c.store(sp, outs[n], a)
                    sp.wait_ge(c.stored, 16 * c.stores)
        if stages == "all":
            start_stage(c, 0, ffn_prefetch(0))
            ffn_stage(c, 0, 2, pair_prefetch("w_ab"))
            with ExitStack() as mixer:
                z = c.sb("z", [P, 32, NT], ctx=mixer)
                vtok = c.sb("vtok", [P, 3, 512], ctx=mixer)
                ymix, ymix_lo = c.two_types("ymix", [P, KT, NT], mixer)
                ab_in_stage(c, z, vtok)
                dsa_stage(c, z, vtok, ymix)
                rwkv_stage(c, z, vtok, ymix)
                c.end_stage()
                out_stage(c, "ab_out", ymix, ymix_lo, 3, 4, ffn_prefetch(1))
            ffn_stage(c, 1, 6, ffn_prefetch(2))
            ffn_stage(c, 2, 8, pair_prefetch("w_cd"))
            with ExitStack() as mixer:
                z = c.sb("z2", [P, 18, NT], ctx=mixer)
                vtok = c.sb("vtok2", [P, 6, 512], ctx=mixer)
                ymix, ymix_lo = c.two_types("ymix2", [P, KT, NT], mixer)
                cd_in_stage(c, z, vtok)
                cd_mix_stage(c, z, vtok, ymix)
                out_stage(c, "cd_out", ymix, ymix_lo, 9, 10, ffn_prefetch(3))
            ffn_stage(c, 3, None, lambda sp: None)
            dump(y=c.x[:, :, :])
        if stages == "ffn":
            start_stage(c, 0, ffn_prefetch(0))
            ffn_stage(c, 0, 2, lambda sp: None)
            dump(x=c.x[:, :, :])
        if stages == "rwkv":
            start_stage(c, 2, pair_prefetch("w_ab"))
            z = c.sb("z", [P, 32, NT])
            vtok = c.sb("vtok", [P, 3, 512])
            ymix = c.sb("ymix", [P, KT, NT])
            ab_in_stage(c, z, vtok)
            rwkv_stage(c, z, vtok, ymix)
            dump(ymix=ymix[:, 4:8])
        if stages == "cd":
            c.pairs = c.pairs_sent = 0
            start_stage(c, 8, pair_prefetch("w_cd"))
            z = c.sb("z2", [P, 18, NT])
            vtok = c.sb("vtok2", [P, 6, 512])
            ymix = c.sb("ymix2", [P, KT, NT])
            cd_in_stage(c, z, vtok)
            cd_mix_stage(c, z, vtok, ymix)
            dump(ymix=ymix[:, :])
        if stages == "dsa":
            start_stage(c, 2, pair_prefetch("w_ab"))
            z = c.sb("z", [P, 32, NT])
            vtok = c.sb("vtok", [P, 3, 512])
            ymix = c.sb("ymix", [P, KT, NT])
            ab_in_stage(c, z, vtok)
            dsa_stage(c, z, vtok, ymix)
            dump(ymix=ymix[:, 0:4])


def columns(w):
    n = w.shape[1] // P
    return w.reshape(KT, P, n, P).transpose(2, 1, 0, 3).reshape(n, P, KT * P)


def pairs(blocks):
    n = blocks.shape[0] // 2
    return blocks.reshape(n, 2, P, -1).transpose(0, 2, 1, 3).reshape(n, P, -1)


def feature_major(a):
    return np.ascontiguousarray(a.reshape(a.shape[0], -1, P).transpose(2, 1, 0))


def half_major(a, n):
    return a.reshape(n, P).T


def lay_out_rwkv(m, i):
    b0 = 3 * 512 + 1024 + 64 + 16
    w = i["ab_w_in"][0]
    q, k, v, qi, ki, wi, zb = np.split(w, [512, 1024, 1536, 2560, 2624, 2640], axis=1)
    cols = np.concatenate([q, k, qi, zb, ki, ki, wi, np.zeros((D_MODEL, 112), np.float32)], 1)
    wv = v.reshape(KT, P, 2048 // 4).transpose(1, 0, 2).reshape(P, 2, 2048).transpose(1, 0, 2)
    m["w_ab"] = np.concatenate([pairs(columns(cols)), wv])
    m["rk_par"] = np.ascontiguousarray(np.concatenate([half_major(i["rwkv_mu"][0], 14)] + [
        half_major(i[n][0].reshape(512), HP) for n in ("rwkv_w0", "rwkv_a0", "rwkv_kk", "rwkv_ka", "rwkv_rk", "rwkv_lnx_g", "rwkv_lnx_b")], 1))
    m["wa2"] = np.concatenate([i["rwkv_w2"][0], i["rwkv_a2"][0]])
    m["g2"] = i["rwkv_g2"][0]
    m["shiftT"] = feature_major(i["state_shift"][0])
    s = i["state_rwkv"][0].reshape(NB, HP, 2, L, L)
    m["s0t"] = np.ascontiguousarray(s.transpose(2, 4, 0, 1, 3).reshape(P, NB, HP, L))
    seg = np.ones(NT, np.float32)
    seg[0:TP:L] = 0
    seg[TP::TS] = 0
    m["seg"] = np.tile(seg, (P, 1))
    s_, t = np.arange(L)[:, None], np.arange(L)[None]
    same = (s_ < NS) & (t < NS) & (s_ // TS == t // TS)
    g = [np.concatenate([(s_ < t) & x, (s_ <= t) & x], 1) for x in (np.ones((L, L), bool), same)]
    m["gmask"] = np.tile(np.stack(g, 1), (2, 1, 1)).astype(np.float32)
    m["amask"] = np.tile(np.stack([(t < s_), (t < s_) & same], 1), (2, 1, 1)).astype(np.float32)
    m["bmask"] = np.tile((s_ < NS) & (s_ // TS == np.arange(NB)[None]), (2, 1)).astype(np.float32)
    m["id2"] = np.tile(np.eye(L, dtype=np.float32), (2, 1))


def lay_out_dsa(m, i):
    m["table"] = i["page_table"].reshape(1, NB * NPG)
    kc = i["cache_k"][0].reshape(-1, P, HP, P)
    m["cache_k"] = np.ascontiguousarray(kc.transpose(0, 3, 2, 1).reshape(-1, P, 512))
    m["cache_v"] = i["cache_v"][0].reshape(-1, P, 512)
    m["cache_i"] = np.ascontiguousarray(np.tile(i["cache_kidx"][0].transpose(0, 2, 1), (1, 2, 1)))
    m["kidg"] = np.tile(i["kidx_g"][0].reshape(64, 1), (2, 1))
    t, s = np.arange(TP)[:, None], np.arange(TP)[None]
    m["cmask"] = np.ascontiguousarray(np.where(s <= t, 0, NEG).astype(np.float32).reshape(2, P, TP).transpose(1, 0, 2))
    t, s = np.arange(NS)[:, None], np.arange(NS)[None]
    m["nmask"] = np.where((s <= t) & (s // TS == t // TS), 0, NEG).astype(np.float32)
    row = np.arange(P)
    b2, par, hp, tt = row // 64, row // 32 % 2, row // 4 % 8, row % 4
    m["esel"] = (np.arange(16)[:, None] == 2 * hp + par).astype(np.float32)
    col = np.arange(NS)
    m["wmask"] = np.stack([(col[None] == ((2 * g + b2) * TS + tt)[:, None]) / 32 for g in range(4)], 1).astype(np.float32)
    m["bsel"] = np.stack([(col[:, None] == ((4 * g + row // 32) * TS + row % 4)[None]) for g in range(2)], 1).astype(np.float32)


def lay_out_cd(m, i):
    w = i["cd_w_in"][0]
    qc, kc, vc, gc, qkd, vd, ig, fg, og = np.split(w, np.cumsum([256, 256, 512, 512, 512, 512, 4, 4]), axis=1)
    pad = np.zeros((D_MODEL, P - 4), np.float32)

    def values(v):
        return v.reshape(KT, P, 512).transpose(1, 0, 2).reshape(P, 2, 2048).transpose(1, 0, 2)
    m["w_cd"] = np.concatenate([pairs(columns(np.concatenate([qc, kc, gc, qkd, og], 1))), values(vc), values(vd),
                                pairs(columns(np.concatenate([ig, pad, fg, pad], 1)))])
    m["w_ab_out"] = pairs(columns(i["ab_w_out"][0]))
    m["w_cd_out"] = pairs(columns(i["cd_w_out"][0]))
    gamma = 1.0 - np.exp2(-5.0 - np.arange(4))
    lg = np.log1p(-np.exp2(-5.0 - np.arange(4, dtype=np.float64)))
    par, hrow = np.arange(P) // 64, np.arange(4)
    g4 = np.exp(TS * lg[2 * np.arange(2)[None] + par[:, None]]).astype(np.float32)
    taps = np.concatenate([i["conv_w"][0].reshape(4, 4, P).transpose(2, 1, 0), i["conv_b"][0].reshape(4, P).T[:, :, None]], 2)
    m["cd_par"] = np.ascontiguousarray(np.concatenate([i["ret_gn"][0].T, i["mlstm_gn"][0].T, taps.reshape(P, 20), g4], 1))
    m["ifb"] = np.ascontiguousarray(i["mlstm_if_b"][0].T)
    pos = np.concatenate([np.arange(TP), np.tile(PAST + np.arange(TS), NB)]).astype(np.float32)
    inv = (np.float32(10000.0) ** (-np.arange(32, dtype=np.float32) / np.float32(32))).astype(np.float32)
    ang = (pos[None] * inv[np.arange(P) % 32][:, None]).astype(np.float32).astype(np.float64)
    m["cs"] = np.stack([np.cos(ang), np.sin(ang)], 1).astype(np.float32)
    r = np.zeros((P, P), np.float32)
    for o in range(P):
        r[o + 32 if o % 64 < 32 else o - 32, o] = -1 if o % 64 < 32 else 1
    m["rot"] = r
    s, j = np.arange(P)[:, None, None], np.arange(TP)[None, None]
    m["dmask"] = np.where(j >= s, np.exp(np.maximum(j - s, 0) * lg[None, :, None]) / 8, 0).astype(np.float32)
    s, j = np.arange(NS)[:, None, None], np.arange(NS)[None, None]
    m["dms"] = np.where((j >= s) & (j // TS == s // TS), np.exp(np.maximum(j - s, 0) * lg[None, :, None]) / 8, 0).astype(np.float32)
    m["gq"] = np.exp((np.arange(NS) % TS + 1)[None, None] * lg[2 * np.arange(2)[None] + par[:, None]][:, :, None]).astype(np.float32)
    last = np.concatenate([TP - 1 - np.arange(TP), np.tile(TS - 1 - np.arange(TS), P // TS)]).reshape(3, P).T
    m["wS"] = (np.exp(last[:, :, None] * lg[None, None]) / 8).astype(np.float32)
    s, j = np.arange(P)[:, None], np.arange(TP)[None]
    m["lmask"] = np.where(j >= s, 0, NEG).astype(np.float32)
    s, j = np.arange(NS)[:, None], np.arange(NS)[None]
    m["lms"] = np.where((j >= s) & (j // TS == s // TS), 0, NEG).astype(np.float32)
    m["sel"] = np.tile(np.eye(4, dtype=np.float32)[:, :, None], (1, 1, P))
    m["selq"] = (hrow[:, None, None] == (2 * np.arange(2)[:, None] + par[None])[None]).astype(np.float32)
    seg = np.ones(NT, np.float32)
    seg[0] = 0
    seg[TP::TS] = 0
    m["rows"] = np.tile(np.stack([seg, np.where(seg == 0, NEG, 0).astype(np.float32)]), (4, 1, 1)).astype(np.float32)
    m["m0"] = np.concatenate([np.zeros((4, 1), np.float32), i["state_mlstm_m"][0].T], 1)
    m["bm"] = (np.arange(NS)[:, None] // TS == np.arange(NB)[None]).astype(np.float32)
    m["convT"] = np.ascontiguousarray(i["state_conv"][0].reshape(NB, 3, 4, P).transpose(3, 2, 0, 1))
    m["n0"] = i["state_mlstm_n"][0].reshape(NB, 256)
    m["n0t"] = np.ascontiguousarray(i["state_mlstm_n"][0].reshape(NB, 2, P).transpose(2, 0, 1))
    m["rs0"] = np.ascontiguousarray(i["state_ret"][0].reshape(NB, 2, P, P).transpose(2, 0, 1, 3))
    C = i["state_mlstm_C"][0]
    m["c0"] = np.ascontiguousarray(C.transpose(2, 0, 1, 3))
    m["c0t"] = np.ascontiguousarray(C.reshape(NB, 2, 2, P, 64).transpose(2, 4, 0, 1, 3).reshape(P, NB, 2, P))


def lay_out(i):
    m = {}
    x = np.concatenate([i["x_prompt"].reshape(TP, D_MODEL), i["x_sample"].reshape(NS, D_MODEL)])
    m["x"] = feature_major(x)
    m["gains"] = np.ascontiguousarray(i["norm_g"].reshape(12, KT, P).transpose(2, 0, 1))
    m["ident"] = np.eye(P, dtype=np.float32)
    m["ones"] = np.ones((P, P), np.float32)
    m["half_ones"] = np.kron(np.eye(2, dtype=np.float32), np.ones((64, 64), np.float32))
    m["eps"] = np.tile(np.array([EPS, 4 * EPS, 1e-5, 64e-5], np.float32), (P, 1))
    wg, wu, wd = (i[k].reshape((4,) + i[k].shape[2:]) for k in ("ffn_wg", "ffn_wu", "ffn_wd"))
    m["w_gu"] = np.stack([np.stack([columns(wg[f]), columns(wu[f])], 2).reshape(FT, P, 2 * KT * P) for f in range(4)])
    m["w_down"] = np.stack([wd[f].reshape(FT, P, KT, P).transpose(2, 1, 0, 3).reshape(KT, P, FT * P) for f in range(4)])
    lay_out_rwkv(m, i)
    lay_out_dsa(m, i)
    lay_out_cd(m, i)
    return m


OUT_SHAPES = {"y": (P, KT, NT), "k": (P, 4, NT), "v_p": (P, 2, 512), "v_s": (NS, 512), "kidx": (64, NT), "shift": (P, 14, 1 + NB),
              "rwkv_p": (P, 4, 64), "rwkv_s": (P, NB, 4, 64), "ret_p": (P, 2, P), "ret_s": (P, NB, 2, P), "C_p": (P, 4, 64),
              "C_s": (P, NB, 4, 64), "n_p": (1, 256), "n_s": (NB, 256), "m": (4, 1 + NB), "conv": (P, 4, 3 * (1 + NB))}


def unpack(r):
    def token_major(a):
        return a.transpose(2, 1, 0).reshape(a.shape[2], -1)
    y, k, kidx = token_major(r["y"]), token_major(r["k"]), r["kidx"].T
    shift = token_major(r["shift"])
    v_p = r["v_p"].transpose(1, 0, 2)
    conv = r["conv"].transpose(2, 1, 0).reshape(1 + NB, 3, 512)
    m = r["m"].T
    prompt = (k[:TP].reshape(1, 1, TP, 8, 64), v_p.reshape(1, 1, TP, 8, 64), kidx[:TP].reshape(1, 1, TP, 64),
              r["rwkv_p"].reshape(2, 64, 4, 64).transpose(2, 0, 3, 1).reshape(1, 1, 8, 64, 64), shift[:1][None],
              r["ret_p"].reshape(2, 64, 2, P).transpose(2, 0, 1, 3).reshape(1, 1, 4, 64, P), r["C_p"].transpose(1, 0, 2)[None, None],
              r["n_p"].reshape(1, 1, 4, 64), m[:1][None], conv[:1][None])
    sample = (k[TP:].reshape(1, NB, TS, 8, 64), r["v_s"].reshape(1, NB, TS, 8, 64), kidx[TP:].reshape(1, NB, TS, 64),
              r["rwkv_s"].reshape(2, 64, NB, 4, 64).transpose(2, 3, 0, 4, 1).reshape(1, NB, 8, 64, 64), shift[1:][None],
              r["ret_s"].reshape(2, 64, NB, 2, P).transpose(2, 3, 0, 1, 4).reshape(1, NB, 4, 64, P),
              r["C_s"].transpose(1, 2, 0, 3)[None], r["n_s"].reshape(1, NB, 4, 64), m[1:][None], conv[1:][None])
    out = (y[:TP].reshape(1, TP, D_MODEL), y[TP:].reshape(NB, TS, D_MODEL)) + prompt + sample
    return tuple(np.ascontiguousarray(a) for a in out)


def kernel(**inputs):
    import concourse.bacc as _bacc
    from concourse import mybir as _mybir
    from concourse.bass_utils import run_bass_kernel_spmd as _run

    nc = _bacc.Bacc("TRN2", target_bir_lowering=False, num_devices=1)
    laid = {name: np.ascontiguousarray(a) for name, a in lay_out({k: np.asarray(v) for k, v in inputs.items()}).items()}
    ins = {name: nc.dram_tensor(f"in_{name}", a.shape, _mybir.dt.from_np(a.dtype), kind="ExternalInput").ap()
           for name, a in laid.items()}
    outs = {name: nc.dram_tensor(f"out_{name}", shape, _mybir.dt.float32, kind="ExternalOutput").ap()
            for name, shape in OUT_SHAPES.items()}
    program(nc, ins, outs)
    r = _run(nc, [{f"in_{name}": a for name, a in laid.items()}], core_ids=[0])
    return unpack({name: r.results[0][f"out_{name}"] for name in OUT_SHAPES})
```

```python
from contextlib import ExitStack

import numpy as np

import concourse.bass as bass
from concourse import mybir

F32 = mybir.dt.float32
I32 = mybir.dt.int32
ALU = mybir.AluOpType
ACT = mybir.ActivationFunctionType
AX_X = mybir.AxisListType.X

P = 128
D_MODEL, D_FF = 1024, 2816
KT = D_MODEL // P
FT = D_FF // P
TP = 256
NB, TS = 8, 4
NS = NB * TS
NT = TP + NS
EPS = 1e-6
RING = 4
BANK = 512
DSLOTS, DK = 4, FT // 2
F32R = mybir.dt.float32r


class Chip:

    def __init__(self, nc, ctx, ins, outs):
        self.nc, self.ctx, self.ins, self.outs = nc, ctx, ins, outs
        self.n_pool = ins["cache_i"].shape[0]
        self.pairs = 0
        self.pairs_sent = 0
        self.downs = 0
        self.downs_sent = 0
        self.presplit = 0
        self.stage_sems = []
        self.stores = 0
        sb, sem = self.sb, self.sem
        self.x = sb("x", [P, KT, NT])
        self.xscratch, self.xhi = self.two_types("x_hi", [P, KT, NT])
        self.xscratch2, self.xlo = self.two_types("x_lo", [P, KT, NT])
        self.rstd = sb("rstd", [P, NT])
        self.gains = sb("gains", [P, 12, KT])
        self.ident = sb("ident", [P, P])
        self.ones = sb("ones", [P, P])
        self.half_ones = sb("half_ones", [P, P])
        self.eps = sb("eps", [P, 4])
        self.ring, self.ring_lo = self.two_types("ring", [P, RING, 2, KT, P])
        size = 2 * 2 * KT * P * 4
        self.whi = nc.alloc_sbuf_tensor_at("pair_hi", [P, 2, 2, KT, P], F32R, offset=(nc.sbuf_top - size) // 32 * 32)
        self.below_whi = nc.sbuf_top - size - 32
        self.down, self.down_lo = self.two_types("down", [P, DSLOTS, DK, P])
        self.ring_landed = [sem(f"ring_landed{i}") for i in range(RING)]
        self.down_landed = [sem(f"down_landed{i}") for i in range(DSLOTS)]
        self.pair_masked, self.pair_split = sem("pair_masked"), sem("pair_split")
        self.down_masked, self.down_split = sem("down_masked"), sem("down_split")
        self.xhi_made = sem("xhi_made")
        self.hidden_raw, self.hidden_masked = sem("hidden_raw"), sem("hidden_masked")
        self.pair_done = sem("pair_done")
        self.down_done = sem("down_done")
        self.stored = sem("stored")
        self.tails = 0
        self.post_sum, self.post_sd, self.x_new, self.x_sq, self.pre_sum, self.pre_sd = (
            sem(n) for n in ("post_sum", "post_sd", "x_new", "x_sq", "pre_sum", "pre_sd"))
        self.y_done, self.y_squared, self.ysq_added = (sem(n) for n in ("y_done", "y_squared", "ysq_added"))
        self.gate_scaled, self.up_scaled, self.silu_done, self.hidden_done = (
            sem(n) for n in ("gate_scaled", "up_scaled", "silu_done", "hidden_done"))
        self.chain = {e: sem(f"chain_{e}") for e in ("dve", "act", "pool")}
        self.links = {e: 0 for e in ("dve", "act", "pool")}
        psum = ctx.enter_context(nc.psum_tensor("psum", [P, 8, BANK], F32))
        self.banks = [psum[:, i] for i in range(8)]
        self.two_banks = [psum[:, 2 * b:2 * b + 2] for b in range(2)]

    def sb(self, name, shape, dt=F32, ctx=None):
        return (ctx or self.ctx).enter_context(self.nc.sbuf_tensor(name, shape, dt))

    def two_types(self, name, shape, ctx=None):
        wide = self.sb(name, shape, ctx=ctx)
        size = 4 * int(np.prod(shape[1:]))
        return wide, self.nc.alloc_sbuf_tensor_at(name + "_r", shape, F32R, offset=self.nc.sbuf_base - size)

    def stage_sem(self, name):
        self.stage_sems.append(self.nc.alloc_semaphore(name=name))
        return self.stage_sems[-1]

    def end_stage(self):
        self.nc.clear_and_free_semaphores(self.stage_sems)
        self.nc.all_engine_barrier()
        self.stage_sems = []

    def sem(self, name):
        return self.ctx.enter_context(self.nc.semaphore(name))

    def link(self, engine, which, ins):
        self.links[which] += 1
        ins.then_inc(self.chain[which], 1)
        engine.wait_ge(self.chain[which], self.links[which])

    def store(self, eng, out, src):
        self.stores += 1
        eng.dma_start(out, src).then_inc(self.stored, 16)


def stores_done(c, sp):
    sp.wait_ge(c.stored, 16 * c.stores)


def send_pairs(c, sp, stream, first, n):
    for j in range(first, first + n):
        s = c.pairs_sent % RING
        if c.pairs_sent >= RING:
            sp.wait_ge(c.pair_done, c.pairs_sent - RING + 1)
        sp.dma_start(c.ring[:, s].rearrange("p a k m -> p (a k m)"), stream[j]).then_inc(c.ring_landed[s], 16)
        c.pairs_sent += 1


def send_pair_loop(c, sp, stream, first, rounds):
    sent0 = c.pairs_sent
    with sp.Fori(0, rounds) as i:
        for u in range(RING):
            s = (sent0 + u) % RING
            sp.wait_ge(c.pair_done, i * RING + (sent0 + u - RING + 1))
            sp.dma_start(c.ring[:, s].rearrange("p a k m -> p (a k m)"),
                         stream[bass.ds(i * RING + (first + u), 1)].rearrange("a p n -> (a p) n")
                         ).then_inc(c.ring_landed[s], 16)
    c.pairs_sent += rounds * RING


def send_downs(c, sp, stream, first, n):
    for j in range(first, first + n):
        s = c.downs_sent % DSLOTS
        if c.downs_sent >= DSLOTS:
            sp.wait_ge(c.down_done, c.downs_sent - DSLOTS + 1)
        sp.dma_start(c.down[:, s].rearrange("p k m -> p (k m)"), stream[j]).then_inc(c.down_landed[s], 16)
        c.downs_sent += 1


def mask(dve, hi, a):
    return dve.tensor_copy(hi, a)


def act_mask(act, hi, a):
    return act.activation(hi, a, ACT.Copy)


def low_bits(eng, lo, a, hi):
    return eng.tensor_tensor(lo, a, hi.bitcast(F32), ALU.subtract)


def three_products(pe, out, w_hi, w_lo, x_hi, x_lo, start, stop):
    pe.matmul(out, w_hi, x_hi, start=start, stop=False)
    pe.matmul(out, w_hi, x_lo, start=False, stop=False)
    return pe.matmul(out, w_lo, x_hi, start=False, stop=stop)


def split_pair(c, dve, whi, first, u, i=0):
    s, b = (first + u) % RING, (first + u) % 2
    hi = whi[:, b].rearrange("p a k m -> p (a k m)")
    w, lo = (a[:, s].rearrange("p a k m -> p (a k m)") for a in (c.ring, c.ring_lo))
    dve.wait_ge(c.ring_landed[s], 16 * (i + (first + u) // RING + 1))
    mask(dve, hi, w).then_inc(c.pair_masked, 1)
    dve.wait_ge(c.pair_masked, i * RING + (first + u + 1))
    low_bits(dve, lo, w, hi).then_inc(c.pair_split, 1)


def first_pairs(c, dve, first):
    for u in range(c.presplit, 2):
        split_pair(c, dve, c.whi, first, u)
    c.presplit = 0


def first_pairs_early(c, dve, first, n):
    for u in range(n):
        split_pair(c, dve, c.whi, first, u)
    c.presplit = n


def x_high(c, act, gain, n):
    act.activation(c.xhi[:, n], c.x[:, n], ACT.Copy, scale=c.gains[:, gain, n:n + 1]).then_inc(c.xhi_made, 1)


def x_low(c, eng, gain, n, nth):
    eng.wait_ge(c.xhi_made, KT * nth + n + 1)
    eng.scalar_tensor_tensor(c.xlo[:, n], c.x[:, n], c.gains[:, gain, n:n + 1], c.xhi[:, n].bitcast(F32), ALU.mult, ALU.subtract)


def sum_of_squares(c, pe, bank, sq, sem, count, step):
    for n in range(KT):
        if n % step == 0:
            pe.wait_ge(sem, count + n // step + 1)
        mm = pe.matmul(bank[:, 0:NT], c.ones[:, :], sq[:, n], start=(n == 0), stop=(n == KT - 1))
    return mm


class Tail:

    def __init__(self, c, name, yg, ysq, y2_last, factor, next_gain, scratch=None):
        self.c, self.yg, self.ysq, self.y2_last, self.factor, self.next_gain = c, yg, ysq, y2_last, factor, next_gain
        ctx = self.scope = ExitStack()
        self.sd = c.sb(f"sd_{name}", [P, NT], ctx=ctx)
        self.rpost = c.sb(f"rpost_{name}", [P, NT], ctx=ctx)
        self.t, self.sq = scratch or [c.sb(f"{n}_{name}", [P, KT, NT], ctx=ctx) for n in ("t", "sq")]
        self.sd2 = c.sb(f"sd2_{name}", [P, NT], ctx=ctx)
        self.done = c.tails
        c.tails += 1

    def pe(self, pe, ysq_added, y_squared, base, bank):
        c = self.c
        pe.wait_ge(ysq_added, (KT - 1) * (self.done + 1))
        pe.matmul(bank[:, 0:NT], c.ones[:, :], self.ysq, start=True, stop=False)
        pe.wait_ge(y_squared, base + KT)
        pe.matmul(bank[:, 0:NT], c.ones[:, :], self.y2_last, start=False, stop=True).then_inc(c.post_sum, 1)
        if self.next_gain is not None:
            sum_of_squares(c, pe, bank, self.sq, c.x_sq, KT // 2 * self.done, 2).then_inc(c.pre_sum, 1)

    def warm(self, act):
        act.activation(self.sd2[:, 0:1], self.c.eps[:, 0:1], ACT.Sqrt)

    def act(self, act, bank):
        c = self.c
        f2 = 1.0 / (self.factor * self.factor)
        act.wait_ge(c.post_sum, self.done + 1)
        act.activation(self.sd[:, :], bank[:, 0:NT], ACT.Sqrt, scale=f2 / D_MODEL,
                       bias=c.eps[:, 0:1] if f2 == 1 else c.eps[:, 1:2]).then_inc(c.post_sd, 1)
        if self.next_gain is None:
            return
        for g in range(KT // 2):
            two = slice(2 * g, 2 * g + 2)
            act.wait_ge(c.x_new, KT // 2 * self.done + g + 1)
            if g == KT // 2 - 1:
                act.activation(self.sq[:, two], c.x[:, two], ACT.Square).then_inc(c.x_sq, 1)
            for n in (2 * g, 2 * g + 1):
                x_high(c, act, self.next_gain, n)
            if g < KT // 2 - 1:
                act.activation(self.sq[:, two], c.x[:, two], ACT.Square).then_inc(c.x_sq, 1)
        act.wait_ge(c.pre_sum, self.done + 1)
        act.activation(self.sd2[:, :], bank[:, 0:NT], ACT.Sqrt, scale=1.0 / D_MODEL,
                       bias=c.eps[:, 0:1]).then_inc(c.pre_sd, 1)

    def dve(self, dve):
        c = self.c
        dve.wait_ge(c.post_sd, self.done + 1)
        c.link(dve, "dve", dve.reciprocal(self.rpost[:, :], self.sd[:, :]))
        r = self.rpost[:, :].rearrange("p (a t) -> p a t", a=1).to_broadcast([P, 2, NT])

        def low(n):
            if self.next_gain is not None and n >= 0:
                x_low(c, dve, self.next_gain, n, self.done + 1)

        for g in range(KT // 2):
            two = slice(2 * g, 2 * g + 2)
            c.links["dve"] += 1
            dve.tensor_tensor(self.t[:, two], self.yg[:, two], r, ALU.mult).then_inc(c.chain["dve"], 1)
            low(2 * g - 2)
            dve.wait_ge(c.chain["dve"], c.links["dve"])
            dve.tensor_tensor(c.x[:, two], c.x[:, two], self.t[:, two], ALU.add).then_inc(c.x_new, 1)
        low(KT - 2)
        if self.next_gain is not None:
            dve.wait_ge(c.pre_sd, self.done + 1)
            dve.reciprocal(c.rstd[:, :], self.sd2[:, :])


    def pool(self, pool):
        c = self.c
        if self.next_gain is not None:
            for n in range(1, KT, 2):
                pool.wait_ge(c.xhi_made, KT * (self.done + 1) + n + 1)
                c.link(pool, "pool", pool.tensor_scalar(self.t[:, n], c.x[:, n], c.gains[:, self.next_gain, n:n + 1], None, ALU.mult))
                low_bits(pool, c.xlo[:, n], self.t[:, n], c.xhi[:, n])


def start_stage(c, gain, prefetch):
    nc = c.nc
    loaded, x_loaded, sq_done, summed, sd_done = (c.sem(n) for n in ("const_loaded", "x_loaded", "x0_sq", "x0_sum", "x0_sd"))
    with ExitStack() as ctx, nc.Block() as block:
        sq = c.sb("sq0", [P, KT, NT], ctx=ctx)
        sd = c.sb("sd0", [P, NT], ctx=ctx)

        @block.sync
        def _(sp):
            sp.dma_start(c.x[:, :, :], c.ins["x"]).then_inc(x_loaded, 16)
            for t, n in ((c.gains, "gains"), (c.ident, "ident"), (c.ones, "ones"), (c.half_ones, "half_ones"),
                         (c.eps, "eps")):
                sp.dma_start(t[:], c.ins[n]).then_inc(loaded, 16)
            prefetch(sp)

        @block.scalar
        def _(act):
            act.wait_ge(x_loaded, 16)
            for n in range(KT):
                act.activation(sq[:, n], c.x[:, n], ACT.Square).then_inc(sq_done, 1)
            act.wait_ge(loaded, 80)
            for n in range(KT):
                x_high(c, act, gain, n)
            act.wait_ge(summed, 1)
            act.activation(sd[:, :], c.banks[7][:, 0:NT], ACT.Sqrt, scale=1.0 / D_MODEL,
                           bias=c.eps[:, 0:1]).then_inc(sd_done, 1)

        @block.tensor
        def _(pe):
            pe.wait_ge(loaded, 80)
            sum_of_squares(c, pe, c.banks[7], sq, sq_done, 0, 1).then_inc(summed, 1)

        @block.vector
        def _(dve):
            dve.wait_ge(loaded, 80)
            for n in range(KT):
                x_low(c, dve, gain, n, 0)
            first_pairs_early(c, dve, c.pairs, 1)
            dve.wait_ge(sd_done, 1)
            dve.reciprocal(c.rstd[:, :], sd[:, :])


def tile(a, n):
    return a[:, n] if isinstance(n, int) else a[:, bass.ds(n, 1)].rearrange("p a t -> p (a t)")


def ffn_stage(c, f, next_gain, prefetch):
    nc = c.nc
    gain = 6 * (f // 2) + (1 if f % 2 == 0 else 5)
    gu, dn = c.ins["w_gu"][f], c.ins["w_down"][f]
    gate_scaled, up_scaled, silu_done, hidden_done = c.gate_scaled, c.up_scaled, c.silu_done, c.hidden_done
    y_done, y_squared, ysq_added = c.y_done, c.y_squared, c.ysq_added
    pairs0, y0, y1 = FT * f, KT * c.tails, (KT - 1) * c.tails
    first, first_down = c.pairs, c.downs
    rounds, rest = (FT - RING) // RING, (FT - RING) % RING
    loops = (FT - 2) // RING
    assert (FT - 2) % RING == 0
    with ExitStack() as ctx:
        def sb(n, shape, dt=F32):
            return c.sb(f"{n}{f}", shape, dt, ctx=ctx)
        hfree, hhi = c.two_types(f"hidden_hi{f}", [P, FT, NT], ctx)
        hidden, hlo = c.two_types(f"hidden{f}", [P, FT, NT], ctx)
        whi, dhi = c.whi, sb("down_hi", [P, 2, DK, P], F32R)
        gate, silu, up = sb("gate", [P, 2, NT]), sb("silu", [P, 2, NT]), sb("up", [P, 2, NT])
        y2 = sb("y2", [P, 2, NT])
        yg = sb("yg", [P, KT, NT])
        ysq = sb("ysq", [P, NT])
        tail = Tail(c, f"ffn{f}", yg, ysq[:, :], y2[:, (KT - 1) % 2], 0.5, next_gain, (hfree[:, 0:KT], hidden[:, 0:KT]))
        ctx.enter_context(tail.scope)
        assert nc.sbuf_base <= c.below_whi
        block = ctx.enter_context(nc.Block())

        @block.sync
        def _(sp):
            send_pair_loop(c, sp, gu, RING, rounds)
            send_pairs(c, sp, gu, RING + rounds * RING, rest)
            send_downs(c, sp, dn, DSLOTS, 2 * KT - DSLOTS)
            prefetch(sp)
            if next_gain is None:
                for g in range(KT // 2):
                    sp.wait_ge(c.x_new, KT // 2 * tail.done + g + 1)
                    c.store(sp, c.outs["y"][:, 2 * g:2 * g + 2], c.x[:, 2 * g:2 * g + 2])
                stores_done(c, sp)

        @block.tensor
        def _(pe):
            def up_pair(u, i=0):
                s, b = (first + u) % RING, (first + u) % 2
                pe.wait_ge(c.pair_split, i * RING + (first + u + 1))
                if u >= 2 or not isinstance(i, int):
                    pe.wait_ge(up_scaled, i * RING + (pairs0 + u - 1))
                for half in range(2):
                    for k in range(KT):
                        mm = three_products(pe, c.banks[2 * (u % 2) + half][:, 0:NT], whi[:, b, half, k], c.ring_lo[:, s, half, k],
                                            c.xhi[:, k], c.xlo[:, k], k == 0, k == KT - 1)
                mm.then_inc(c.pair_done, 1)
            for u in range(RING):
                up_pair(u)
            with pe.Fori(1, FT // RING) as i:
                for u in range(RING):
                    up_pair(u, i)
            for u in range(FT - FT % RING, FT):
                up_pair(u)
            pe.wait_ge(hidden_done, pairs0 + FT - 2)
            for n in range(KT):
                if n >= 2:
                    pe.wait_ge(y_done, y0 + n - 1)
                for h in range(2):
                    j = first_down + 2 * n + h
                    s = j % DSLOTS
                    pe.wait_ge(c.down_split, j + 1)
                    for i in range(DK):
                        k = h * DK + i
                        if n == 0 and k == FT - 2:
                            pe.wait_ge(hidden_done, pairs0 + FT)
                        mm = three_products(pe, c.banks[4 + n % 2][:, 0:NT], dhi[:, j % 2, i], c.down_lo[:, s, i], hhi[:, k], hlo[:, k],
                                            k == 0, k == FT - 1)
                    mm.then_inc(c.down_done, 1)
            tail.pe(pe, ysq_added, y_squared, y0, c.banks[6])

        @block.scalar
        def _(act):
            with act.Fori(0, FT // 2) as i:
                for b in range(2):
                    act.wait_ge(gate_scaled, i * 2 + (pairs0 + b + 1))
                    act.activation(silu[:, b], gate[:, b], ACT.Silu).then_inc(silu_done, 1)
            tail.warm(act)
            for n in range(KT):
                act.wait_ge(c.down_done, first_down + 2 * n + 2)
                if n >= 2:
                    act.wait_ge(ysq_added, y1 + n - 1)
                act.activation(y2[:, n % 2], c.banks[4 + n % 2][:, 0:NT], ACT.Square).then_inc(y_squared, 1)
                act.activation(yg[:, n], c.banks[4 + n % 2][:, 0:NT], ACT.Copy, scale=c.gains[:, gain, n:n + 1]).then_inc(y_done, 1)
            tail.act(act, c.banks[6])

        @block.vector
        def _(dve):
            def scale(u, i=0):
                b = u % 2
                dve.wait_ge(c.pair_done, i * RING + (first + u + 1))
                dve.tensor_tensor(gate[:, b], c.banks[2 * b][:, 0:NT], c.rstd[:, :], ALU.mult).then_inc(gate_scaled, 1)
                dve.tensor_tensor(up[:, b], c.banks[2 * b + 1][:, 0:NT], c.rstd[:, :], ALU.mult).then_inc(up_scaled, 1)

            def mask_hidden(u, i=0):
                dve.wait_ge(c.hidden_raw, i * RING + (pairs0 + u + 1))
                mask(dve, tile(hhi, i * RING + u), tile(hidden, i * RING + u)).then_inc(c.hidden_masked, 1)

            def split_down(i):
                j = first_down + i
                s = j % DSLOTS
                hi, w, lo = (a.rearrange("p k m -> p (k m)") for a in (dhi[:, j % 2], c.down[:, s], c.down_lo[:, s]))
                dve.wait_ge(c.down_landed[s], 16 * (j // DSLOTS + 1))
                if i >= 2:
                    dve.wait_ge(c.down_done, j - 1)
                mask(dve, hi, w).then_inc(c.down_masked, 1)
                dve.wait_ge(c.down_masked, j + 1)
                low_bits(dve, lo, w, hi).then_inc(c.down_split, 1)

            first_pairs(c, dve, first)
            with dve.Fori(0, loops) as i:
                for u in range(RING):
                    scale(u, i)
                    split_pair(c, dve, whi, first, u + 2, i)
                    mask_hidden(u, i)
            for j in range(2):
                scale(FT - 2 + j)
                mask_hidden(FT - 2 + j)
                split_down(j)
            for n in range(2, 2 * KT):
                split_down(n)
            if next_gain is not None:
                first_pairs_early(c, dve, first + FT, 2)
            dve.wait_ge(y_done, y0 + KT)
            tail.dve(dve)

        @block.gpsimd
        def _(pool):
            with pool.Fori(0, FT // 2) as i:
                for b in range(2):
                    n = i * 2 + (pairs0 + b + 1)
                    h = tile(hidden, i * 2 + b)
                    pool.wait_ge(up_scaled, n)
                    pool.wait_ge(silu_done, n)
                    pool.tensor_tensor(h, silu[:, b], up[:, b], ALU.mult).then_inc(c.hidden_raw, 1)
                    pool.wait_ge(c.hidden_masked, n)
                    low_bits(pool, tile(hlo, i * 2 + b), h, tile(hhi, i * 2 + b)).then_inc(hidden_done, 1)
            pool.wait_ge(y_squared, y0 + 1)
            pool.tensor_copy(ysq[:, :], y2[:, 0]).then_inc(ysq_added, 1)
            for n in range(1, KT - 1):
                pool.wait_ge(ysq_added, y1 + n)
                pool.wait_ge(y_squared, y0 + n + 1)
                pool.tensor_tensor(ysq[:, :], ysq[:, :], y2[:, n % 2], ALU.add).then_inc(ysq_added, 1)
            tail.pool(pool)

    c.pairs += FT
    c.downs += 2 * KT



def project_pe(c, pe, whi, z_done, npairs):
    first = c.pairs

    def one(u, i=0):
        s, b = (first + u) % RING, (first + u) % 2
        pe.wait_ge(c.pair_split, i * RING + (first + u + 1))
        if u >= 2 or not isinstance(i, int):
            pe.wait_ge(z_done, i * RING + (u - 1))
        for half in range(2):
            for k in range(KT):
                mm = three_products(pe, c.banks[2 * (u % 2) + half][:, 0:NT], whi[:, b, half, k], c.ring_lo[:, s, half, k],
                                    c.xhi[:, k], c.xlo[:, k], k == 0, k == KT - 1)
        mm.then_inc(c.pair_done, 1)

    for u in range(RING):
        one(u)
    with pe.Fori(1, npairs // RING) as i:
        for u in range(RING):
            one(u, i)


def project_dve(c, dve, whi, z, z_done, npairs, first):
    first_pairs(c, dve, first)
    with dve.Fori(0, npairs // RING) as i:
        for u in range(RING):
            dve.wait_ge(c.pair_done, i * RING + (first + u + 1))
            dve.tensor_tensor(z[:, bass.ds(i * (2 * RING) + 2 * u, 2)], c.two_banks[u % 2][:, :, 0:NT],
                              c.rstd[:, :].rearrange("p (a t) -> p a t", a=1).to_broadcast([P, 2, NT]),
                              ALU.mult).then_inc(z_done, 1)
            split_pair(c, dve, whi, first, u + 2, i)


def project_values(c, pe, whi, pair, tile_done):
    s, b = pair % RING, pair % 2
    assert b == 0
    hi, lo = (a.rearrange("p s a k m -> p (s a k m)").rearrange("p (k n) -> p k n", k=KT) for a in (whi[:, 0:2], c.ring_lo[:, s:s + 2]))
    pe.wait_ge(c.pair_split, pair + 2)
    for i, (t0, n) in enumerate(TOK):
        for k in range(KT):
            cols = slice(t0, t0 + n)
            mm = three_products(pe, c.banks[4 + i][0:n, :], c.xhi[:, k, cols], c.xlo[:, k, cols], hi[:, k], lo[:, k], k == 0, k == KT - 1)
        tile_done(i, mm)


TOK = ((0, P), (P, P), (TP, NS))


def token_rstd_pe(c, pe, rt_sum):
    for i, (t0, n) in enumerate(TOK):
        mm = pe.matmul(c.banks[7][0:n, i:i + 1], c.rstd[0:1, t0:t0 + n], c.ones[0:1, 0:1], start=True, stop=True)
    mm.then_inc(rt_sum, 1)


def ab_in_stage(c, z, vtok, idx):
    nc, npairs = c.nc, 16
    stream = c.ins["w_ab"]
    z_done, v_sum, rt_sum, rt_ready, v_done = (
        c.sem(n + "_ab") for n in ("z_done", "v_sum", "rt_sum", "rt_ready", "v_done"))
    first = c.pairs
    with ExitStack() as ctx:
        rt = c.sb("rt_ab", [P, 3], ctx=ctx)
        whi = c.whi
        block = ctx.enter_context(nc.Block())

        @block.sync
        def _(sp):
            send_pair_loop(c, sp, stream, RING, 3)
            send_pairs(c, sp, stream, 16, 2)
            sp.wait_ge(v_done, 3)
            c.store(sp, c.outs["v_p"], vtok[:, 0:2])
            c.store(sp, c.outs["v_s"], vtok[0:NS, 2])
            sp.wait_ge(z_done, npairs)
            c.store(sp, c.outs["k"], z[:, 4:8])

        @block.tensor
        def _(pe):
            project_pe(c, pe, whi, z_done, npairs)
            token_rstd_pe(c, pe, rt_sum)
            project_values(c, pe, whi, first + 16, lambda i, mm: mm.then_inc(*((v_sum, 1) if i < 2 else (c.pair_done, 2))))

        @block.scalar
        def _(act):
            act.dma_start(idx.table[:, :], c.ins["table"]).then_inc(idx.table_loaded, 16)
            act.wait_ge(idx.table_loaded, 16)
            with act.Fori(0, NB) as b:
                for j in range(NPG):
                    page = act.value_load(idx.table[0:1, bass.ds(b * NPG + j, 1)], min_val=0, max_val=c.n_pool - 1)
                    act.dma_start(idx.keys[:, bass.ds(b, 1), j * P:(j + 1) * P].rearrange("p a n -> p (a n)"),
                                  c.ins["cache_i"][bass.ds(page, 1)].rearrange("a p n -> (a p) n")).then_inc(idx.landed, 16)
            act.wait_ge(rt_sum, 1)
            for i, (t0, n) in enumerate(TOK):
                act.activation(rt[0:n, i:i + 1], c.banks[7][0:n, i:i + 1], ACT.Copy).then_inc(rt_ready, 1)
            for i, (t0, n) in enumerate(TOK):
                act.wait_ge(rt_ready, i + 1)
                if i < 2:
                    act.wait_ge(v_sum, i + 1)
                else:
                    act.wait_ge(c.pair_done, first + npairs + 2)
                act.activation(vtok[0:n, i], c.banks[4 + i][0:n, :], ACT.Copy, scale=rt[0:n, i:i + 1]).then_inc(v_done, 1)

        @block.vector
        def _(dve):
            project_dve(c, dve, whi, z, z_done, npairs, first)

    c.pairs += npairs + 2


CH = 5
L = 64
NP_ = CH * L
HP = 4
Z_R, Z_K, Z_V, Z_WA, Z_G = 16, 20, 24, 28, 29
EXP_HALF = float(np.exp(-0.5))


def rwkv_stage(c, z, vtok, ymix):
    nc = c.nc
    S = {}
    for n in ("mix_loaded", "par_loaded", "state_loaded", "shift_ready", "mixed", "lora_in", "lora_sum", "lora_out", "ld_done", "cum_done", "w_done",
              "kk_sq", "kk_sum", "kk_max", "kk_sd", "kk_rows", "kk_all", "ar_done", "bk_done", "prod_done", "bonus_sum", "sv_done",
              "act_grp", "act_out", "dve_grp", "dve_out", "pw_sum", "pw_out", "pwt_sum", "pwt_out", "x_sum", "x_out",
              "rhs_sum", "rhs_out", "sa_sum", "sa_out", "y_sum", "y_out", "st_sum", "st_out",
              "i0_sum", "i0_out", "ub_done", "ss_sum", "ss_out", "mean_sum", "yc_done", "yc_sq", "var_sum", "var_sd", "var_rows", "var_all", "yn_done", "zeroed"):
        S[n] = c.stage_sem(n + "_rk")
    with ExitStack() as ctx:
        def sb(n, shape):
            return c.sb(n + "_rk", shape, ctx=ctx)
        par = sb("par", [P, 14 + 8 * HP])
        mu = par[:, 0:14]
        w0, a0, kkw, ka, rk, lng, lnb, omka = (par[:, 14 + 4 * j:18 + 4 * j] for j in range(8))
        wa2, g2 = sb("wa2", [P, 512]), sb("g2", [P, 512])
        shiftT = sb("shiftT", [P, 14, NB])
        zlast = sb("zlast", [P, 14, 1 + NB])
        s0t = sb("s0t", [P, NB, HP, L])
        seg = sb("seg", [P, NT])
        gmask = sb("gmask", [P, 2, P])
        amask = sb("amask", [P, 2, L])
        bmask = sb("bmask", [P, NB])
        id2 = sb("id2", [P, L])
        pair_cols, pair_rows = sb("pair_cols", [P, HP, 8]), sb("pair_rows", [8, HP, P])
        D = sb("D", [P, 14, NT])
        lw = sb("lw", [P, 2, NT])
        e1, e2, e3 = D[:, 0:4], D[:, 4:8], D[:, 8:12]
        f1, f2, f3 = (sb(n, [P, HP, NT]) for n in ("f1", "f2", "f3"))
        U = sb("U", [P, CH, 2, HP, L])
        spare = c.ring[:, :].rearrange("p s a k m -> p (s a k m)")
        AR = spare[:, 0:2 * HP * NP_].rearrange("p (a h n) -> p a h n", a=2, h=HP)
        BK = spare[:, 2 * HP * NP_:4 * HP * NP_].rearrange("p (h c a l) -> p h c a l", h=HP, c=CH, a=2)
        BKt = spare[:, 4 * HP * NP_:4 * HP * NP_ + CH * HP * P].rearrange("p (c h n) -> p c h n", c=CH, h=HP)
        G = c.down[:, :].rearrange("p s k m -> p (s k m)")[:, 0:CH * 2 * HP * P].rearrange("p (c q h n) -> p c q h n", c=CH, q=2, h=HP)
        av, Gt = c.xscratch2[:, 0:HP], c.xscratch2[:, HP:2 * HP]
        spare = z[:, 0:16].rearrange("p a t -> p (a t)")
        PW = [spare[:, o:o + CH * HP * L].rearrange("p (m l) -> p m l", l=L) for o in (0, CH * HP * L)]
        PWT = [spare[:, 2 * CH * HP * L:3 * CH * HP * L].rearrange("p (m l) -> p m l", l=L),
               vtok[:, :].rearrange("p a n -> p (a n)")[:, 0:CH * HP * L].rearrange("p (m l) -> p m l", l=L)]
        xflat = c.xscratch[:, :].rearrange("p k t -> p (k t)")
        X = xflat[:, 0:CH * HP * L].rearrange("p (n l) -> p n l", l=L)
        AKV = sb("AKV", [P, CH, HP, L])
        RHS, STt = (xflat[:, o:o + HP * L].rearrange("p (h l) -> p h l", h=HP) for o in (CH * HP * L, (CH + 1) * HP * L))
        ST = sb("ST", [P, 2, HP, L])
        rows8 = xflat[0:8, (CH + 1) * HP * L:(CH + 1) * HP * L + NT]
        I0 = xflat[:, (CH + 2) * HP * L:(CH + 3) * HP * L].rearrange("p (h a n) -> p h a n", h=HP, a=2)
        block = ctx.enter_context(nc.Block())
        B = c.banks
        r, k, v = z[:, Z_R:Z_R + 4], z[:, Z_K:Z_K + 4], z[:, Z_V:Z_V + 4]
        yT = f3
        UBs = [z[:, o:o + 4].rearrange("p a t -> p (a t)")[:, 0:2 * NB * L].rearrange("p (u b l) -> p u b l", u=2, b=NB)
               for o in (0, 4)]

        def half(q):
            return slice(q * 64, q * 64 + 64)

        def bc(ap, shape):
            return ap.to_broadcast(shape)

        @block.sync
        def _(sp):
            for dst, src in ((par[:, 0:14 + 7 * HP], "rk_par"), (shiftT[:, :, :], "shiftT")):
                sp.dma_start(dst, c.ins[src]).then_inc(S["mix_loaded"], 16)
            for dst, src in ((wa2[:, :], "wa2"), (g2[:, :], "g2"), (seg[:, :], "seg"), (gmask[:, :, :], "gmask"), (amask[:, :, :], "amask"), (bmask[:, :], "bmask"),
                             (id2[:, :], "id2"), (pair_cols[:, :, :], "pair_cols"), (pair_rows[:, :, :], "pair_rows")):
                sp.dma_start(dst, c.ins[src]).then_inc(S["par_loaded"], 16)
            sp.dma_start(s0t[:, :, :, :], c.ins["s0t"]).then_inc(S["state_loaded"], 16)
            sp.wait_ge(S["shift_ready"], 1)
            c.store(sp, c.outs["shift"], zlast[:, :, :])
            sp.wait_ge(S["st_out"], 4)
            c.store(sp, c.outs["rwkv_p"], ST[:, 1])
            sp.wait_ge(S["ss_out"], HP)
            c.store(sp, c.outs["rwkv_s"], s0t[:, :, :, :])
            stores_done(c, sp)

        @block.gpsimd
        def _(pool):
            pool.memset(AR[:, :, :, NT:NP_], 0.0).then_inc(S["zeroed"], 1)
            pool.memset(BK[:, :, 4, :, NS:L], 0.0).then_inc(S["zeroed"], 1)
            pool.memset(U[:, :, :, :, :], 0.0).then_inc(S["zeroed"], 1)

        @block.vector
        def _(dve):
            def ln(ins):
                c.link(dve, "dve", ins)
            dve.wait_ge(S["mix_loaded"], 32)
            zz = z[:, 16:30]
            dve.tensor_copy(zlast[:, :, 0:1], zz[:, :, TP - 1:TP])
            ln(dve.tensor_copy(zlast[:, :, 1:1 + NB], zz[:, :, TP + TS - 1:NT:TS]))
            dve.tensor_scalar(omka, ka, -1.0, 1.0, ALU.mult, ALU.add)
            dve.tensor_tensor(D[:, :, 1:TP], zz[:, :, 0:TP - 1], zz[:, :, 1:TP], ALU.subtract).then_inc(S["shift_ready"], 1)
            dve.tensor_scalar(D[:, :, 0:1], zz[:, :, 0:1], -1.0, None, ALU.mult)
            Ds = D[:, :, TP:NT].rearrange("p a (b t) -> p a b t", t=TS)
            zs = zz[:, :, TP:NT].rearrange("p a (b t) -> p a b t", t=TS)
            dve.tensor_tensor(Ds[:, :, :, 1:TS], zs[:, :, :, 0:TS - 1], zs[:, :, :, 1:TS], ALU.subtract)
            ln(dve.tensor_tensor(Ds[:, :, :, 0], shiftT[:, :, :], zs[:, :, :, 0], ALU.subtract))
            for j in [12, 13, 4, 5, 6, 7, 0, 1, 2, 3, 8, 9, 10, 11]:
                ins = dve.scalar_tensor_tensor(zz[:, j], D[:, j], mu[:, j:j + 1], zz[:, j], ALU.mult, ALU.add).then_inc(S["mixed"], 1)
            dve.wait_ge(S["mixed"], 14)
            dve.wait_ge(S["par_loaded"], 16 * 9)
            for h in range(HP):
                dve.tensor_scalar(f1[:, h], k[:, h], kkw[:, h:h + 1], None, ALU.mult).then_inc(S["kk_sq"], 1)
            dve.wait_ge(S["kk_sum"], 1)
            dve.tensor_scalar(rows8, B[4][0:8, 0:NT], 1e-24, None, ALU.max).then_inc(S["kk_max"], 1)
            dve.wait_ge(S["lora_out"], HP)
            ln(dve.tensor_scalar(e1, e1, -EXP_HALF, None, ALU.mult))
            for h in range(HP):
                last = dve.tensor_tensor_scan(e2[:, h], seg[:, :], e1[:, h], 0.0, ALU.mult, ALU.add)
            ln(last)
            dve.tensor_tensor(e3, e2, e1, ALU.subtract).then_inc(S["cum_done"], 1)
            dve.wait_ge(S["kk_sd"], 1)
            dve.reciprocal(rows8, rows8).then_inc(S["kk_rows"], 1)
            for h in range(HP):
                dve.wait_ge(S["kk_all"], h + 1)
                last = dve.tensor_tensor(f1[:, h], f1[:, h], B[4 + h][:, 0:NT], ALU.mult)
            ln(last)
            dve.wait_ge(S["lora_out"], 2 * HP)
            dve.tensor_tensor(f2[:, :, :], f1[:, :, :], av[:, :, :], ALU.mult)
            for h in range(HP):
                last = dve.tensor_scalar(f3[:, h], av[:, h], ka[:, h:h + 1], omka[:, h:h + 1], ALU.mult, ALU.add)
            ln(last)
            ln(dve.tensor_tensor(k, k, f3[:, :, :], ALU.mult))
            dve.wait_ge(S["w_done"], 3)
            dve.wait_ge(S["zeroed"], 3)
            dve.scalar_tensor_tensor(AR[:, 0, :, 0:NT], f1[:, :, :], -1.0, e3, ALU.mult, ALU.mult)
            dve.tensor_tensor(AR[:, 1, :, 0:NT], r, e1, ALU.mult).then_inc(S["ar_done"], 1)
            for q in range(2):
                for slot, a in ((q, f2), (1 - q, k)):
                    for c0, c1, n in ((0, 4, L), (4, 5, NS)):
                        cols = slice(c0 * L, c0 * L + (c1 - c0) * n)
                        last = dve.tensor_tensor(BK[half(q), :, c0:c1, slot, 0:n],
                                                 a[half(q), :, cols].rearrange("p h (c l) -> p h c l", l=n),
                                                 e2[half(q), :, cols].rearrange("p h (c l) -> p h c l", l=n), ALU.mult)
            last.then_inc(S["bk_done"], 1)
            dve.wait_ge(S["bk_done"], 1)
            for h in range(HP):
                dve.scalar_tensor_tensor(e2[:, h], r[:, h], rk[:, h:h + 1], k[:, h], ALU.mult, ALU.mult).then_inc(S["prod_done"], 1)
            for c_ in range(CH):
                var = 0 if c_ < 4 else 1
                for q in range(2):
                    g = 2 * c_ + q
                    dve.wait_ge(S["dve_grp"], g + 1)
                    last = dve.tensor_tensor(G[:, c_, q], B[4 + g % 2][:, :].rearrange("p (h n) -> p h n", h=HP),
                                             bc(gmask[:, var:var + 1, :], [P, HP, P]), ALU.mult).then_inc(S["dve_out"], 1)
            for c_ in range(CH):
                var = 0 if c_ < 4 else 1
                g = 10 + c_
                dve.wait_ge(S["dve_grp"], g + 1)
                dve.tensor_tensor(PW[0][:, c_ * HP:c_ * HP + HP], B[4 + g % 2][:, 0:256].rearrange("p (h n) -> p h n", h=HP),
                                  bc(amask[:, var:var + 1, :], [P, HP, L]), ALU.mult).then_inc(S["dve_out"], 1)
            dve.wait_ge(S["dve_out"], 15)
            for q in range(2):
                for c_ in range(CH):
                    dve.tensor_copy(PWT[0][half(q), c_ * HP:c_ * HP + HP], G[half(q), c_, q, :, 0:L])
                    last = dve.tensor_tensor(X[half(q), c_ * HP:c_ * HP + HP], G[half(q), c_, q, :, 0:L],
                                             bc(id2[half(q), :].rearrange("p (a n) -> p a n", a=1), [64, HP, L]), ALU.add)
            last.then_inc(S["pwt_out"], 1)
            for c_ in range(CH):
                dve.wait_ge(S["dve_grp"], 16 + c_)
                dve.tensor_copy(AKV[:, c_], B[4 + (15 + c_) % 2][:, 0:256].rearrange("p (h n) -> p h n", h=HP)).then_inc(S["dve_out"], 1)
            dve.wait_ge(S["pwt_out"], 1)
            n = 0
            for it in range(1, 6):
                for g, (m0, m1) in enumerate(GROUPS[it > 1]):
                    n += 1
                    dve.wait_ge(S["x_sum"], n)
                    w = (m1 - m0) * L
                    dve.tensor_tensor(X[:, m0:m1], X[:, m0:m1], B[6 + n % 2][:, 0:w].rearrange("p (m n) -> p m n", n=L), ALU.add).then_inc(S["x_out"], 1)
            dve.wait_ge(S["bonus_sum"], HP)
            for h in range(HP):
                last = dve.tensor_tensor(f1[:, h], B[h][:, 0:NT], v[:, h], ALU.mult)
                last.then_inc(S["sv_done"], 1)
            for c_ in range(4):
                if c_ == 0:
                    dve.wait_ge(S["dve_out"], 20)
                    dve.tensor_copy(RHS[:, :, :], AKV[:, 0]).then_inc(S["rhs_out"], 1)
                else:
                    dve.wait_ge(S["rhs_sum"], c_)
                    dve.tensor_tensor(RHS[:, :, :], AKV[:, c_], B[0][:, 0:256].rearrange("p (h n) -> p h n", h=HP), ALU.add).then_inc(S["rhs_out"], 1)
                wc = bc(e1[:, :, c_ * L + L - 1:c_ * L + L], [P, HP, L])
                dve.wait_ge(S["st_sum"], c_ + 1)
                ps = B[3][:, 0:256].rearrange("p (h n) -> p h n", h=HP)
                if c_ == 0:
                    dve.tensor_tensor(ST[:, 0], ps, wc, ALU.mult).then_inc(S["st_out"], 1)
                else:
                    dve.wait_ge(S["st_out"], c_)
                    ln(dve.tensor_tensor(STt[:, :, :], ps, ST[:, (c_ - 1) % 2], ALU.add))
                    dve.tensor_tensor(ST[:, c_ % 2], STt[:, :, :], wc, ALU.mult).then_inc(S["st_out"], 1)
            dve.wait_ge(S["sa_sum"], 4)
            ln(dve.memset(RHS[:, :, :], 0.0))
            dve.wait_ge(S["rhs_sum"], 4)
            for q in range(2):
                lo = slice(q * 64, q * 64 + NS)
                last = dve.tensor_tensor(RHS[lo], AKV[lo, 4], B[0][lo, 0:256].rearrange("p (h n) -> p h n", h=HP), ALU.add)
            last.then_inc(S["rhs_out"], 1)
            dve.wait_ge(S["sa_out"], 5)
            def restricted(h):
                if h >= 2:
                    dve.wait_ge(S["ss_sum"], h - 1)
                for q in range(2):
                    last = dve.tensor_tensor(UBs[h % 2][:, q], bc(U[:, 4, q, h].rearrange("p (a l) -> p a l", a=1), [P, NB, L]),
                                      bc(bmask[:, :].rearrange("p (b a) -> p b a", a=1), [P, NB, L]), ALU.mult)
                last.then_inc(S["ub_done"], 1)

            restricted(0)
            for h in range(HP):
                if h + 1 < HP:
                    restricted(h + 1)
                dve.wait_ge(S["ss_sum"], h + 1)
                ln(dve.tensor_tensor(s0t[:, :, h], s0t[:, :, h], B[4 + h % 2][:, :].rearrange("p (b l) -> p b l", b=NB), ALU.add))
                dve.tensor_tensor(s0t[:, :, h], s0t[:, :, h],
                                  bc(e1[:, h, TP + TS - 1:NT:TS].rearrange("p (b a) -> p b a", a=1), [P, NB, L]), ALU.mult).then_inc(S["ss_out"], 1)
            dve.wait_ge(S["y_out"], 5)
            dve.wait_ge(S["mean_sum"], HP)
            for h in range(HP):
                dve.scalar_tensor_tensor(e2[:, h], B[h][:, 0:NT], -1.0 / 64, yT[:, h], ALU.mult, ALU.add).then_inc(S["yc_done"], 1)
            dve.wait_ge(S["var_sd"], 1)
            dve.reciprocal(rows8, rows8).then_inc(S["var_rows"], 1)
            for h in range(HP):
                dve.wait_ge(S["var_all"], h + 1)
                last = dve.tensor_tensor(e2[:, h], e2[:, h], B[4 + h][:, 0:NT], ALU.mult)
            ln(last)
            for h in range(HP):
                last = dve.tensor_scalar(e3[:, h], e2[:, h], lng[:, h:h + 1], lnb[:, h:h + 1], ALU.mult, ALU.add)
            ln(last)
            ln(dve.tensor_tensor(e3, e3, f1[:, :, :], ALU.add))
            dve.tensor_tensor(ymix[:, 4:8], e3, Gt[:, :, :], ALU.mult).then_inc(S["yn_done"], 1)

        @block.scalar
        def _(act):
            act.wait_ge(S["mixed"], 2)
            act.activation(lw[0:64, 0], z[0:64, Z_WA], ACT.Tanh).then_inc(S["lora_in"], 1)
            act.activation(lw[:, 1], z[:, Z_G], ACT.Sigmoid).then_inc(S["lora_in"], 1)
            act.wait_ge(S["mixed"], 14)
            for h in range(HP):
                act.wait_ge(S["lora_sum"], h + 1)
                act.activation(e1[:, h], B[h][:, 0:NT], ACT.Sigmoid, bias=w0[:, h:h + 1]).then_inc(S["lora_out"], 1)
            for h in range(HP):
                act.wait_ge(S["lora_sum"], HP + h + 1)
                act.activation(av[:, h], B[4 + h][:, 0:NT], ACT.Sigmoid, bias=a0[:, h:h + 1]).then_inc(S["lora_out"], 1)
            for h in range(HP):
                act.wait_ge(S["lora_sum"], 2 * HP + h + 1)
                act.activation(Gt[:, h], B[h][:, 0:NT], ACT.Copy).then_inc(S["lora_out"], 1)
            act.wait_ge(S["kk_sq"], HP)
            act.activation(f2[:, :, :], f1[:, :, :], ACT.Square).then_inc(S["ld_done"], 1)
            act.wait_ge(S["kk_max"], 1)
            act.activation(rows8, rows8, ACT.Sqrt).then_inc(S["kk_sd"], 1)
            act.wait_ge(S["cum_done"], 1)
            act.activation(e3, e3, ACT.Exp).then_inc(S["w_done"], 1)
            act.activation(e1, e2, ACT.Exp).then_inc(S["w_done"], 1)
            act.wait_ge(S["w_done"], 2)
            act.activation(e2, e2, ACT.Exp, scale=-1.0).then_inc(S["w_done"], 1)
            act.wait_ge(S["zeroed"], 3)
            for c_ in range(CH):
                act.wait_ge(S["act_grp"], c_ + 1)
                n = L if c_ < 4 else NS
                for q in range(2):
                    lo = (1 - q) * 64
                    last = act.activation(U[lo:lo + n, c_, q], B[c_ % 3][lo:lo + n, 0:256].rearrange("p (h l) -> p h l", h=HP), ACT.Copy)
                last.then_inc(S["act_out"], 1)
            for c_ in range(CH):
                act.wait_ge(S["act_grp"], CH + c_ + 1)
                act.activation(BKt[:, c_], B[(CH + c_) % 3][:, :].rearrange("p (h l) -> p h l", h=HP), ACT.Copy).then_inc(S["act_out"], 1)
            n = 0
            for it in range(1, 6):
                src, dst = (it - 1) % 2, it % 2
                for g, (m0, m1) in enumerate(GROUPS[it > 1]):
                    n += 1
                    act.wait_ge(S["pw_sum"], n)
                    w = (m1 - m0) * L
                    act.activation(PW[dst][:, m0:m1], B[g][:, 0:w].rearrange("p (m n) -> p m n", n=L), ACT.Copy).then_inc(S["pw_out"], 1)
                    if it < 5:
                        act.wait_ge(S["pwt_sum"], n)
                        act.activation(PWT[dst][:, m0:m1], B[3 + g][:, 0:w].rearrange("p (m n) -> p m n", n=L), ACT.Copy).then_inc(S["pwt_out"], 1)
            act.wait_ge(S["i0_sum"], 1)
            act.activation(I0[:, :, :, :], B[5][:, 0:256].rearrange("p (h a t) -> p h a t", h=HP, a=2), ACT.Copy).then_inc(S["i0_out"], 1)
            for c_ in range(CH):
                act.wait_ge(S["sa_sum"], c_ + 1)
                for q in range(2):
                    last = act.activation(U[half(q), c_, q], B[1][half(q), 0:256].rearrange("p (h l) -> p h l", h=HP), ACT.Copy)
                last.then_inc(S["sa_out"], 1)
                act.wait_ge(S["y_sum"], c_ + 1)
                n = L if c_ < 4 else NS
                act.activation(yT[:, :, c_ * L:c_ * L + n], B[2][:, 0:HP * n].rearrange("p (h t) -> p h t", h=HP), ACT.Copy).then_inc(S["y_out"], 1)
            for h in range(HP):
                act.wait_ge(S["yc_done"], h + 1)
                act.activation(f2[:, h], e2[:, h], ACT.Square).then_inc(S["yc_sq"], 1)
            act.wait_ge(S["var_sum"], 1)
            act.activation(rows8, B[4][0:8, 0:NT], ACT.Sqrt, scale=1.0 / 64, bias=c.eps[0:8, 3:4]).then_inc(S["var_sd"], 1)

        @block.tensor
        def _(pe):
            pe.wait_ge(S["par_loaded"], 16 * 9)
            pe.wait_ge(S["lora_in"], 2)
            for h in range(HP):
                pe.matmul(B[h][:, 0:NT], wa2[0:64, h * P:h * P + P], lw[0:64, 0], start=True, stop=True).then_inc(S["lora_sum"], 1)
            for h in range(HP):
                pe.matmul(B[4 + h][:, 0:NT], wa2[64:128, h * P:h * P + P], z[64:128, Z_WA], start=True, stop=True).then_inc(S["lora_sum"], 1)
            for h in range(HP):
                pe.wait_ge(S["lora_out"], h + 1)
                pe.matmul(B[h][:, 0:NT], g2[:, h * P:h * P + P], lw[:, 1], start=True, stop=True).then_inc(S["lora_sum"], 1)
            pe.wait_ge(S["lora_out"], 2 * HP)
            pe.wait_ge(S["ld_done"], 1)
            for h in range(HP):
                mm = pe.matmul(B[4][0:8, 0:NT], pair_cols[:, h], f2[:, h], start=(h == 0), stop=(h == HP - 1))
            mm.then_inc(S["kk_sum"], 1)
            pe.wait_ge(S["kk_rows"], 1)
            for h in range(HP):
                pe.matmul(B[4 + h][:, 0:NT], pair_rows[:, h], rows8, start=True, stop=True).then_inc(S["kk_all"], 1)
            pe.wait_ge(S["lora_out"], 3 * HP)
            pe.wait_ge(S["mixed"], 14)
            for c_ in range(CH):
                n = L if c_ < 4 else NS
                if c_ >= 3:
                    pe.wait_ge(S["act_out"], c_ - 2)
                for q in range(2):
                    lo = (1 - q) * 64
                    for h in range(HP):
                        mm = pe.matmul(B[c_ % 3][lo:lo + n, h * L:h * L + L], v[:, h, c_ * L:c_ * L + n],
                                       c.ident[:, half(q)], start=True, stop=True)
                mm.then_inc(S["act_grp"], 1)
            pe.wait_ge(S["bk_done"], 1)
            for c_ in range(CH):
                pe.wait_ge(S["act_out"], CH + c_ - 2)
                for h in range(HP):
                    mm = pe.transpose(B[(CH + c_) % 3][:, h * P:h * P + P], BK[:, h, c_].rearrange("p a l -> p (a l)"), c.ident[:, :])
                mm.then_inc(S["act_grp"], 1)
            g = 0
            for c_ in range(CH):
                for q in range(2):
                    if g >= 2:
                        pe.wait_ge(S["dve_out"], g - 1)
                    for h in range(HP):
                        mm = pe.matmul(B[4 + g % 2][:, h * P:h * P + P], BK[half(q), h, c_].rearrange("p a l -> p (a l)"),
                                       AR[half(q), :, h, c_ * L:c_ * L + L], start=True, stop=True)
                    mm.then_inc(S["dve_grp"], 1)
                    g += 1
            for c_ in range(CH):
                pe.wait_ge(S["dve_out"], g - 1)
                for h in range(HP):
                    for q in range(2):
                        mm = pe.matmul(B[4 + g % 2][half(q), h * L:h * L + L], AR[half(q), 0, h, c_ * L:c_ * L + L],
                                       BK[half(q), h, c_, q], start=True, stop=True)
                mm.then_inc(S["dve_grp"], 1)
                g += 1
            pe.wait_ge(S["act_out"], CH)
            for c_ in range(CH):
                pe.wait_ge(S["dve_out"], g - 1)
                for h in range(HP):
                    for q in range(2):
                        o = half(1 - q)
                        mm = pe.matmul(B[4 + g % 2][half(q), h * L:h * L + L], G[o, c_, q, h, 0:L], U[o, c_, q, h], start=True, stop=True)
                mm.then_inc(S["dve_grp"], 1)
                g += 1
            pe.wait_ge(S["dve_out"], 20)
            pe.wait_ge(S["act_out"], 2 * CH)
            pe.wait_ge(S["pwt_out"], 1)
            n = 0
            for it in range(1, 6):
                src, dst = (it - 1) % 2, it % 2
                n0 = n
                groups = GROUPS[it > 1]
                if it == 2:
                    pe.wait_ge(S["pw_out"], n)
                    pe.wait_ge(S["pwt_out"], 1 + n)
                for g, (m0, m1) in enumerate(groups):
                    n += 1
                    if it > 2:
                        pe.wait_ge(S["pw_out"], n - len(groups))
                        pe.wait_ge(S["pwt_out"], 1 + n - len(groups))
                    for m in range(m0, m1):
                        for q in range(2):
                            mm = pe.matmul(B[g][half(q), (m - m0) * L:(m - m0) * L + L], PWT[src][half(q), m], PW[src][half(q), m], start=True, stop=True)
                    mm.then_inc(S["pw_sum"], 1)
                    if it < 5:
                        for m in range(m0, m1):
                            for q in range(2):
                                mm = pe.matmul(B[3 + g][half(q), (m - m0) * L:(m - m0) * L + L], PW[src][half(q), m], PWT[src][half(q), m], start=True, stop=True)
                        mm.then_inc(S["pwt_sum"], 1)
                n = n0
                for g, (m0, m1) in enumerate(groups):
                    n += 1
                    pe.wait_ge(S["pw_out"], n)
                    if n > 2:
                        pe.wait_ge(S["x_out"], n - 2)
                    if it > 1:
                        pe.wait_ge(S["x_out"], n - len(groups) if it > 2 else 3)
                    for m in range(m0, m1):
                        for q in range(2):
                            mm = pe.matmul(B[6 + n % 2][half(q), (m - m0) * L:(m - m0) * L + L], PW[dst][half(q), m], X[half(q), m], start=True, stop=True)
                    mm.then_inc(S["x_sum"], 1)
            n_x = n
            pe.wait_ge(S["prod_done"], HP)
            for h in range(HP):
                pe.matmul(B[h][:, 0:NT], c.half_ones[:, :], e2[:, h], start=True, stop=True).then_inc(S["bonus_sum"], 1)
            pe.wait_ge(S["state_loaded"], 16)
            for b in range(NB):
                for h in range(HP):
                    for q in range(2):
                        mm = pe.matmul(B[5][half(q), 0:256].rearrange("p (h a t) -> p h a t", h=HP, a=2)[:, h, :, b * TS:b * TS + TS],
                                       s0t[half(q), b, h], AR[half(q), :, h, TP + b * TS:TP + b * TS + TS], start=True, stop=True)
            mm.then_inc(S["i0_sum"], 1)
            pe.wait_ge(S["x_out"], n_x)
            pe.wait_ge(S["sv_done"], HP)
            for c_ in range(CH):
                if 0 < c_ < 4:
                    pe.wait_ge(S["st_out"], c_)
                    for h in range(HP):
                        for q in range(2):
                            mm = pe.matmul(B[0][half(q), h * L:h * L + L], AR[half(q), 0, h, c_ * L:c_ * L + L], ST[half(q), (c_ - 1) % 2, h], start=True, stop=True)
                    mm.then_inc(S["rhs_sum"], 1)
                if c_ == 4:
                    pe.wait_ge(S["i0_out"], 1)
                    for h in range(HP):
                        for q in range(2):
                            mm = pe.matmul(B[0][q * 64:q * 64 + NS, h * L:h * L + L], I0[half(q), h, 0], c.ident[half(q), half(q)], start=True, stop=True)
                    mm.then_inc(S["rhs_sum"], 1)
                pe.wait_ge(S["rhs_out"], c_ + 1)
                for h in range(HP):
                    for q in range(2):
                        mm = pe.matmul(B[1][half(q), h * L:h * L + L], X[half(q), c_ * HP + h], RHS[half(q), h], start=True, stop=True)
                mm.then_inc(S["sa_sum"], 1)
                pe.wait_ge(S["sa_out"], c_ + 1)
                n = L if c_ < 4 else NS
                if c_ < 4:
                    if c_ > 0:
                        pe.wait_ge(S["st_out"], c_)
                    for h in range(HP):
                        for q in range(2):
                            mm = pe.matmul(B[3][half(q), h * L:h * L + L], BKt[:, c_, h, half(q)], U[:, c_, q, h], start=True, stop=True)
                    mm.then_inc(S["st_sum"], 1)
                if c_ > 0:
                    pe.wait_ge(S["y_out"], c_)
                for h in range(HP):
                    for q in range(2):
                        mm = pe.matmul(B[2][half(q), h * n:h * n + n], U[:, c_, q, h], G[:, c_, q, h, L:L + n], start=True, stop=(c_ == 0))
                        if 0 < c_ < 4:
                            mm = pe.matmul(B[2][half(q), h * n:h * n + n], ST[half(q), (c_ - 1) % 2, h], AR[half(q), 1, h, c_ * L:c_ * L + L], start=False, stop=True)
                        if c_ == 4:
                            mm = pe.matmul(B[2][half(q), h * n:h * n + n], c.ident[half(q), half(q)], I0[half(q), h, 1], start=False, stop=True)
                mm.then_inc(S["y_sum"], 1)
            for h in range(HP):
                pe.wait_ge(S["ub_done"], h + 1)
                if h > 1:
                    pe.wait_ge(S["ss_out"], h - 1)
                for q in range(2):
                    mm = pe.matmul(B[4 + h % 2][half(q), :], BKt[:, 4, h, half(q)], UBs[h % 2][:, q], start=True, stop=True)
                mm.then_inc(S["ss_sum"], 1)
            pe.wait_ge(S["y_out"], 5)
            for h in range(HP):
                pe.matmul(B[h][:, 0:NT], c.half_ones[:, :], yT[:, h], start=True, stop=True).then_inc(S["mean_sum"], 1)
            pe.wait_ge(S["ss_out"], HP)
            for h in range(HP):
                pe.wait_ge(S["yc_sq"], h + 1)
                mm = pe.matmul(B[4][0:8, 0:NT], pair_cols[:, h], f2[:, h], start=(h == 0), stop=(h == HP - 1))
            mm.then_inc(S["var_sum"], 1)
            pe.wait_ge(S["var_rows"], 1)
            for h in range(HP):
                pe.matmul(B[4 + h][:, 0:NT], pair_rows[:, h], rows8, start=True, stop=True).then_inc(S["var_all"], 1)


GROUPS = (((0, 8), (8, 16), (16, 20)), ((0, 8), (8, 16)))



NEG = -1.0e30
TAKEN = -3.0e38
KP = 64
KS = 256
PAST = 1024
NPG = 8
KEYS = PAST + NS
CHUNKS = ((0, 512), (512, 512), (PAST, NS))
SCALE_A = 64 ** -0.5


class IndexKeys:

    def __init__(self, c, ctx):
        self.table = c.sb("table", [1, NB * NPG], I32, ctx=ctx)
        self.keys = c.sb("index_keys", [P, NB, PAST], ctx=ctx)
        self.table_loaded, self.landed = c.stage_sem("table_loaded"), c.stage_sem("index_keys_landed")


def dsa_stage(c, z, vtok, ymix, idx):
    nc = c.nc
    S = {n: c.stage_sem(n + "_ds") for n in (
        "par_loaded", "ki_sq", "ki_sum", "ki_sd", "ki_done", "wi_sum", "wi_done", "qi_done", "qz_zero", "qz_done",
        "ip_sum", "ip_rel", "ip_acc", "is_sum", "is_rel", "is_used", "is_out",
        "tp_max", "tp_rep", "mp_done", "ts_max", "ts_rep", "ms_done",
        "sp_sum", "ri_done", "nb_done", "sp_exp", "pn_done", "pt_sum", "pt_out", "op_sum", "op_out",
        "ks_sum", "ks_out", "mb_sum", "mb_done", "ss_nb", "ss_exp", "ss_norm", "st_sum", "st_out", "pv_sum", "pv_out", "kv_used")}
    kv_landed = [c.stage_sem(f"kv_landed{i}") for i in range(5)]
    with ExitStack() as ctx:
        def sb(n, shape, dt=F32):
            return c.sb(n + "_ds", shape, dt, ctx=ctx)
        table, kix = idx.table, idx.keys
        kidg = sb("kidg", [P, 1])
        cmask = sb("cmask", [P, 2, TP])
        nmask = sb("nmask", [NS, NS])
        esel = sb("esel", [16, P])
        wmask = sb("wmask", [P, 4, NS])
        bsel = sb("bsel", [NS, 2, P])
        kisq, kisd = sb("kisq", [P, NT]), sb("kisd", [P, NT])
        wip, wsel = sb("wip", [P, 32]), sb("wsel", [P, 4, NS])
        qi = sb("qi", [P, NB, 2, 8, TS])
        qz = sb("qz", [P, NB, HP, NS])
        spare = c.down[:, :].rearrange("p s k m -> p (s k m)")
        rel = spare[:, 0:3 * 512].rearrange("p (u n) -> p u n", u=3)
        sc = spare[:, 3 * 512:3 * 512 + 2 * KEYS].rearrange("p (g n) -> p g n", g=2)
        ip = sb("ip", [P, 2, TP])
        work = sb("work", [P, 2, TP])
        t8 = sb("t8", [P, 2, 8])
        mp = sb("mp", [P, 2, TP])
        iss, wks = sb("iss", [NS, KEYS]), sb("wks", [NS, KEYS])
        t8s = sb("t8s", [NS, 8])
        xflat = c.xscratch[:, :].rearrange("p k t -> p (k t)")
        pa = xflat[:, 0:4 * TP].rearrange("p (a b t) -> p a b t", a=2, b=2)
        pa_flat = xflat[:, 0:4 * TP].rearrange("p (g n) -> p g n", g=2)
        pt = xflat[:, 4 * TP:8 * TP].rearrange("p (a b t) -> p a b t", a=2, b=2)
        mx, nb_, rs, ri = (sb(n, [P, 2, 2]) for n in ("mx", "nb", "rs", "ri"))
        mxs, nbs, rss, ris = (sb(n, [P, 2]) for n in ("mxs", "nbs", "rss", "ris"))
        pts = c.xscratch2[:, :].rearrange("p k t -> p (k t)")[:, 0:9 * 2 * P].rearrange("p (g j r) -> p g j r", g=2, j=9)
        ring_kv = c.ring[:, :].rearrange("p (s u) a k m -> p s (u a k m)", s=2)
        kix_kv = kix[:, :].rearrange("p (s b) n -> p s (b n)", s=2)
        slots = [ring_kv[:, 0], ring_kv[:, 1], kix_kv[:, 0], kix_kv[:, 1]]
        after_sc = 3 * 512 + 2 * KEYS
        PIECES = (0, 512, 1024, after_sc, after_sc + 512, after_sc + 1024)
        assert PIECES[5] + 512 <= 2 * FT * P
        two_pages = sb("two_pages", [P, 1024])
        VALUE_SLOTS = (2, 3, 0, 1, 4, 2, 3, 0)
        VALUE_LOADS = (1, 1, 5, 5, 1, 2, 2, 6)

        def page_of(slot, j):
            if slot < 4:
                return slots[slot][:, j * 512:(j + 1) * 512]
            return two_pages[:, (j - 6) * 512:(j - 5) * 512] if j >= 6 else spare[:, PIECES[j]:PIECES[j] + 512]

        block = ctx.enter_context(nc.Block())
        B = c.banks
        q, k, qz_src, ki = z[:, 0:4], z[:, 4:8], z[:, 8:16], z[:, 30]

        def half(u):
            return slice(u * 64, u * 64 + 64)

        @block.sync
        def _(sp):
            for dst, src in ((kidg[:, :], "kidg"), (cmask[:, :, :], "cmask"), (nmask[:, :], "nmask"), (esel[:, :], "esel"),
                             (wmask[:, :, :], "wmask"), (bsel[:, :, :], "bsel")):
                sp.dma_start(dst, c.ins[src]).then_inc(S["par_loaded"], 16)

            def load(src, b, slot, wait):
                pages = [sp.value_load(table[0:1, bass.ds(b * NPG + j, 1)], min_val=0, max_val=c.n_pool - 1) for j in range(NPG)]
                if wait:
                    sp.wait_ge(*wait)
                for j, page in enumerate(pages):
                    sp.dma_start(page_of(slot, j),
                                 c.ins[src][bass.ds(page, 1)].rearrange("a p n -> (a p) n")).then_inc(kv_landed[slot], 16)
            for b in range(2):
                load("cache_k", b, b, None)
            with sp.Fori(0, NB // 2 - 1) as i:
                for s in range(2):
                    load("cache_k", i * 2 + (2 + s), s, (S["kv_used"], i * 2 + (s + 1)))
            for b in range(2):
                load("cache_v", b, VALUE_SLOTS[b], (S["is_sum"], 12))
            for b in range(2, NB):
                wait = (S["kv_used"], NB - 1 + b - 2) if b < 4 else (S["is_used"], 12) if b == 4 else (S["kv_used"], NB + b - 4)
                load("cache_v", b, VALUE_SLOTS[b], wait)
            sp.wait_ge(S["ki_done"], 1)
            c.store(sp, c.outs["kidx"], ki[0:64])
            stores_done(c, sp)

        @block.gpsimd
        def _(pool):
            pool.memset(qi[:, :, :, :, :], 0.0).then_inc(S["qz_zero"], 1)
            pool.memset(qz[:, :, :, :], 0.0).then_inc(S["qz_zero"], 1)

        @block.tensor
        def _(pe):
            pe.wait_ge(S["ki_sq"], 1)
            pe.matmul(B[0][:, 0:NT], c.half_ones[:, :], kisq[:, :], start=True, stop=True).then_inc(S["ki_sum"], 1)
            pe.wait_ge(S["par_loaded"], 96)
            for t in range(2):
                pe.matmul(B[1][:, t * 16:t * 16 + 16], z[0:16, 31, t * P:t * P + P], c.ident[0:16, 0:16], start=True, stop=True)
            pe.matmul(B[1][:, 32:64], esel[:, :], z[0:16, 31, TP:NT], start=True, stop=True).then_inc(S["wi_sum"], 1)
            pe.wait_ge(S["ki_done"], 1)
            for u in range(16):
                t, j, p_ = u // 8, (u // 2) % 4, u % 2
                if u >= 4:
                    pe.wait_ge(S["ip_rel"], u - 3)
                for e in range(2):
                    mm = pe.matmul(B[2 + u % 4][:, e * TP:(e + 1) * TP], qz_src[half(p_), 2 * j + e, t * P:(t + 1) * P], ki[half(p_), 0:TP],
                                   start=True, stop=True)
                mm.then_inc(S["ip_sum"], 1)
            pe.wait_ge(S["qi_done"], 1)
            pe.wait_ge(S["wi_done"], 1)
            pe.wait_ge(S["ip_rel"], 16)

            def weigh(n):
                g, ch = n // 3, n % 3
                c0, w = CHUNKS[ch]
                pe.wait_ge(S["is_rel"], n + 1)
                pe.matmul(B[5 + ch][0:NS, 0:w], wsel[:, g], rel[:, n % 3, 0:w], start=(g == 0), stop=(g == 3)).then_inc(S["is_used"], 1)

            for n in range(12):
                g, ch = n // 3, n % 3
                c0, w = CHUNKS[ch]
                if ch == 0:
                    pe.wait_ge(idx.landed, 16 * NB * NPG)
                if n >= 3:
                    pe.wait_ge(S["is_rel"], n - 2)
                for e in range(2):
                    b = 2 * g + e
                    rhs = kix[:, b, c0:c0 + w] if ch < 2 else ki[:, TP:NT]
                    mm = pe.matmul(B[2 + n % 3][64 * e:64 * e + 64, 0:w], qi[:, b].rearrange("p a h t -> p (a h t)"), rhs, start=True, stop=True)
                mm.then_inc(S["is_sum"], 1)
                if n >= 1:
                    weigh(n - 1)
            weigh(11)
            pe.wait_ge(S["wi_done"], 1)

            def probs_out(h):
                pe.wait_ge(S["pn_done"], h + 1)
                if h >= 2:
                    pe.wait_ge(S["pt_out"], h - 1)
                for kt in range(2):
                    for t in range(2):
                        mm = pe.transpose(B[2 + h % 2][:, kt * TP + t * P:kt * TP + t * P + P], pa[:, h % 2, t, kt * P:kt * P + P], c.ident[:, :])
                mm.then_inc(S["pt_sum"], 1)

            def values(h):
                hp, p_ = h // 2, h % 2
                pe.wait_ge(S["pt_out"], h + 1)
                if h == 0:
                    pe.wait_ge(S["is_rel"], 12)
                if p_ == 0 and hp >= 1:
                    pe.wait_ge(S["op_out"], hp)
                for kt in range(2):
                    mm = pe.matmul(B[4][half(p_), 0:TP], vtok[:, kt, h * 64:h * 64 + 64], pt[:, h % 2, kt], start=(kt == 0), stop=(kt == 1))
                mm.then_inc(S["op_sum"], 1)

            def key_scores(b):
                b4 = b % 4
                if b == 0:
                    pe.wait_ge(S["qz_done"], 1)
                    pe.wait_ge(S["is_out"], 3)
                if b == 4:
                    pe.wait_ge(S["ks_out"], 3)
                pe.wait_ge(kv_landed[b % 2], 128 * (b // 2 + 1))
                kb = slots[b % 2].rearrange("p (j h n) -> p j h n", j=NPG, h=HP)
                for ch, (c0, w) in enumerate(CHUNKS):
                    for h in range(HP):
                        rhs = kb[:, 4 * ch:4 * ch + 4, h] if ch < 2 else k[:, h, TP:NT]
                        mm = pe.matmul(B[5 + ch][32 * b4:32 * b4 + 32, 0:w], qz[:, b, h], rhs, start=(h == 0), stop=(h == HP - 1))
                    if ch == 1:
                        mm.then_inc(S["kv_used"], 1)
                mm.then_inc(S["ks_sum"], 1)

            for h in range(8):
                if h == 0:
                    pe.wait_ge(S["mp_done"], 1)
                if h >= 2:
                    pe.wait_ge(S["sp_exp"], h - 1)
                for t in range(2):
                    out = B[h % 2][:, t * TP:(t + 1) * TP]
                    pe.matmul(out, q[half(h % 2), h // 2, t * P:(t + 1) * P], k[half(h % 2), h // 2, 0:TP], start=True, stop=False)
                    mm = pe.matmul(out, c.ident[:, :], mp[:, t], start=False, stop=True)
                mm.then_inc(S["sp_sum"], 1)
                if h >= 1:
                    probs_out(h - 1)
                if h >= 2:
                    values(h - 2)
                key_scores(h)
            probs_out(7)
            values(6)
            values(7)
            pe.wait_ge(S["ms_done"], 1)
            pe.wait_ge(S["ks_out"], 6)
            for n in range(6):
                g, ch = n // 3, n % 3
                c0, w = CHUNKS[ch]
                if n >= 2:
                    pe.wait_ge(S["mb_done"], n - 1)
                pe.matmul(B[6 + n % 2][:, 0:w], bsel[:, g], iss[:, c0:c0 + w], start=True, stop=True).then_inc(S["mb_sum"], 1)
            pe.wait_ge(S["pt_out"], 8)
            for g in range(2):
                pe.wait_ge(S["ss_norm"], g + 1)
                for m in range(3):
                    n = 3 * g + m
                    if n >= 3:
                        pe.wait_ge(S["st_out"], n - 2)
                    for j in range(4 * m, min(4 * m + 4, 9)):
                        w = P if j < 8 else NS
                        mm = pe.transpose(B[m][0:w, (j - 4 * m) * P:(j - 4 * m + 1) * P], sc[:, g, j * P:j * P + w], c.ident[:, :])
                    mm.then_inc(S["st_sum"], 1)
            def heads_transposed(g):
                pe.wait_ge(S["pv_out"], g + 1)
                pe.wait_ge(S["st_out"], 6)
                for h in range(HP):
                    mm = pe.transpose(B[g][:, h * P:h * P + P], pa_flat[:, g, h * P:h * P + P], c.ident[:, :])
                mm.then_inc(S["pv_sum"], 1)

            for b in range(NB):
                g, b4 = b // 4, b % 4
                pe.wait_ge(kv_landed[VALUE_SLOTS[b]], 128 * VALUE_LOADS[b])
                if b4 == 0:
                    pe.wait_ge(S["st_out"], 3 * g + 3)
                cols = slice(32 * b4, 32 * b4 + 32)
                for j in range(NPG):
                    pe.matmul(B[5 + g][cols, :], pts[:, g, j, cols], page_of(VALUE_SLOTS[b], j), start=(j == 0), stop=False)
                pe.matmul(B[5 + g][cols, :], pts[0:NS, g, 8, cols], vtok[0:NS, 2, :], start=False, stop=True).then_inc(S["kv_used"], 1)
                if b == 4:
                    heads_transposed(0)
            heads_transposed(1)

        def pt_out(act, h):
            act.wait_ge(S["pt_sum"], h + 1)
            if h >= 2:
                act.wait_ge(S["op_sum"], h - 1)
            act.activation(pt[:, h % 2], B[2 + h % 2][:, :].rearrange("p (k n) -> p k n", k=2), ACT.Copy).then_inc(S["pt_out"], 1)

        @block.scalar
        def _(act):
            act.activation(kisq[:, :], ki, ACT.Square).then_inc(S["ki_sq"], 1)
            act.wait_ge(S["ki_sum"], 1)
            act.activation(kisd[:, :], B[0][:, 0:NT], ACT.Sqrt, scale=1.0 / 64, bias=c.eps[:, 0:1]).then_inc(S["ki_sd"], 1)
            for u in range(16):
                act.wait_ge(S["ip_sum"], u + 1)
                if u >= 3:
                    act.wait_ge(S["ip_acc"], 2 * (u - 2))
                act.activation(rel[:, u % 3], B[2 + u % 4][:, :], ACT.Relu).then_inc(S["ip_rel"], 1)
            act.wait_ge(S["ip_acc"], 32)
            for n in range(12):
                w = CHUNKS[n % 3][1]
                act.wait_ge(S["is_sum"], n + 1)
                if n >= 3:
                    act.wait_ge(S["is_used"], n - 2)
                act.activation(rel[:, n % 3, 0:w], B[2 + n % 3][:, 0:w], ACT.Relu).then_inc(S["is_rel"], 1)
            def keys_out(g):
                for ch, (c0, w) in enumerate(CHUNKS):
                    act.wait_ge(S["ks_sum"], 4 * g + 4)
                    act.activation(sc[:, g, c0:c0 + w], B[5 + ch][:, 0:w], ACT.Copy).then_inc(S["ks_out"], 1)

            def norm(h):
                act.wait_ge(S["ri_done"], h + 1)
                for t in range(2):
                    ins = act.activation(pa[:, h % 2, t], pa[:, h % 2, t], ACT.Copy, scale=ri[:, h % 2, t:t + 1])
                ins.then_inc(S["pn_done"], 1)

            for h in range(8):
                act.wait_ge(S["nb_done"], h + 1)
                for t in range(2):
                    ins = act.activation(pa[:, h % 2, t], B[h % 2][:, t * TP:(t + 1) * TP], ACT.Exp, scale=SCALE_A, bias=nb_[:, h % 2, t:t + 1],
                                         accum_out=rs[:, h % 2, t:t + 1])
                ins.then_inc(S["sp_exp"], 1)
                if h >= 1:
                    norm(h - 1)
                    pt_out(act, h - 1)
                if h == 3:
                    keys_out(0)
            norm(7)
            pt_out(act, 7)
            keys_out(1)
            for g in range(2):
                act.wait_ge(S["ss_nb"], g + 1)
                act.activation(sc[:, g], sc[:, g], ACT.Exp, scale=SCALE_A, bias=nbs[:, g:g + 1], accum_out=rss[:, g:g + 1]).then_inc(S["ss_exp"], 1)
            for n in range(6):
                g, m = n // 3, n % 3
                act.wait_ge(S["st_sum"], n + 1)
                if m < 2:
                    act.activation(pts[:, g, 4 * m:4 * m + 4], B[m][:, :].rearrange("p (j r) -> p j r", j=4), ACT.Copy).then_inc(S["st_out"], 1)
                else:
                    act.activation(pts[0:NS, g, 8], B[m][0:NS, 0:P], ACT.Copy).then_inc(S["st_out"], 1)
            for g in range(2):
                act.wait_ge(S["kv_used"], NB + 4 * g + 4)
                act.activation(pa_flat[:, g], B[5 + g][:, :], ACT.Copy).then_inc(S["pv_out"], 1)

        @block.vector
        def _(dve):
            def ln(ins):
                c.link(dve, "dve", ins)
            dve.wait_ge(S["par_loaded"], 96)
            dve.wait_ge(S["ki_sd"], 1)
            ln(dve.reciprocal(kisd[:, :], kisd[:, :]))
            dve.scalar_tensor_tensor(ki, ki, kidg[:, 0:1], kisd[:, :], ALU.mult, ALU.mult).then_inc(S["ki_done"], 1)
            dve.wait_ge(S["wi_sum"], 1)
            dve.tensor_scalar(wip[:, :], B[1][:, 0:32], 1.0 / 32, None, ALU.mult)
            dve.tensor_tensor(wsel[:, :, :], wmask[:, :, :], B[1][:, 32:64].rearrange("p (a n) -> p a n", a=1).to_broadcast([P, 4, NS]),
                              ALU.mult).then_inc(S["wi_done"], 1)
            dve.wait_ge(S["qz_zero"], 1)
            for p_ in range(2):
                last = dve.tensor_copy(qi[half(p_), :, p_], qz_src[half(p_), :, TP:NT].rearrange("p h (b t) -> p b h t", t=TS))
            last.then_inc(S["qi_done"], 1)
            ln(dve.tensor_copy(ip[:, :, :], cmask[:, :, :]))
            n = 0
            for u in range(16):
                t, j, p_ = u // 8, (u // 2) % 4, u % 2
                dve.wait_ge(S["ip_rel"], u + 1)
                for e in range(2):
                    h = 2 * (2 * j + e) + p_
                    if n and n != 16:
                        dve.wait_ge(S["ip_acc"], n)
                    dve.scalar_tensor_tensor(ip[:, t], rel[:, u % 3, e * TP:(e + 1) * TP], wip[:, t * 16 + h:t * 16 + h + 1], ip[:, t],
                                             ALU.mult, ALU.add).then_inc(S["ip_acc"], 1)
                    n += 1
            dve.wait_ge(S["ip_acc"], 32)
            ln(dve.tensor_copy(work[:, :, :], ip[:, :, :]))
            n = 0
            for i in range(KP // 8):
                for t in range(2):
                    if i:
                        dve.wait_ge(S["tp_rep"], n - 1)
                    dve.max(t8[:, t], work[:, t]).then_inc(S["tp_max"], 1)
                    n += 1
                for t in range(2):
                    dve.wait_ge(S["tp_max"], n - 1 + t)
                    dve.match_replace(out=work[:, t], in_to_replace=t8[:, t], in_values=work[:, t], imm_value=TAKEN).then_inc(S["tp_rep"], 1)
            dve.wait_ge(S["tp_rep"], n)
            ln(dve.tensor_scalar(work[:, :, :], work[:, :, :], -2.0e38, NEG, ALU.is_gt, ALU.mult))
            dve.tensor_tensor(mp[:, :, :], work[:, :, :], cmask[:, :, :], ALU.add).then_inc(S["mp_done"], 1)
            dve.wait_ge(S["qz_zero"], 2)
            for h in range(HP):
                for p_ in range(2):
                    last = dve.tensor_copy(qz[half(p_), :, h, (2 * h + p_) * TS:(2 * h + p_) * TS + TS],
                                           q[half(p_), h, TP:NT].rearrange("p (b t) -> p b t", t=TS))
            last.then_inc(S["qz_done"], 1)

            def head(h):
                bf = h % 2
                dve.wait_ge(S["sp_sum"], h + 1)
                ln(dve.tensor_reduce(mx[:, bf], B[bf][:, :].rearrange("p (t n) -> p t n", t=2), AX_X, ALU.max))
                dve.tensor_scalar(nb_[:, bf], mx[:, bf], -SCALE_A, None, ALU.mult).then_inc(S["nb_done"], 1)

            def norm(h):
                bf = h % 2
                dve.wait_ge(S["sp_exp"], h + 1)
                dve.reciprocal(ri[:, bf], rs[:, bf]).then_inc(S["ri_done"], 1)

            def out(hp):
                dve.wait_ge(S["op_sum"], 2 * hp + 2)
                dve.tensor_copy(ymix[:, hp, 0:TP], B[4][:, 0:TP]).then_inc(S["op_out"], 1)

            for ch, (c0, w) in enumerate(CHUNKS):
                dve.wait_ge(S["is_used"], 10 + ch)
                if ch < 2:
                    dve.tensor_copy(iss[:, c0:c0 + w], B[5 + ch][0:NS, 0:w]).then_inc(S["is_out"], 1)
                else:
                    dve.tensor_tensor(iss[:, c0:c0 + w], B[5 + ch][0:NS, 0:w], nmask[:, :], ALU.add).then_inc(S["is_out"], 1)
            dve.wait_ge(S["is_out"], 3)
            ln(dve.tensor_copy(wks[:, :], iss[:, :]))

            def top_eight(i):
                if i:
                    dve.wait_ge(S["ts_rep"], i)
                dve.max(t8s[:, :], wks[:, :]).then_inc(S["ts_max"], 1)
                dve.wait_ge(S["ts_max"], i + 1)
                dve.match_replace(out=wks[:, :], in_to_replace=t8s[:, :], in_values=wks[:, :], imm_value=TAKEN).then_inc(S["ts_rep"], 1)

            for h in range(8):
                head(h)
                if h >= 1:
                    norm(h - 1)
                if h >= 4 and h % 2 == 0:
                    out(h // 2 - 2)
                for i in range(h * (KS // 8) // 8, (h + 1) * (KS // 8) // 8):
                    top_eight(i)
            norm(7)
            out(2)
            out(3)
            dve.wait_ge(S["ts_rep"], KS // 8)
            ln(dve.tensor_scalar(iss[:, :], wks[:, :], -2.0e38, NEG, ALU.is_gt, ALU.mult))
            dve.tensor_tensor(iss[:, PAST:KEYS], iss[:, PAST:KEYS], nmask[:, :], ALU.add).then_inc(S["ms_done"], 1)
            for g in range(2):
                for ch, (c0, w) in enumerate(CHUNKS):
                    n = 3 * g + ch
                    dve.wait_ge(S["ks_out"], n + 1)
                    dve.wait_ge(S["mb_sum"], n + 1)
                    dve.tensor_tensor(sc[:, g, c0:c0 + w], sc[:, g, c0:c0 + w], B[6 + n % 2][:, 0:w], ALU.add).then_inc(S["mb_done"], 1)
                dve.wait_ge(S["mb_done"], 3 * g + 3)
                ln(dve.tensor_reduce(mxs[:, g:g + 1], sc[:, g], AX_X, ALU.max))
                dve.tensor_scalar(nbs[:, g:g + 1], mxs[:, g:g + 1], -SCALE_A, None, ALU.mult).then_inc(S["ss_nb"], 1)
            for g in range(2):
                dve.wait_ge(S["ss_exp"], g + 1)
                ln(dve.reciprocal(ris[:, g:g + 1], rss[:, g:g + 1]))
                dve.tensor_scalar(sc[:, g], sc[:, g], ris[:, g:g + 1], None, ALU.mult).then_inc(S["ss_norm"], 1)
            for g in range(2):
                dve.wait_ge(S["pv_sum"], g + 1)
                for h in range(8):
                    src = B[g][half(h % 2), (h // 2) * P:(h // 2) * P + P].rearrange("p (b h t) -> p b h t", b=4, h=8)
                    dve.tensor_copy(ymix[half(h % 2), h // 2, TP + 16 * g:TP + 16 * g + 16].rearrange("p (b t) -> p b t", t=TS), src[:, :, h])


def cd_in_stage(c, z, vtok, params):
    nc, npairs = c.nc, 8
    stream = c.ins["w_cd"]
    z_done, v_sum, rt_sum, rt_ready, v_done = (
        c.sem(n + "_cd") for n in ("z_done", "v_sum", "rt_sum", "rt_ready", "v_done"))
    first = c.pairs
    assert first % RING == 0
    with ExitStack() as ctx:
        rt = c.sb("rt_cd", [P, 3], ctx=ctx)
        whi = c.whi
        block = ctx.enter_context(nc.Block())

        @block.sync
        def _(sp):
            send_pairs(c, sp, stream, RING, 9)

        @block.tensor
        def _(pe):
            project_pe(c, pe, whi, z_done, npairs)
            token_rstd_pe(c, pe, rt_sum)
            for w in range(2):
                if w == 1:
                    pe.wait_ge(v_done, 3)
                project_values(c, pe, whi, first + npairs + 2 * w,
                               lambda i, mm: mm.then_inc(*((v_sum, 1) if i < 2 else (c.pair_done, 2))))
            s, b = (first + 12) % RING, (first + 12) % 2
            pe.wait_ge(c.pair_split, first + 13)
            pe.wait_ge(z_done, npairs)
            for half in range(2):
                for k in range(KT):
                    mm = three_products(pe, c.banks[half][:, 0:NT], whi[:, b, half, k], c.ring_lo[:, s, half, k], c.xhi[:, k], c.xlo[:, k],
                                        k == 0, k == KT - 1)
            mm.then_inc(c.pair_done, 1)

        @block.scalar
        def _(act):
            params.load(c, act)
            act.wait_ge(rt_sum, 1)
            for i, (t0, n) in enumerate(TOK):
                act.activation(rt[0:n, i:i + 1], c.banks[7][0:n, i:i + 1], ACT.Copy).then_inc(rt_ready, 1)
            for w in range(2):
                for i, (t0, n) in enumerate(TOK):
                    act.wait_ge(rt_ready, i + 1)
                    if i < 2:
                        act.wait_ge(v_sum, 2 * w + i + 1)
                    else:
                        act.wait_ge(c.pair_done, first + npairs + 2 * w + 2)
                    act.activation(vtok[0:n, 3 * w + i], c.banks[4 + i][0:n, :], ACT.Copy, scale=rt[0:n, i:i + 1]).then_inc(v_done, 1)

        @block.vector
        def _(dve):
            project_dve(c, dve, whi, z, z_done, npairs, first)
            for u in range(10, 13):
                dve.wait_ge(c.pair_done, first + (10 if u < 12 else 12))
                split_pair(c, dve, whi, first, u)
            dve.wait_ge(c.pair_done, first + 13)
            for half in range(2):
                dve.tensor_tensor(z[:, 16 + half], c.banks[half][:, 0:NT], c.rstd[:, :], ALU.mult)

    c.pairs += npairs + 5


SEQ = TP + TS - 1
ST_COLS = 384
EXT = 3 + TP


class CdParams:

    def __init__(self, c, ctx):
        def sb(n, shape, src=None):
            t = c.sb(n + "_cm", shape, ctx=ctx)
            self.loads.append((t, src or n))
            return t
        self.loads = []
        self.loaded = c.stage_sem("cd_params_loaded")
        self.par = sb("par", [P, 8 + 4 * 5 + 2], "cd_par")
        self.ifb = sb("ifb", [4, 2])
        self.cs = sb("cs", [P, 2, NT])
        self.rot = sb("rot", [P, P])
        self.dmask, self.dms = sb("dmask", [P, 4, TP]), sb("dms", [NS, 4, NS])
        self.gq = sb("gq", [P, 2, NS])
        self.wS = sb("wS", [P, 3, 4])
        self.lmask, self.lms = sb("lmask", [P, TP]), sb("lms", [NS, NS])
        self.head_cols, self.head_rows = sb("head_cols", [P, 8, 8]), sb("head_rows", [8, 8, P])
        self.sel = sb("sel", [4, 4, P])
        self.selq = sb("selq", [4, 2, P])
        self.rows = sb("rows", [4, 2, NT])
        self.m0 = sb("m0", [4, 1 + NB])
        self.bm = sb("bm", [NS, NB])
        self.convT = sb("convT", [P, 4, NB, 3])
        self.n = len(self.loads)

    def load(self, c, eng):
        for t, src in self.loads:
            eng.dma_start(t[:], c.ins[src]).then_inc(self.loaded, 16)


def cd_mix_stage(c, z, vtok, ymix, params):
    nc = c.nc
    S = {n: c.sem(n + "_cm") for n in (
        "n_loaded", "rs_loaded", "c_loaded", "rot_sum", "rope_done", "qdec_done", "ext_pad", "conv_out", "conv_done", "silu_done",
        "gate_x", "gate_e", "gate_ln", "gate_arg", "gate_exp", "m_done", "s_sum", "s_out", "kt_sum", "kt_out", "y_sum", "y_out", "rp_sum", "rp_out",
        "vb_done", "rn_sum", "rn_out", "e_sum", "e_exp", "qk_sum", "a_done", "emj_sum", "emj_out", "sq_sum", "qsc_done", "car_sum", "car_out",
        "wt_sum", "wt_out", "kd_sum", "kd_out", "num_sum", "h_done", "cp_sum", "cp_out", "kb_done", "cn_sum", "cn_out", "n_sum", "n_out",
        "mean_sum", "yc_done", "yc_sq", "var_sum", "var_sd", "var_rows", "var_all", "var_used", "gates_done")}
    with ExitStack() as ctx:
        def sb(n, shape, dt=F32):
            return c.sb(n + "_cm", shape, dt, ctx=ctx)
        p_ = params
        par, ifb, cs, rot, dmask, dms, gq, wS, lmask, lms = p_.par, p_.ifb, p_.cs, p_.rot, p_.dmask, p_.dms, p_.gq, p_.wS, p_.lmask, p_.lms
        head_cols, head_rows, sel, selq, rows, m0, bm, convT = p_.head_cols, p_.head_rows, p_.sel, p_.selq, p_.rows, p_.m0, p_.bm, p_.convT
        gn, tap, g4 = par[:, 0:8], par[:, 8:28].rearrange("p (a i) -> p a i", i=5), par[:, 28:30]
        spare = c.ring[:, :].rearrange("p s a k m -> p (s a k m)")
        rs0 = spare[:, 0:2048].rearrange("p (b h e) -> p b h e", b=NB, h=2)
        c0t = spare[:, 2048:4096].rearrange("p (b h e) -> p b h e", b=NB, h=2)
        c0 = spare[:, 4096:6144].rearrange("p (b h d) -> p b h d", b=NB, h=4)
        ext = spare[:, 6144:6144 + 4 * 315].rearrange("p (a n) -> p a n", a=4)
        spare2 = c.down[:, :].rearrange("p s k m -> p (s k m)")
        scT = spare2[:, 0:8 * ST_COLS].rearrange("p (h n) -> p h n", h=8)
        E = spare2[:, 8 * ST_COLS:12 * ST_COLS].rearrange("p (h n) -> p h n", h=4)
        n0 = spare2[0:NB, 5376:5632]
        n0t = sb("n0t", [P, NB, 2])
        tmp = sb("tmp", [P, 2, NT])
        qdec, qsc, qn = sb("qdec", [P, 2, NS]), sb("qsc", [P, 2, NS]), sb("qn", [P, 2, NS])
        cacc = sb("cacc", [P, 4, NT])
        qk = sb("qk", [P, 4, NT])
        clast = sb("clast", [P, 4, 3 * (1 + NB)])
        g = sb("g", [4, 9, NT])
        gx, gn_, ge, gb, gu, gM, gsc, gem, gws = (g[:, j] for j in range(9))
        negM = sb("negM", [4, NT])
        car, mnew = sb("car", [4, NB]), sb("mnew", [4, 1 + NB])
        scs = sb("scs", [NS, 8, NS])
        Es = sb("Es", [NS, 4, NS])
        kw, kws = sb("kw", [P, 3, 256]), sb("kws", [P, 3, 256])
        wt = sb("wt", [P, 3, 4])
        emj = sb("emj", [P, 4, NT])
        carp = sb("carp", [P, 4, NB])
        carb = sb("carb", [NB, 4])
        VB = sb("VB", [NS, 2, NB, P])
        KB = sb("KB", [NS, 4, NB, 64])
        hN = c.xscratch
        hd, hr = sb("hd", [P, NT]), sb("hr", [P, NT])
        yc, ysq = c.xscratch2, sb("ysq", [P, 8, NT])
        rows8 = hd[0:8, :]
        rsp = spare2[:, 4608:4864].rearrange("p (h e) -> p h e", h=2)
        csp = spare2[:, 4864:5120].rearrange("p (h d) -> p h d", h=4)
        nsp = spare2[0:1, 5120:5376]
        block = ctx.enter_context(nc.Block())
        B = c.banks
        vc, vd = vtok[:, 0:3], vtok[:, 3:6]
        Q, K, GC, OG = z[:, 0:2], z[:, 2:4], z[:, 4:8], z[:, 12:16]

        def half(u):
            return slice(u * 64, u * 64 + 64)

        def sel_row(h):
            return sel[:, h, 0:1].to_broadcast([4, TP])

        def seqs_(ap):
            return ap.rearrange("p (b t) -> p b t", t=TS)

        def seqs(ap):
            return ap[..., TP:NT].rearrange("p (b t) -> p b t", t=TS)

        @block.sync
        def _(sp):
            for dst, src in ((n0[:, :], "n0"), (n0t[:, :, :], "n0t")):
                sp.dma_start(dst, c.ins[src]).then_inc(S["n_loaded"], 16)
            sp.dma_start(rs0, c.ins["rs0"]).then_inc(S["rs_loaded"], 16)
            sp.dma_start(c0t, c.ins["c0t"]).then_inc(S["c_loaded"], 16)
            sp.dma_start(c0, c.ins["c0"]).then_inc(S["c_loaded"], 16)
            sp.wait_ge(S["conv_out"], 2)
            c.store(sp, c.outs["conv"], clast[:, :, :])
            sp.wait_ge(S["gate_arg"], 1)
            c.store(sp, c.outs["m"], mnew[:, :])
            sp.wait_ge(S["rp_out"], 1)
            c.store(sp, c.outs["ret_p"], rsp[:, :, :])
            sp.wait_ge(S["rn_out"], 4)
            c.store(sp, c.outs["ret_s"], rs0)
            sp.wait_ge(S["cp_out"], 1)
            c.store(sp, c.outs["C_p"], csp[:, :, :])
            sp.wait_ge(S["cn_out"], 4)
            c.store(sp, c.outs["C_s"], c0)
            sp.wait_ge(S["n_out"], 2)
            c.store(sp, c.outs["n_p"], nsp[:, :])
            c.store(sp, c.outs["n_s"], n0[:, :])
            stores_done(c, sp)

        @block.gpsimd
        def _(pool):
            pool.memset(ext[:, :, 0:3], 0.0).then_inc(S["ext_pad"], 1)

        @block.vector
        def _(dve):
            def ln(ins):
                c.link(dve, "dve", ins)
            dve.wait_ge(params.loaded, 16 * params.n)
            ln(dve.tensor_scalar(gx, z[0:4, 17], ifb[:, 1:2], None, ALU.add))
            ln(dve.tensor_scalar(gn_, gx, -1.0, None, ALU.mult))
            dve.tensor_tensor(ge, gx, gn_, ALU.min).then_inc(S["gate_x"], 1)
            dve.tensor_scalar(gx, gx, 0.0, None, ALU.min)
            dve.tensor_scalar(gu, z[0:4, 16], ifb[:, 0:1], None, ALU.add)
            for i in range(4):
                dve.wait_ge(S["rot_sum"], i + 1)
                dve.tensor_tensor(tmp[:, 0], z[:, i], cs[:, 0], ALU.mult)
                ln(dve.tensor_tensor(tmp[:, 1], B[i][:, 0:NT], cs[:, 1], ALU.mult))
                dve.tensor_tensor(z[:, i], tmp[:, 0], tmp[:, 1], ALU.add).then_inc(S["rope_done"], 1)
                dve.wait_ge(S["rope_done"], i + 1)
            dve.tensor_tensor(qdec[:, :, :], Q[:, :, TP:NT], gq[:, :, :], ALU.mult).then_inc(S["qdec_done"], 1)
            dve.wait_ge(S["gate_ln"], 1)
            ln(dve.tensor_tensor(gx, gx, ge, ALU.subtract))
            ln(dve.tensor_tensor_scan(gb, rows[:, 0], gx, 0.0, ALU.mult, ALU.add))
            ln(dve.tensor_tensor(gu, gu, gb, ALU.subtract))
            ln(dve.tensor_copy(gn_, gu))
            dve.tensor_scalar(gn_[:, 0:1], gu[:, 0:1], 0.0, None, ALU.max)
            ln(dve.tensor_tensor(gn_[:, TP:NT:TS], gu[:, TP:NT:TS], m0[:, 1:], ALU.max))
            ln(dve.tensor_tensor_scan(gM, rows[:, 1], gn_, 0.0, ALU.add, ALU.max))
            dve.tensor_scalar(negM[:, :], gM, -1.0, None, ALU.mult)
            dve.tensor_tensor(seqs(gsc), m0[:, 1:].rearrange("p (b a) -> p b a", a=1).to_broadcast([4, NB, TS]), seqs(gM), ALU.subtract)
            ln(dve.tensor_tensor(gem, gb, gM, ALU.add))
            dve.tensor_scalar(gws[:, 0:TP], gu[:, 0:TP], gM[:, TP - 1:TP], None, ALU.subtract)
            dve.tensor_tensor(seqs(gws), seqs(gu), gM[:, SEQ::TS].rearrange("p (b a) -> p b a", a=1).to_broadcast([4, NB, TS]), ALU.subtract)
            dve.tensor_tensor(car[:, :], m0[:, 1:], gM[:, SEQ::TS], ALU.subtract)
            dve.tensor_copy(mnew[:, 0:1], gem[:, TP - 1:TP])
            dve.tensor_copy(mnew[:, 1:], gem[:, SEQ::TS]).then_inc(S["gate_arg"], 1)
            for h in range(4):
                dve.wait_ge(S["s_sum"], h + 1)
                dve.tensor_tensor(scT[:, h, 0:TP], B[h][:, 0:TP], dmask[:, h], ALU.mult)
                dve.tensor_tensor(scT[:, h, TP:ST_COLS], B[h][:, TP:ST_COLS], dmask[:, h, 0:P], ALU.mult)
                dve.tensor_tensor(scs[:, h], B[h][0:NS, ST_COLS:ST_COLS + NS], dms[:, h], ALU.mult).then_inc(S["s_out"], 1)
            dve.wait_ge(S["kt_sum"], 1)
            for i, (t0, n) in enumerate(TOK):
                last = dve.tensor_tensor(kw[0:n, i].rearrange("p (h d) -> p h d", h=4),
                                         B[4 + i // 2][0:n, (i % 2) * 256:(i % 2) * 256 + 256].rearrange("p (h d) -> p h d", h=4),
                                         wS[0:n, i].rearrange("p (h a) -> p h a", a=1).to_broadcast([n, 4, 64]), ALU.mult)
            last.then_inc(S["kt_out"], 1)
            dve.wait_ge(S["ext_pad"], 1)
            es = ext[:, :, EXT:].rearrange("p a (b t) -> p a b t", t=7)
            dve.tensor_copy(ext[:, :, 3:EXT], z[:, 8:12, 0:TP])
            for a in range(4):
                dve.tensor_copy(es[:, a, :, 0:3], convT[:, a])
                last = dve.tensor_copy(es[:, a, :, 3:7], seqs(z[:, 8 + a]))
            ln(last)
            dve.tensor_copy(clast[:, :, 0:3], ext[:, :, TP:EXT]).then_inc(S["conv_out"], 1)
            for a in range(4):
                last = dve.tensor_copy(clast[:, a, 3:].rearrange("p (b t) -> p b t", t=3), es[:, a, :, 4:7])
            last.then_inc(S["conv_out"], 1)
            for i in range(4):
                for a in range(4):
                    for dst, src in ((cacc[:, a, 0:TP], ext[:, a, 3 - i:3 - i + TP]), (seqs(cacc[:, a]), es[:, a, :, 3 - i:7 - i])):
                        if i == 0:
                            last = dve.tensor_scalar(dst, src, tap[:, a, 3:4], tap[:, a, 4:5], ALU.mult, ALU.add)
                        else:
                            last = dve.scalar_tensor_tensor(dst, src, tap[:, a, 3 - i:4 - i], dst, ALU.mult, ALU.add)
                if i < 3:
                    ln(last)
            last.then_inc(S["conv_done"], 1)
            for hp in range(2):
                if hp:
                    dve.wait_ge(S["rn_sum"], 1)
                for p_ in range(2):
                    h = 2 * hp + p_
                    last = dve.tensor_tensor(VB[:, p_], vc[0:NS, 2, h * P:h * P + P].rearrange("p (a e) -> p a e", a=1).to_broadcast([NS, NB, P]),
                                             bm[:, :].rearrange("p (b a) -> p b a", a=1).to_broadcast([NS, NB, P]), ALU.mult)
                last.then_inc(S["vb_done"], 1)
                dve.wait_ge(S["rn_sum"], hp + 1)
                for m in range(2):
                    dve.scalar_tensor_tensor(rs0[:, 4 * m:4 * m + 4, hp], rs0[:, 4 * m:4 * m + 4, hp], g4[:, hp:hp + 1],
                                             B[6 + m][:, :].rearrange("p (b e) -> p b e", b=4), ALU.mult, ALU.add).then_inc(S["rn_out"], 1)
            for h in range(4):
                dve.wait_ge(S["e_exp"], h + 1)
                dve.wait_ge(S["qk_sum"], h + 1)
                bk = B[4 + h % 2]
                dve.scalar_tensor_tensor(scT[:, 4 + h], bk[:, 0:ST_COLS], 0.125, E[:, h], ALU.mult, ALU.mult)
                dve.scalar_tensor_tensor(scs[:, 4 + h], bk[0:NS, ST_COLS:ST_COLS + NS], 0.125, Es[:, h], ALU.mult, ALU.mult).then_inc(S["a_done"], 1)
            dve.wait_ge(S["sq_sum"], 1)
            ln(dve.tensor_tensor(qsc[:, :, :], qk[:, 0:2, TP:NT], B[6][:, 0:2 * NS].rearrange("p (h n) -> p h n", h=2), ALU.mult))
            dve.wait_ge(S["n_loaded"], 32)
            for hp in range(2):
                last = dve.tensor_tensor(seqs_(qn[:, hp]), seqs_(qsc[:, hp]), n0t[:, :, hp:hp + 1].to_broadcast([P, NB, TS]), ALU.mult)
            last.then_inc(S["qsc_done"], 1)
            dve.wait_ge(S["wt_sum"], 1)
            ln(dve.tensor_scalar(wt[:, 0:2], B[7][:, 0:8].rearrange("p (i h) -> p i h", i=2), 0.125, None, ALU.mult))
            ln(dve.tensor_scalar(wt[0:NS, 2], B[7][0:NS, 8:12], 0.125, None, ALU.mult))
            dve.wait_ge(S["kd_sum"], 1)
            for i, (t0, n) in enumerate(TOK):
                last = dve.tensor_tensor(kws[0:n, i].rearrange("p (h d) -> p h d", h=4),
                                         B[4 + i // 2][0:n, (i % 2) * 256:(i % 2) * 256 + 256].rearrange("p (h d) -> p h d", h=4),
                                         wt[0:n, i].rearrange("p (h a) -> p h a", a=1).to_broadcast([n, 4, 64]), ALU.mult)
            last.then_inc(S["kd_out"], 1)
            for h in range(4):
                dve.wait_ge(S["num_sum"], h + 1)
                dve.wait_ge(S["emj_out"], 4)
                bn = 2 * (h % 2)
                ln(dve.scalar_tensor_tensor(hd[:, :], B[bn + 1][:, 0:NT], -1.0, emj[:, h], ALU.mult, ALU.max))
                ln(dve.tensor_tensor(hd[:, :], B[bn + 1][:, 0:NT], hd[:, :], ALU.max))
                ln(dve.reciprocal(hr[:, :], hd[:, :]))
                dve.tensor_tensor(hN[:, 4 + h], B[bn][:, 0:NT], hr[:, :], ALU.mult).then_inc(S["h_done"], 1)
            dve.wait_ge(S["kd_out"], 1)
            for h in range(4):
                last = dve.tensor_tensor(KB[:, h], kws[0:NS, 2, h * 64:h * 64 + 64].rearrange("p (a d) -> p a d", a=1).to_broadcast([NS, NB, 64]),
                                         bm[:, :].rearrange("p (b a) -> p b a", a=1).to_broadcast([NS, NB, 64]), ALU.mult)
                last.then_inc(S["kb_done"], 1)
            for h in range(4):
                dve.wait_ge(S["car_out"], 1)
                ln(dve.tensor_tensor(c0[:, :, h], c0[:, :, h], carp[:, h].rearrange("p (b a) -> p b a", a=1).to_broadcast([P, NB, 64]), ALU.mult))
                dve.wait_ge(S["cn_sum"], h + 1)
                dve.tensor_tensor(c0[:, :, h], c0[:, :, h], B[4 + h % 2][:, :].rearrange("p (b d) -> p b d", b=NB), ALU.add).then_inc(S["cn_out"], 1)
            ln(dve.tensor_tensor(n0[:, :].rearrange("p (h d) -> p h d", h=4), n0[:, :].rearrange("p (h d) -> p h d", h=4),
                                 carb[:, :].rearrange("p (h a) -> p h a", a=1).to_broadcast([NB, 4, 64]), ALU.mult))
            dve.wait_ge(S["n_sum"], 1)
            dve.tensor_tensor(n0[:, :], n0[:, :], B[7][0:NB, 0:256], ALU.add).then_inc(S["n_out"], 1)
            for h in range(8):
                dve.wait_ge(S["mean_sum"], h + 1)
                dve.scalar_tensor_tensor(yc[:, h], B[h % 4][:, 0:NT], -1.0 / P, hN[:, h], ALU.mult, ALU.add).then_inc(S["yc_done"], 1)
            dve.wait_ge(S["var_sd"], 1)
            dve.reciprocal(rows8, rows8).then_inc(S["var_rows"], 1)
            for h in range(8):
                dve.wait_ge(S["var_all"], h + 1)
                dve.scalar_tensor_tensor(yc[:, h], yc[:, h], gn[:, h:h + 1], B[4 + h % 4][:, 0:NT], ALU.mult, ALU.mult).then_inc(S["var_used"], 1)
                dve.wait_ge(S["var_used"], h + 1)
                if h == 0:
                    dve.wait_ge(S["gates_done"], 8)
                last = dve.tensor_tensor(ymix[:, h], yc[:, h], ymix[:, h], ALU.mult)
            ln(last)


        @block.scalar
        def _(act):
            act.wait_ge(S["gate_x"], 1)
            c.link(act, "act", act.activation(ge, ge, ACT.Exp))
            act.activation(ge, ge, ACT.Ln, bias=c.ones[0:4, 0:1]).then_inc(S["gate_ln"], 1)
            act.wait_ge(S["gate_arg"], 1)
            act.activation(gsc[:, TP:NT], gsc[:, TP:NT], ACT.Exp)
            act.activation(gws, gws, ACT.Exp)
            act.activation(car[:, :], car[:, :], ACT.Exp).then_inc(S["gate_exp"], 1)
            for h in range(4):
                act.wait_ge(S["e_sum"], h + 1)
                act.activation(E[:, h], B[6 + h % 2][:, 0:ST_COLS], ACT.Exp)
                act.activation(Es[:, h], B[6 + h % 2][0:NS, ST_COLS:ST_COLS + NS], ACT.Exp).then_inc(S["e_exp"], 1)
            for h in range(4):
                act.wait_ge(S["y_sum"], h + 1)
                act.activation(hN[:, h], B[h][:, 0:NT], ACT.Copy).then_inc(S["y_out"], 1)
            act.wait_ge(S["rp_sum"], 1)
            act.activation(rsp[:, :, :], B[4][:, 0:256].rearrange("p (h e) -> p h e", h=2), ACT.Copy).then_inc(S["rp_out"], 1)
            act.wait_ge(S["conv_done"], 1)
            for a in range(4):
                act.activation(qk[:, a], cacc[:, a], ACT.Silu).then_inc(S["silu_done"], 1)
            for h in range(4):
                act.activation(ymix[:, h], GC[:, h], ACT.Silu).then_inc(S["gates_done"], 1)
            for h in range(4):
                act.activation(ymix[:, 4 + h], OG[:, h], ACT.Sigmoid).then_inc(S["gates_done"], 1)
            for h in range(4):
                act.wait_ge(S["emj_sum"], h + 1)
                act.activation(emj[:, h], B[h][:, 0:NT], ACT.Exp, scale=-1.0).then_inc(S["emj_out"], 1)
            act.wait_ge(S["car_sum"], 1)
            act.activation(carp[:, :, :], B[5][:, 0:4 * NB].rearrange("p (h b) -> p h b", h=4), ACT.Copy)
            act.activation(carb[:, :], B[5][0:NB, 64:68], ACT.Copy).then_inc(S["car_out"], 1)
            act.wait_ge(S["cp_sum"], 1)
            act.activation(csp[:, :, :], B[6][:, 0:256].rearrange("p (h d) -> p h d", h=4), ACT.Copy).then_inc(S["cp_out"], 1)
            act.wait_ge(S["n_sum"], 1)
            act.wait_ge(S["n_out"], 1)
            act.activation(nsp[:, :], B[7][0:1, 256:512], ACT.Copy).then_inc(S["n_out"], 1)
            for h in range(8):
                act.wait_ge(S["yc_done"], h + 1)
                act.activation(ysq[:, h], yc[:, h], ACT.Square).then_inc(S["yc_sq"], 1)
            act.wait_ge(S["var_sum"], 1)
            act.activation(rows8, B[4][0:8, 0:NT], ACT.Sqrt, scale=1.0 / P, bias=c.eps[0:8, 2:3]).then_inc(S["var_sd"], 1)

        @block.tensor
        def _(pe):
            sg_ = dict(skip_group_check=True)
            pe.wait_ge(params.loaded, 16 * params.n)
            for i in range(4):
                pe.matmul(B[i][:, 0:NT], rot[:, :], z[:, i], start=True, stop=True).then_inc(S["rot_sum"], 1)
            for h in range(4):
                pe.wait_ge(S["rope_done"], 4)
                hf, hp = half(h % 2), h // 2
                pe.matmul(B[h][:, 0:TP], K[hf, hp, 0:P], Q[hf, hp, 0:TP], start=True, stop=True)
                pe.matmul(B[h][:, TP:ST_COLS], K[hf, hp, P:TP], Q[hf, hp, P:TP], start=True, stop=True)
                pe.matmul(B[h][0:NS, ST_COLS:ST_COLS + NS], K[hf, hp, TP:NT], Q[hf, hp, TP:NT], start=True, stop=True).then_inc(S["s_sum"], 1)
            for i, (t0, n) in enumerate(TOK):
                for hp in range(2):
                    o = (i % 2) * 256 + hp * P
                    mm = pe.transpose(B[4 + i // 2][0:n, o:o + P], K[:, hp, t0:t0 + n], c.ident[:, :])
            mm.then_inc(S["kt_sum"], 1)
            pe.wait_ge(S["gate_arg"], 1)
            for h in range(4):
                if h >= 2:
                    pe.wait_ge(S["e_exp"], h - 1)
                bk = B[6 + h % 2]
                for o, w, s0, j0 in ((0, TP, 0, 0), (TP, P, P, P)):
                    pe.matmul(bk[:, o:o + w], gu[:, s0:s0 + P], sel_row(h)[:, 0:w], start=True, stop=False)
                    pe.matmul(bk[:, o:o + w], sel[:, h], negM[:, j0:j0 + w], start=False, stop=False)
                    pe.matmul(bk[:, o:o + w], c.ident[:, :], lmask[:, 0:w], start=False, stop=True)
                o = ST_COLS
                pe.matmul(bk[0:NS, o:o + NS], gu[:, TP:NT], sel_row(h)[:, 0:NS], start=True, stop=False)
                pe.matmul(bk[0:NS, o:o + NS], sel[:, h, 0:NS], negM[:, TP:NT], start=False, stop=False)
                pe.matmul(bk[0:NS, o:o + NS], c.ident[0:NS, 0:NS], lms[:, :], start=False, stop=True).then_inc(S["e_sum"], 1)
            pe.wait_ge(S["qdec_done"], 1)
            pe.wait_ge(S["rs_loaded"], 16)
            for h in range(4):
                hf, hp = half(h % 2), h // 2
                pe.wait_ge(S["s_out"], h + 1)
                v_ = vc[:, :, h * P:h * P + P]
                pe.matmul(B[h][:, 0:TP], v_[:, 0], scT[:, h, 0:TP], start=True, stop=False, **sg_)
                pe.matmul(B[h][:, P:TP], v_[:, 1], scT[:, h, TP:ST_COLS], start=False, stop=True, **sg_)
                pe.matmul(B[h][:, TP:NT], v_[0:NS, 2], scs[:, h], start=False, stop=False, **sg_)
                for b in range(NB):
                    o = TP + b * TS
                    mm = pe.matmul(B[h][:, o:o + TS], rs0[hf, b, hp], qdec[hf, hp, b * TS:b * TS + TS], start=False, stop=True, **sg_)
                mm.then_inc(S["y_sum"], 1)
            pe.wait_ge(S["kt_out"], 1)
            for h in range(4):
                hf, hp = half(h % 2), h // 2
                for i in range(2):
                    mm = pe.matmul(B[4][hf, hp * P:hp * P + P], kw[:, i, h * 64:h * 64 + 64], vc[:, i, h * P:h * P + P], start=(i == 0), stop=(i == 1))
            mm.then_inc(S["rp_sum"], 1)
            pe.wait_ge(S["e_exp"], 4)
            for hp in range(2):
                pe.wait_ge(S["vb_done"], hp + 1)
                if hp:
                    pe.wait_ge(S["rn_out"], 2)
                for m in range(2):
                    for p_ in range(2):
                        h = 2 * hp + p_
                        mm = pe.matmul(B[6 + m][half(p_), :], kw[0:NS, 2, h * 64:h * 64 + 64],
                                       VB[:, p_, 4 * m:4 * m + 4].rearrange("p b e -> p (b e)"), start=True, stop=True)
                mm.then_inc(S["rn_sum"], 1)
            pe.wait_ge(S["silu_done"], 4)
            pe.wait_ge(S["rp_out"], 1)
            for h in range(4):
                hf, hp = half(h % 2), h // 2
                if h >= 2:
                    pe.wait_ge(S["a_done"], h - 1)
                bk = B[4 + h % 2]
                pe.matmul(bk[:, 0:TP], qk[hf, 2 + hp, 0:P], qk[hf, hp, 0:TP], start=True, stop=True)
                pe.matmul(bk[:, TP:ST_COLS], qk[hf, 2 + hp, P:TP], qk[hf, hp, P:TP], start=True, stop=True)
                pe.matmul(bk[0:NS, ST_COLS:ST_COLS + NS], qk[hf, 2 + hp, TP:NT], qk[hf, hp, TP:NT], start=True, stop=True).then_inc(S["qk_sum"], 1)
            pe.wait_ge(S["rn_out"], 4)
            pe.wait_ge(S["gate_exp"], 1)
            for hp in range(2):
                mm = pe.matmul(B[6][:, hp * NS:hp * NS + NS], selq[:, hp], gsc[:, TP:NT], start=True, stop=True)
            mm.then_inc(S["sq_sum"], 1)
            for i, (t0, n) in enumerate(TOK):
                mm = pe.matmul(B[7][0:n, 4 * i:4 * i + 4], gws[:, t0:t0 + n], c.ident[0:4, 0:4], start=True, stop=True)
            mm.then_inc(S["wt_sum"], 1)
            for h in range(4):
                pe.wait_ge(S["y_out"], h + 1)
                pe.matmul(B[h][:, 0:NT], sel[:, h], gem, start=True, stop=True).then_inc(S["emj_sum"], 1)
            pe.wait_ge(S["a_done"], 4)
            for i, (t0, n) in enumerate(TOK):
                for hp in range(2):
                    o = (i % 2) * 256 + hp * P
                    mm = pe.transpose(B[4 + i // 2][0:n, o:o + P], qk[:, 2 + hp, t0:t0 + n], c.ident[:, :])
            mm.then_inc(S["kd_sum"], 1)
            pe.wait_ge(S["qsc_done"], 1)
            pe.wait_ge(S["c_loaded"], 32)
            pe.wait_ge(S["emj_out"], 4)
            for h in range(4):
                hf, hp = half(h % 2), h // 2
                if h >= 2:
                    pe.wait_ge(S["h_done"], h - 1)
                v_ = vd[:, :, h * P:h * P + P]
                for bn, l0, l1, l2 in ((2 * (h % 2), v_[:, 0], v_[:, 1], v_[0:NS, 2]),
                                       (2 * (h % 2) + 1, c.ones[:, :], c.ones[:, :], c.ones[0:NS, :])):
                    pe.matmul(B[bn][:, 0:TP], l0, scT[:, 4 + h, 0:TP], start=True, stop=False, **sg_)
                    pe.matmul(B[bn][:, P:TP], l1, scT[:, 4 + h, TP:ST_COLS], start=False, stop=True, **sg_)
                    pe.matmul(B[bn][:, TP:NT], l2, scs[:, 4 + h], start=False, stop=False, **sg_)
                for b in range(NB):
                    o = TP + b * TS
                    pe.matmul(B[2 * (h % 2)][:, o:o + TS], c0t[hf, b, hp], qsc[hf, hp, b * TS:b * TS + TS], start=False, stop=True, **sg_)
                pe.matmul(B[2 * (h % 2) + 1][:, TP:NT], c.ones[hf, :], qn[hf, hp], start=False, stop=True, **sg_).then_inc(S["num_sum"], 1)
            pe.wait_ge(S["kd_out"], 1)
            for h in range(4):
                for i in range(2):
                    mm = pe.matmul(B[6][:, h * 64:h * 64 + 64], vd[:, i, h * P:h * P + P], kws[:, i, h * 64:h * 64 + 64], start=(i == 0), stop=(i == 1))
            mm.then_inc(S["cp_sum"], 1)
            pe.matmul(B[7][0:NB, 0:256], bm[:, :], kws[0:NS, 2], start=True, stop=True)
            for i in range(2):
                mm = pe.matmul(B[7][0:1, 256:512], c.ones[:, 0:1], kws[:, i], start=(i == 0), stop=(i == 1))
            mm.then_inc(S["n_sum"], 1)
            for h in range(4):
                mm = pe.matmul(B[5][:, h * NB:h * NB + NB], sel[:, h], car[:, :], start=True, stop=True)
            mm = pe.matmul(B[5][0:NB, 64:68], car[:, :], c.ident[0:4, 0:4], start=True, stop=True)
            mm.then_inc(S["car_sum"], 1)
            for h in range(4):
                pe.wait_ge(S["kb_done"], h + 1)
                if h == 0:
                    pe.wait_ge(S["car_out"], 1)
                if h >= 2:
                    pe.wait_ge(S["cn_out"], h - 1)
                pe.matmul(B[4 + h % 2][:, :], vd[0:NS, 2, h * P:h * P + P], KB[:, h].rearrange("p b d -> p (b d)"), start=True, stop=True).then_inc(S["cn_sum"], 1)
            pe.wait_ge(S["h_done"], 4)
            for h in range(8):
                if h >= 4:
                    pe.wait_ge(S["yc_done"], h - 3)
                pe.matmul(B[h % 4][:, 0:NT], c.ones[:, :], hN[:, h], start=True, stop=True).then_inc(S["mean_sum"], 1)
            pe.wait_ge(S["cp_out"], 1)
            pe.wait_ge(S["n_out"], 2)
            pe.wait_ge(S["cn_out"], 4)
            for h in range(8):
                pe.wait_ge(S["yc_sq"], h + 1)
                mm = pe.matmul(B[4][0:8, 0:NT], head_cols[:, h], ysq[:, h], start=(h == 0), stop=(h == 7))
            mm.then_inc(S["var_sum"], 1)
            pe.wait_ge(S["var_rows"], 1)
            for h in range(8):
                if h >= 4:
                    pe.wait_ge(S["var_used"], h - 3)
                pe.matmul(B[4 + h % 4][:, 0:NT], head_rows[:, h], rows8, start=True, stop=True).then_inc(S["var_all"], 1)



def out_stage(c, name, ymix, ymix_lo, gain, next_gain, prefetch):
    nc = c.nc
    out_sum, y_done, y_squared, ysq_added = c.sem(f"out_sum_{name}"), c.y_done, c.y_squared, c.ysq_added
    y0, y1 = KT * c.tails, (KT - 1) * c.tails
    ymix_high, ymix_split = c.sem(f"ymix_high_{name}"), c.sem(f"ymix_split_{name}")
    first = c.pairs
    with ExitStack() as ctx:
        whi = c.whi
        y2 = c.sb(f"y2_{name}", [P, 2, NT], ctx=ctx)
        yg = c.sb(f"yg_{name}", [P, KT, NT], ctx=ctx)
        ysq = c.sb(f"ysq_{name}", [P, NT], ctx=ctx)
        tail = Tail(c, name, yg, ysq[:, :], y2[:, (KT - 1) % 2], 1.0, next_gain)
        ctx.enter_context(tail.scope)
        assert nc.sbuf_base <= c.below_whi
        block = ctx.enter_context(nc.Block())

        @block.sync
        def _(sp):
            send_pairs(c, sp, c.ins["w_" + name], 0, 4)
            prefetch(sp)

        @block.tensor
        def _(pe):
            for n in range(KT):
                s, b = (first + n // 2) % RING, (first + n // 2) % 2
                if n % 2 == 0:
                    pe.wait_ge(c.pair_split, first + n // 2 + 1)
                if n >= 2:
                    pe.wait_ge(y_done, y0 + n - 1)
                for k in range(KT):
                    if n == 0:
                        pe.wait_ge(ymix_split, k + 1)
                    mm = three_products(pe, c.banks[4 + n % 2][:, 0:NT], whi[:, b, n % 2, k], c.ring_lo[:, s, n % 2, k], c.xhi[:, k], ymix_lo[:, k],
                                        k == 0, k == KT - 1)
                mm.then_inc(*((c.pair_done, 1) if n % 2 else (out_sum, 1)))
            tail.pe(pe, ysq_added, y_squared, y0, c.banks[6])

        @block.scalar
        def _(act):
            for k in range(KT):
                act_mask(act, c.xhi[:, k], ymix[:, k]).then_inc(ymix_high, 1)
            tail.warm(act)
            for n in range(KT):
                if n % 2:
                    act.wait_ge(c.pair_done, first + n // 2 + 1)
                else:
                    act.wait_ge(out_sum, n // 2 + 1)
                if n >= 2:
                    act.wait_ge(ysq_added, y1 + n - 1)
                act.activation(y2[:, n % 2], c.banks[4 + n % 2][:, 0:NT], ACT.Square).then_inc(y_squared, 1)
                act.activation(yg[:, n], c.banks[4 + n % 2][:, 0:NT], ACT.Copy, scale=c.gains[:, gain, n:n + 1]).then_inc(y_done, 1)
            tail.act(act, c.banks[6])

        @block.vector
        def _(dve):
            for k in range(KT):
                dve.wait_ge(ymix_high, k + 1)
                low_bits(dve, ymix_lo[:, k], ymix[:, k], c.xhi[:, k]).then_inc(ymix_split, 1)
            split_pair(c, dve, whi, first, 0)
            split_pair(c, dve, whi, first, 1)
            for u in range(2, 4):
                dve.wait_ge(c.pair_done, first + u - 1)
                split_pair(c, dve, whi, first, u)
            dve.wait_ge(c.pair_done, first + 4)
            first_pairs_early(c, dve, first + 4, 1)
            dve.wait_ge(y_done, y0 + KT)
            tail.dve(dve)

        @block.gpsimd
        def _(pool):
            pool.wait_ge(y_squared, y0 + 1)
            pool.tensor_copy(ysq[:, :], y2[:, 0]).then_inc(ysq_added, 1)
            for n in range(1, KT - 1):
                pool.wait_ge(ysq_added, y1 + n)
                pool.wait_ge(y_squared, y0 + n + 1)
                pool.tensor_tensor(ysq[:, :], ysq[:, :], y2[:, n % 2], ALU.add).then_inc(ysq_added, 1)
            tail.pool(pool)

    c.pairs += 4


def program(nc, ins, outs):
    with ExitStack() as ctx:
        c = Chip(nc, ctx, ins, outs)

        def ffn_prefetch(f):
            def prefetch(sp):
                send_pairs(c, sp, c.ins["w_gu"][f], 0, RING)
                send_downs(c, sp, c.ins["w_down"][f], 0, DSLOTS)
            return prefetch

        def pair_prefetch(name):
            return lambda sp: send_pairs(c, sp, c.ins[name], 0, RING)

        start_stage(c, 0, ffn_prefetch(0))
        ffn_stage(c, 0, 2, pair_prefetch("w_ab"))
        with ExitStack() as mixer:
            z = c.sb("z", [P, 32, NT], ctx=mixer)
            vtok = c.sb("vtok", [P, 3, 512], ctx=mixer)
            ymix, ymix_lo = c.two_types("ymix", [P, KT, NT], mixer)
            with ExitStack() as attention:
                idx = IndexKeys(c, attention)
                ab_in_stage(c, z, vtok, idx)
                dsa_stage(c, z, vtok, ymix, idx)
            rwkv_stage(c, z, vtok, ymix)
            c.end_stage()
            out_stage(c, "ab_out", ymix, ymix_lo, 3, 4, ffn_prefetch(1))
        ffn_stage(c, 1, 6, ffn_prefetch(2))
        ffn_stage(c, 2, 8, pair_prefetch("w_cd"))
        with ExitStack() as mixer:
            z = c.sb("z2", [P, 18, NT], ctx=mixer)
            vtok = c.sb("vtok2", [P, 6, 512], ctx=mixer)
            ymix, ymix_lo = c.two_types("ymix2", [P, KT, NT], mixer)
            with ExitStack() as mix:
                params = CdParams(c, mix)
                cd_in_stage(c, z, vtok, params)
                cd_mix_stage(c, z, vtok, ymix, params)
            out_stage(c, "cd_out", ymix, ymix_lo, 9, 10, ffn_prefetch(3))
        ffn_stage(c, 3, None, lambda sp: None)


def columns(w):
    n = w.shape[1] // P
    return w.reshape(KT, P, n, P).transpose(2, 1, 0, 3).reshape(n, P, KT * P)


def pairs(blocks):
    n = blocks.shape[0] // 2
    return blocks.reshape(n, 2, P, -1).transpose(0, 2, 1, 3).reshape(n, P, -1)


def feature_major(a):
    return np.ascontiguousarray(a.reshape(a.shape[0], -1, P).transpose(2, 1, 0))


def half_major(a, n):
    return a.reshape(n, P).T


def lay_out_rwkv(m, i):
    b0 = 3 * 512 + 1024 + 64 + 16
    w = i["ab_w_in"][0]
    q, k, v, qi, ki, wi, zb = np.split(w, [512, 1024, 1536, 2560, 2624, 2640], axis=1)
    cols = np.concatenate([q, k, qi, zb, ki, ki, wi, np.zeros((D_MODEL, 112), np.float32)], 1)
    wv = v.reshape(KT, P, 2048 // 4).transpose(1, 0, 2).reshape(P, 2, 2048).transpose(1, 0, 2)
    m["w_ab"] = np.concatenate([pairs(columns(cols)), wv])
    m["rk_par"] = np.ascontiguousarray(np.concatenate([half_major(i["rwkv_mu"][0], 14)] + [
        half_major(i[n][0].reshape(512), HP) for n in ("rwkv_w0", "rwkv_a0", "rwkv_kk", "rwkv_ka", "rwkv_rk", "rwkv_lnx_g", "rwkv_lnx_b")], 1))
    m["wa2"] = np.concatenate([i["rwkv_w2"][0], i["rwkv_a2"][0]])
    m["g2"] = i["rwkv_g2"][0]
    m["shiftT"] = feature_major(i["state_shift"][0])
    s = i["state_rwkv"][0].reshape(NB, HP, 2, L, L)
    m["s0t"] = np.ascontiguousarray(s.transpose(2, 4, 0, 1, 3).reshape(P, NB, HP, L))
    seg = np.ones(NT, np.float32)
    seg[0:TP:L] = 0
    seg[TP::TS] = 0
    m["seg"] = np.tile(seg, (P, 1))
    s_, t = np.arange(L)[:, None], np.arange(L)[None]
    same = (s_ < NS) & (t < NS) & (s_ // TS == t // TS)
    g = [np.concatenate([(s_ < t) & x, (s_ <= t) & x], 1) for x in (np.ones((L, L), bool), same)]
    m["gmask"] = np.tile(np.stack(g, 1), (2, 1, 1)).astype(np.float32)
    m["amask"] = np.tile(np.stack([(t < s_), (t < s_) & same], 1), (2, 1, 1)).astype(np.float32)
    m["bmask"] = np.tile((s_ < NS) & (s_ // TS == np.arange(NB)[None]), (2, 1)).astype(np.float32)
    m["id2"] = np.tile(np.eye(L, dtype=np.float32), (2, 1))


def lay_out_dsa(m, i):
    m["table"] = i["page_table"].reshape(1, NB * NPG)
    kc = i["cache_k"][0].reshape(-1, P, HP, P)
    m["cache_k"] = np.ascontiguousarray(kc.transpose(0, 3, 2, 1).reshape(-1, P, 512))
    m["cache_v"] = i["cache_v"][0].reshape(-1, P, 512)
    m["cache_i"] = np.ascontiguousarray(np.tile(i["cache_kidx"][0].transpose(0, 2, 1), (1, 2, 1)))
    m["kidg"] = np.tile(i["kidx_g"][0].reshape(64, 1), (2, 1))
    t, s = np.arange(TP)[:, None], np.arange(TP)[None]
    m["cmask"] = np.ascontiguousarray(np.where(s <= t, 0, NEG).astype(np.float32).reshape(2, P, TP).transpose(1, 0, 2))
    t, s = np.arange(NS)[:, None], np.arange(NS)[None]
    m["nmask"] = np.where((s <= t) & (s // TS == t // TS), 0, NEG).astype(np.float32)
    row = np.arange(P)
    b2, par, hp, tt = row // 64, row // 32 % 2, row // 4 % 8, row % 4
    m["esel"] = (np.arange(16)[:, None] == 2 * hp + par).astype(np.float32)
    col = np.arange(NS)
    m["wmask"] = np.stack([(col[None] == ((2 * g + b2) * TS + tt)[:, None]) / 32 for g in range(4)], 1).astype(np.float32)
    m["bsel"] = np.stack([(col[:, None] == ((4 * g + row // 32) * TS + row % 4)[None]) for g in range(2)], 1).astype(np.float32)


def lay_out_cd(m, i):
    w = i["cd_w_in"][0]
    qc, kc, vc, gc, qkd, vd, ig, fg, og = np.split(w, np.cumsum([256, 256, 512, 512, 512, 512, 4, 4]), axis=1)
    pad = np.zeros((D_MODEL, P - 4), np.float32)

    def values(v):
        return v.reshape(KT, P, 512).transpose(1, 0, 2).reshape(P, 2, 2048).transpose(1, 0, 2)
    m["w_cd"] = np.concatenate([pairs(columns(np.concatenate([qc, kc, gc, qkd, og], 1))), values(vc), values(vd),
                                pairs(columns(np.concatenate([ig, pad, fg, pad], 1)))])
    m["w_ab_out"] = pairs(columns(i["ab_w_out"][0]))
    m["w_cd_out"] = pairs(columns(i["cd_w_out"][0]))
    gamma = 1.0 - np.exp2(-5.0 - np.arange(4))
    lg = np.log1p(-np.exp2(-5.0 - np.arange(4, dtype=np.float64)))
    par, hrow = np.arange(P) // 64, np.arange(4)
    g4 = np.exp(TS * lg[2 * np.arange(2)[None] + par[:, None]]).astype(np.float32)
    taps = np.concatenate([i["conv_w"][0].reshape(4, 4, P).transpose(2, 1, 0), i["conv_b"][0].reshape(4, P).T[:, :, None]], 2)
    m["cd_par"] = np.ascontiguousarray(np.concatenate([i["ret_gn"][0].T, i["mlstm_gn"][0].T, taps.reshape(P, 20), g4], 1))
    m["ifb"] = np.ascontiguousarray(i["mlstm_if_b"][0].T)
    pos = np.concatenate([np.arange(TP), np.tile(PAST + np.arange(TS), NB)]).astype(np.float32)
    inv = (np.float32(10000.0) ** (-np.arange(32, dtype=np.float32) / np.float32(32))).astype(np.float32)
    ang = (pos[None] * inv[np.arange(P) % 32][:, None]).astype(np.float32).astype(np.float64)
    m["cs"] = np.stack([np.cos(ang), np.sin(ang)], 1).astype(np.float32)
    r = np.zeros((P, P), np.float32)
    for o in range(P):
        r[o + 32 if o % 64 < 32 else o - 32, o] = -1 if o % 64 < 32 else 1
    m["rot"] = r
    s, j = np.arange(P)[:, None, None], np.arange(TP)[None, None]
    m["dmask"] = np.where(j >= s, np.exp(np.maximum(j - s, 0) * lg[None, :, None]) / 8, 0).astype(np.float32)
    s, j = np.arange(NS)[:, None, None], np.arange(NS)[None, None]
    m["dms"] = np.where((j >= s) & (j // TS == s // TS), np.exp(np.maximum(j - s, 0) * lg[None, :, None]) / 8, 0).astype(np.float32)
    m["gq"] = np.exp((np.arange(NS) % TS + 1)[None, None] * lg[2 * np.arange(2)[None] + par[:, None]][:, :, None]).astype(np.float32)
    last = np.concatenate([TP - 1 - np.arange(TP), np.tile(TS - 1 - np.arange(TS), P // TS)]).reshape(3, P).T
    m["wS"] = (np.exp(last[:, :, None] * lg[None, None]) / 8).astype(np.float32)
    s, j = np.arange(P)[:, None], np.arange(TP)[None]
    m["lmask"] = np.where(j >= s, 0, NEG).astype(np.float32)
    s, j = np.arange(NS)[:, None], np.arange(NS)[None]
    m["lms"] = np.where((j >= s) & (j // TS == s // TS), 0, NEG).astype(np.float32)
    m["sel"] = np.tile(np.eye(4, dtype=np.float32)[:, :, None], (1, 1, P))
    m["selq"] = (hrow[:, None, None] == (2 * np.arange(2)[:, None] + par[None])[None]).astype(np.float32)
    seg = np.ones(NT, np.float32)
    seg[0] = 0
    seg[TP::TS] = 0
    m["rows"] = np.tile(np.stack([seg, np.where(seg == 0, NEG, 0).astype(np.float32)]), (4, 1, 1)).astype(np.float32)
    m["m0"] = np.concatenate([np.zeros((4, 1), np.float32), i["state_mlstm_m"][0].T], 1)
    m["bm"] = (np.arange(NS)[:, None] // TS == np.arange(NB)[None]).astype(np.float32)
    m["convT"] = np.ascontiguousarray(i["state_conv"][0].reshape(NB, 3, 4, P).transpose(3, 2, 0, 1))
    m["n0"] = i["state_mlstm_n"][0].reshape(NB, 256)
    m["n0t"] = np.ascontiguousarray(i["state_mlstm_n"][0].reshape(NB, 2, P).transpose(2, 0, 1))
    m["rs0"] = np.ascontiguousarray(i["state_ret"][0].reshape(NB, 2, P, P).transpose(2, 0, 1, 3))
    C = i["state_mlstm_C"][0]
    m["c0"] = np.ascontiguousarray(C.transpose(2, 0, 1, 3))
    m["c0t"] = np.ascontiguousarray(C.reshape(NB, 2, 2, P, 64).transpose(2, 4, 0, 1, 3).reshape(P, NB, 2, P))


def lay_out(i):
    m = {}
    x = np.concatenate([i["x_prompt"].reshape(TP, D_MODEL), i["x_sample"].reshape(NS, D_MODEL)])
    m["x"] = feature_major(x)
    m["gains"] = np.ascontiguousarray(i["norm_g"].reshape(12, KT, P).transpose(2, 0, 1))
    m["ident"] = np.eye(P, dtype=np.float32)
    m["ones"] = np.ones((P, P), np.float32)
    m["half_ones"] = np.kron(np.eye(2, dtype=np.float32), np.ones((64, 64), np.float32))
    q = np.arange(P) // 64
    pair = (np.arange(8)[:, None, None] == 2 * np.arange(4)[:, None] + q[None]).astype(np.float32)
    m["pair_rows"], m["pair_cols"] = pair, np.ascontiguousarray(pair.transpose(2, 1, 0))
    m["head_rows"] = np.tile(np.eye(8, dtype=np.float32)[:, :, None], (1, 1, P))
    m["head_cols"] = np.tile(np.eye(8, dtype=np.float32)[None], (P, 1, 1))
    m["eps"] = np.tile(np.array([EPS, 4 * EPS, 1e-5, 64e-5], np.float32), (P, 1))
    wg, wu, wd = (i[k].reshape((4,) + i[k].shape[2:]) for k in ("ffn_wg", "ffn_wu", "ffn_wd"))
    m["w_gu"] = np.stack([np.stack([columns(wg[f]), columns(wu[f])], 2).reshape(FT, P, 2 * KT * P) for f in range(4)])
    m["w_down"] = np.stack([wd[f].reshape(FT, P, KT, P).transpose(2, 1, 0, 3).reshape(KT, P, 2, DK * P)
                            .transpose(0, 2, 1, 3).reshape(2 * KT, P, DK * P) for f in range(4)])
    lay_out_rwkv(m, i)
    lay_out_dsa(m, i)
    lay_out_cd(m, i)
    return m


OUT_SHAPES = {"y": (P, KT, NT), "k": (P, 4, NT), "v_p": (P, 2, 512), "v_s": (NS, 512), "kidx": (64, NT), "shift": (P, 14, 1 + NB),
              "rwkv_p": (P, 4, 64), "rwkv_s": (P, NB, 4, 64), "ret_p": (P, 2, P), "ret_s": (P, NB, 2, P), "C_p": (P, 4, 64),
              "C_s": (P, NB, 4, 64), "n_p": (1, 256), "n_s": (NB, 256), "m": (4, 1 + NB), "conv": (P, 4, 3 * (1 + NB))}


def unpack(r):
    def token_major(a):
        return a.transpose(2, 1, 0).reshape(a.shape[2], -1)
    y, k, kidx = token_major(r["y"]), token_major(r["k"]), r["kidx"].T
    shift = token_major(r["shift"])
    v_p = r["v_p"].transpose(1, 0, 2)
    conv = r["conv"].transpose(2, 1, 0).reshape(1 + NB, 3, 512)
    m = r["m"].T
    prompt = (k[:TP].reshape(1, 1, TP, 8, 64), v_p.reshape(1, 1, TP, 8, 64), kidx[:TP].reshape(1, 1, TP, 64),
              r["rwkv_p"].reshape(2, 64, 4, 64).transpose(2, 0, 3, 1).reshape(1, 1, 8, 64, 64), shift[:1][None],
              r["ret_p"].reshape(2, 64, 2, P).transpose(2, 0, 1, 3).reshape(1, 1, 4, 64, P), r["C_p"].transpose(1, 0, 2)[None, None],
              r["n_p"].reshape(1, 1, 4, 64), m[:1][None], conv[:1][None])
    sample = (k[TP:].reshape(1, NB, TS, 8, 64), r["v_s"].reshape(1, NB, TS, 8, 64), kidx[TP:].reshape(1, NB, TS, 64),
              r["rwkv_s"].reshape(2, 64, NB, 4, 64).transpose(2, 3, 0, 4, 1).reshape(1, NB, 8, 64, 64), shift[1:][None],
              r["ret_s"].reshape(2, 64, NB, 2, P).transpose(2, 3, 0, 1, 4).reshape(1, NB, 4, 64, P),
              r["C_s"].transpose(1, 2, 0, 3)[None], r["n_s"].reshape(1, NB, 4, 64), m[1:][None], conv[1:][None])
    out = (y[:TP].reshape(1, TP, D_MODEL), y[TP:].reshape(NB, TS, D_MODEL)) + prompt + sample
    return tuple(np.ascontiguousarray(a) for a in out)


def kernel(**inputs):
    import concourse.bacc as _bacc
    from concourse import mybir as _mybir
    from concourse.bass_utils import run_bass_kernel_spmd as _run

    nc = _bacc.Bacc("TRN2", target_bir_lowering=False, num_devices=1)
    laid = {name: np.ascontiguousarray(a) for name, a in lay_out({k: np.asarray(v) for k, v in inputs.items()}).items()}
    ins = {name: nc.dram_tensor(f"in_{name}", a.shape, _mybir.dt.from_np(a.dtype), kind="ExternalInput").ap()
           for name, a in laid.items()}
    outs = {name: nc.dram_tensor(f"out_{name}", shape, _mybir.dt.float32, kind="ExternalOutput").ap()
            for name, shape in OUT_SHAPES.items()}
    program(nc, ins, outs)
    r = _run(nc, [{f"in_{name}": a for name, a in laid.items()}], core_ids=[0])
    return unpack({name: r.results[0][f"out_{name}"] for name in OUT_SHAPES})
```
